# Optimizing a Trainium2 kernel written in Bass

```python
import math
import jax, jax.numpy as jnp
from jax import lax
import numpy as np

D_MODEL = 1024
BATCH = 1
SEQ = 256
DEPTH = 2

N_MIXERS = 4
RMS_EPS = 1e-6
D_FF = ((8 * D_MODEL // 3 + 255) // 256) * 256
DA_HEAD_DIM = 64
DA_HEADS = D_MODEL // (2 * DA_HEAD_DIM)
DA_QBLOCK = 128
RT_HEADS = 4
RT_KEY_DIM = D_MODEL // RT_HEADS
RT_VAL_DIM = 2 * RT_KEY_DIM
RT_CHUNK = 128
SG_WIDTH = 3 * D_MODEL
SG_GROUPS = 8
SG_CHUNK = 128
LRU_WIDTH = ((4 * D_MODEL // 3 + 255) // 256) * 256
LRU_BLOCK = 128
LRU_BLOCKS = LRU_WIDTH // LRU_BLOCK
CONV_WIDTH = 4
RG_C = 8.0


def _rms(x, gain):
    x32 = x.astype(jnp.float32)
    y = x32 * lax.rsqrt(jnp.mean(x32 * x32, axis=-1, keepdims=True) + RMS_EPS)
    return (y * gain.astype(jnp.float32)).astype(x.dtype)

def _swiglu(xn, w_in, w_out):
    a, b = jnp.split(xn @ w_in, 2, axis=-1)
    return (jax.nn.silu(a) * b) @ w_out

def _lambda_init(layer_idx):
    return 0.8 - 0.6 * math.exp(-0.3 * layer_idx)

def _diff_attention(xn, w_in, q_gain, k_gain, lam, subln, w_out, lam_init):
    B, T, _ = xn.shape
    H, Dh = DA_HEADS, DA_HEAD_DIM
    q, k, v = jnp.split(xn @ w_in, 3, axis=-1)
    q = _rms(q.reshape(B, T, H, 2, Dh), q_gain) * (Dh ** -0.5)
    k = _rms(k.reshape(B, T, H, 2, Dh), k_gain)
    q = q.transpose(0, 2, 3, 1, 4)
    k = k.transpose(0, 2, 3, 1, 4)
    v = v.reshape(B, T, H, 2 * Dh).transpose(0, 2, 1, 3)
    lam32 = lam.astype(jnp.float32)
    lmbda = (jnp.exp(jnp.sum(lam32[0] * lam32[1])) - jnp.exp(jnp.sum(lam32[2] * lam32[3]))
             + lam_init)
    slopes = 2.0 ** (-8.0 * jnp.arange(1, H + 1, dtype=jnp.float32) / H)
    nb = T // DA_QBLOCK
    q_blocks = q.reshape(B, H, 2, nb, DA_QBLOCK, Dh).transpose(3, 0, 1, 2, 4, 5)
    key_pos = jnp.arange(T)

    def block(args):
        qb, n = args
        q_pos = n * DA_QBLOCK + jnp.arange(DA_QBLOCK)
        s = jnp.einsum('bhmqd,bhmkd->bhmqk', qb, k, preferred_element_type=jnp.float32)
        dist = (q_pos[:, None] - key_pos[None, :]).astype(jnp.float32)
        bias = jnp.where(dist >= 0, -slopes[:, None, None] * dist, -jnp.inf)
        p = jax.nn.softmax(s + bias[None, :, None], axis=-1)
        a = p[:, :, 0] - lmbda * p[:, :, 1]
        return jnp.einsum('bhqk,bhkd->bhqd', a.astype(v.dtype), v)

    o = lax.map(block, (q_blocks, jnp.arange(nb)))
    o = o.transpose(1, 0, 3, 2, 4).reshape(B, T, H, 2 * Dh)
    o = _rms(o, subln) * (1.0 - lam_init)
    return o.reshape(B, T, H * 2 * Dh).astype(xn.dtype) @ w_out

def _retention(xn, w_in, subln, w_out):
    B, T, _ = xn.shape
    H, Dk, Dv, C = RT_HEADS, RT_KEY_DIM, RT_VAL_DIM, RT_CHUNK
    nc = T // C
    proj = xn @ w_in
    q, k, v, g = jnp.split(proj, [H * Dk, 2 * H * Dk, 2 * H * Dk + H * Dv], axis=-1)

    def to_chunks(t, d):
        t = t.astype(jnp.float32).reshape(B, T, H, d).transpose(0, 2, 1, 3)
        return t.reshape(B, H, nc, C, d).transpose(2, 0, 1, 3, 4)

    qc = to_chunks(q, Dk)
    kc = to_chunks(k, Dk) * (Dk ** -0.5)
    vc = to_chunks(v, Dv)
    gamma = 1.0 - 2.0 ** (-5.0 - jnp.arange(H, dtype=jnp.float32))
    log_g = jnp.log(gamma)
    idx = jnp.arange(C, dtype=jnp.float32)
    diff = idx[:, None] - idx[None, :]
    decay_intra = jnp.where(diff >= 0, jnp.exp(jnp.maximum(diff, 0.0) * log_g[:, None, None]), 0.0)
    xi = jnp.exp((idx + 1.0) * log_g[:, None])
    zeta = jnp.exp((C - 1.0 - idx) * log_g[:, None])
    g_chunk = jnp.exp(C * log_g)

    def step(R, inp):
        qq, kk, vv = inp
        att = jnp.einsum('bhqd,bhkd->bhqk', qq, kk) * decay_intra
        o = (jnp.einsum('bhqk,bhkv->bhqv', att, vv)
             + jnp.einsum('bhqd,bhdv->bhqv', qq, R) * xi[:, :, None])
        R = g_chunk[:, None, None] * R + jnp.einsum('bhkd,bhkv->bhdv', kk * zeta[:, :, None], vv)
        return R, o

    R0 = jnp.zeros((B, H, Dk, Dv), jnp.float32)
    _, o = lax.scan(step, R0, (qc, kc, vc))
    o = o.transpose(1, 0, 3, 2, 4).reshape(B, T, H, Dv)
    o = _rms(o, subln).reshape(B, T, H * Dv)
    return (jax.nn.silu(g.astype(jnp.float32)) * o).astype(xn.dtype) @ w_out

def _spatial_gating(xn, w_in, v_gain, w_s, b_s, w_out):
    B, T, _ = xn.shape
    C, G = SG_CHUNK, SG_GROUPS
    nc = T // C
    z = jax.nn.gelu(xn @ w_in)
    u, v = jnp.split(z, 2, axis=-1)
    v = _rms(v, v_gain).reshape(B, nc, C, G, SG_WIDTH // G)
    ws = w_s * jnp.tril(jnp.ones((C, C), w_s.dtype))
    mixed = jnp.einsum('gts,bnsgc->bntgc', ws, v) + jnp.transpose(b_s)[None, None, :, :, None]
    return (u * mixed.reshape(B, T, SG_WIDTH)) @ w_out

def _rglru_block(xn, w_in, conv_w, conv_b, w_a, b_a, w_x, b_x, lam, w_out):
    B, T, _ = xn.shape
    gate_br, xb = jnp.split(xn @ w_in, 2, axis=-1)
    gate = jax.nn.gelu(gate_br)
    xb = lax.conv_general_dilated(
        xb, conv_w[:, None, :].astype(xb.dtype), window_strides=(1,),
        padding=[(CONV_WIDTH - 1, 0)], dimension_numbers=('NWC', 'WIO', 'NWC'),
        feature_group_count=LRU_WIDTH) + conv_b
    xb = xb.astype(jnp.float32)
    xblk = xb.reshape(B, T, LRU_BLOCKS, LRU_BLOCK)
    r = jax.nn.sigmoid(jnp.einsum('btnc,ncd->btnd', xblk, w_a.astype(jnp.float32))
                       .reshape(B, T, LRU_WIDTH) + b_a)
    i = jax.nn.sigmoid(jnp.einsum('btnc,ncd->btnd', xblk, w_x.astype(jnp.float32))
                       .reshape(B, T, LRU_WIDTH) + b_x)
    log_a = -RG_C * r * jax.nn.softplus(-lam.astype(jnp.float32))
    a = jnp.exp(log_a)
    b = jnp.sqrt(jnp.maximum(-jnp.expm1(2.0 * log_a), 1e-12)) * (i * xb)

    def combine(c1, c2):
        a1, b1 = c1
        a2, b2 = c2
        return a1 * a2, a2 * b1 + b2

    _, h = lax.associative_scan(combine, (a, b), axis=1)
    return (h * gate.astype(jnp.float32)).astype(xn.dtype) @ w_out

def first_inputs(seed: int = 0) -> dict:
    key = jax.random.key(seed)
    keys = iter(jax.random.split(key, 40))
    f32 = jnp.float32

    def nrm(shape, scale):
        return scale * jax.random.normal(next(keys), shape, f32)

    def gain(shape):
        return 1.0 + 0.02 * jax.random.normal(next(keys), shape, f32)

    na, nr, ns, nl = [len(range(m, DEPTH, N_MIXERS)) for m in range(N_MIXERS)]
    D = D_MODEL
    da_width = DA_HEADS * 2 * DA_HEAD_DIM
    rt_in = 2 * RT_HEADS * RT_KEY_DIM + 2 * RT_HEADS * RT_VAL_DIM
    inp = {}
    inp['x'] = jax.random.normal(next(keys), (BATCH, SEQ, D), f32)
    inp['ffn1_norm'] = gain((DEPTH, D))
    inp['ffn1_w_in'] = nrm((DEPTH, D, 2 * D_FF), D ** -0.5)
    inp['ffn1_w_out'] = nrm((DEPTH, D_FF, D), D_FF ** -0.5)
    inp['mix_norm'] = gain((DEPTH, D))
    inp['ffn2_norm'] = gain((DEPTH, D))
    inp['ffn2_w_in'] = nrm((DEPTH, D, 2 * D_FF), D ** -0.5)
    inp['ffn2_w_out'] = nrm((DEPTH, D_FF, D), D_FF ** -0.5)
    inp['da_w_in'] = nrm((na, D, 3 * da_width), D ** -0.5)
    inp['da_q_gain'] = gain((na, DA_HEAD_DIM))
    inp['da_k_gain'] = gain((na, DA_HEAD_DIM))
    inp['da_lambda'] = nrm((na, 4, DA_HEAD_DIM), 0.1)
    inp['da_subln'] = gain((na, 2 * DA_HEAD_DIM))
    inp['da_w_out'] = nrm((na, da_width, D), da_width ** -0.5)
    inp['rt_w_in'] = nrm((nr, D, rt_in), D ** -0.5)
    inp['rt_subln'] = gain((nr, RT_HEADS, RT_VAL_DIM))
    inp['rt_w_out'] = nrm((nr, RT_HEADS * RT_VAL_DIM, D), (RT_HEADS * RT_VAL_DIM) ** -0.5)
    inp['sg_w_in'] = nrm((ns, D, 2 * SG_WIDTH), D ** -0.5)
    inp['sg_v_gain'] = gain((ns, SG_WIDTH))
    inp['sg_w_s'] = nrm((ns, SG_GROUPS, SG_CHUNK, SG_CHUNK), SG_CHUNK ** -0.5)
    inp['sg_b_s'] = 1.0 + nrm((ns, SG_GROUPS, SG_CHUNK), 0.1)
    inp['sg_w_out'] = nrm((ns, SG_WIDTH, D), SG_WIDTH ** -0.5)
    inp['lr_w_in'] = nrm((nl, D, 2 * LRU_WIDTH), D ** -0.5)
    inp['lr_conv_w'] = nrm((nl, CONV_WIDTH, LRU_WIDTH), CONV_WIDTH ** -0.5)
    inp['lr_conv_b'] = nrm((nl, LRU_WIDTH), 0.01)
    inp['lr_w_a'] = nrm((nl, LRU_BLOCKS, LRU_BLOCK, LRU_BLOCK), LRU_BLOCK ** -0.5)
    inp['lr_b_a'] = nrm((nl, LRU_WIDTH), 0.01)
    inp['lr_w_x'] = nrm((nl, LRU_BLOCKS, LRU_BLOCK, LRU_BLOCK), LRU_BLOCK ** -0.5)
    inp['lr_b_x'] = nrm((nl, LRU_WIDTH), 0.01)
    a0 = jax.random.uniform(next(keys), (nl, LRU_WIDTH), f32, 0.9, 0.999)
    s = a0 ** (1.0 / RG_C)
    inp['lr_lambda'] = jnp.log(s) - jnp.log1p(-s)
    inp['lr_w_out'] = nrm((nl, LRU_WIDTH, D), LRU_WIDTH ** -0.5)
    return inp

def first_block(x, ffn1_norm, ffn1_w_in, ffn1_w_out, mix_norm, ffn2_norm, ffn2_w_in, ffn2_w_out,
              da_w_in, da_q_gain, da_k_gain, da_lambda, da_subln, da_w_out,
              rt_w_in, rt_subln, rt_w_out,
              sg_w_in, sg_v_gain, sg_w_s, sg_b_s, sg_w_out,
              lr_w_in, lr_conv_w, lr_conv_b, lr_w_a, lr_b_a, lr_w_x, lr_b_x, lr_lambda, lr_w_out):
    for i in range(DEPTH):
        kind = i % N_MIXERS
        j = i // N_MIXERS
        h = x + 0.5 * _swiglu(_rms(x, ffn1_norm[i]), ffn1_w_in[i], ffn1_w_out[i])
        xn = _rms(h, mix_norm[i])
        if kind == 0:
            m = _diff_attention(xn, da_w_in[j], da_q_gain[j], da_k_gain[j], da_lambda[j],
                                da_subln[j], da_w_out[j], _lambda_init(i))
        elif kind == 1:
            m = _retention(xn, rt_w_in[j], rt_subln[j], rt_w_out[j])
        elif kind == 2:
            m = _spatial_gating(xn, sg_w_in[j], sg_v_gain[j], sg_w_s[j], sg_b_s[j], sg_w_out[j])
        else:
            m = _rglru_block(xn, lr_w_in[j], lr_conv_w[j], lr_conv_b[j], lr_w_a[j], lr_b_a[j],
                             lr_w_x[j], lr_b_x[j], lr_lambda[j], lr_w_out[j])
        h = h + m.astype(h.dtype)
        x = h + 0.5 * _swiglu(_rms(h, ffn2_norm[i]), ffn2_w_in[i], ffn2_w_out[i])
    return x


DEPTH_2 = 1

CHUNK = 64
N_PAST_CHUNKS = 8
BAND = (N_PAST_CHUNKS + 1) * CHUNK
ATT_HEADS = 8
ATT_HEAD_DIM = 64
ATT_WIDTH = ATT_HEADS * ATT_HEAD_DIM
MAX_REL = 256
N_REL = 2 * MAX_REL + 1
DN_HEADS = 4
DN_HEAD_DIM = 128
DN_WIDTH = DN_HEADS * DN_HEAD_DIM
CONV_K = 4
D_FF_2 = 4 * D_MODEL
EPS = 1e-6
SPLITS = [ATT_WIDTH, 2 * ATT_WIDTH, 3 * ATT_WIDTH,
          3 * ATT_WIDTH + 3 * DN_WIDTH,
          3 * ATT_WIDTH + 4 * DN_WIDTH,
          3 * ATT_WIDTH + 4 * DN_WIDTH + DN_HEADS]
IN_COLS = 3 * ATT_WIDTH + 4 * DN_WIDTH + 2 * DN_HEADS


def rms_norm(x, g):
    xf = x.astype(jnp.float32)
    y = xf * lax.rsqrt(jnp.mean(xf * xf, axis=-1, keepdims=True) + EPS)
    return (y * g.astype(jnp.float32)).astype(x.dtype)

def l2_norm(x):
    xf = x.astype(jnp.float32)
    return xf * lax.rsqrt(jnp.sum(xf * xf, axis=-1, keepdims=True) + EPS)

def chunked_rel_attention(q, k, v, q_gain, k_gain, rel_bias):
    B, L, H, Dh = q.shape
    nc = L // CHUNK
    q = rms_norm(q, q_gain)
    k = rms_norm(k, k_gain)
    qc = q.reshape(B, nc, CHUNK, H, Dh)
    pad = ((0, 0), (N_PAST_CHUNKS * CHUNK, 0), (0, 0), (0, 0))
    kp = jnp.pad(k, pad).reshape(B, nc + N_PAST_CHUNKS, CHUNK, H, Dh)
    vp = jnp.pad(v, pad).reshape(B, nc + N_PAST_CHUNKS, CHUNK, H, Dh)
    kb = jnp.concatenate([kp[:, j:j + nc] for j in range(N_PAST_CHUNKS + 1)], axis=2)
    vb = jnp.concatenate([vp[:, j:j + nc] for j in range(N_PAST_CHUNKS + 1)], axis=2)
    scores = jnp.einsum('bcqhd,bckhd->bchqk', qc, kb,
                        preferred_element_type=jnp.float32) * (Dh ** -0.5)
    q_pos = N_PAST_CHUNKS * CHUNK + np.arange(CHUNK)
    k_pos = np.arange(BAND)
    rel_idx = np.clip(q_pos[:, None] - k_pos[None, :], -MAX_REL, MAX_REL) + MAX_REL
    bias = rel_bias.astype(jnp.float32)[:, rel_idx]
    scores = scores + bias[None, None]
    key_chunk = jnp.arange(nc)[:, None] + jnp.asarray(k_pos // CHUNK)[None, :] - N_PAST_CHUNKS
    valid = key_chunk >= 0
    scores = jnp.where(valid[None, :, None, None, :], scores, jnp.finfo(jnp.float32).min)
    p = jax.nn.softmax(scores, axis=-1).astype(v.dtype)
    o = jnp.einsum('bchqk,bckhd->bcqhd', p, vb)
    return o.reshape(B, L, H * Dh)

def causal_short_conv(x, w):
    L = x.shape[1]
    xp = jnp.pad(x, ((0, 0), (CONV_K - 1, 0), (0, 0)))
    y = xp[:, 0:L] * w[0]
    for j in range(1, CONV_K):
        y = y + xp[:, j:j + L] * w[j]
    return jax.nn.silu(y)

def gated_delta_rule(q, k, v, g, beta):
    B, L, H, Dk = q.shape
    Dv = v.shape[-1]
    nc = L // CHUNK
    f32 = jnp.float32
    q = l2_norm(q) * (Dk ** -0.5)
    k = l2_norm(k)
    v = v.astype(f32)

    def to_chunks(t):
        return jnp.transpose(t.reshape(B, nc, CHUNK, H, -1), (0, 3, 1, 2, 4))

    q, k, v = to_chunks(q), to_chunks(k), to_chunks(v)
    g = jnp.transpose(g.astype(f32).reshape(B, nc, CHUNK, H), (0, 3, 1, 2))
    beta = jnp.transpose(beta.astype(f32).reshape(B, nc, CHUNK, H), (0, 3, 1, 2))
    decay = jnp.cumsum(g, axis=-1)
    tril = jnp.asarray(np.tril(np.ones((CHUNK, CHUNK), dtype=bool)))
    strict = jnp.asarray(np.tril(np.ones((CHUNK, CHUNK), dtype=bool), -1))
    diff = decay[..., :, None] - decay[..., None, :]
    l_mask = jnp.where(tril, jnp.exp(jnp.where(tril, diff, 0.0)), 0.0)
    k_beta = k * beta[..., None]
    v_beta = v * beta[..., None]
    a_strict = jnp.where(strict, jnp.einsum('bhnid,bhnjd->bhnij', k_beta, k) * l_mask, 0.0)
    t_mat = a_strict + jnp.eye(CHUNK, dtype=f32)
    value = lax.linalg.triangular_solve(t_mat, v_beta, left_side=True, lower=True,
                                        unit_diagonal=True)
    k_cumdecay = lax.linalg.triangular_solve(t_mat, k_beta * jnp.exp(decay)[..., None],
                                             left_side=True, lower=True, unit_diagonal=True)
    attn_intra = jnp.where(tril, jnp.einsum('bhnid,bhnjd->bhnij', q, k) * l_mask, 0.0)
    q_decay = q * jnp.exp(decay)[..., None]
    k_tail = k * jnp.exp(decay[..., -1:] - decay)[..., None]
    chunk_decay = jnp.exp(decay[..., -1])

    def step(S, inp):
        qd, kc, val, att, kt, cd = inp
        v_new = val - jnp.einsum('bhcd,bhde->bhce', kc, S)
        o = jnp.einsum('bhcd,bhde->bhce', qd, S) + jnp.einsum('bhij,bhje->bhie', att, v_new)
        S = S * cd[..., None, None] + jnp.einsum('bhcd,bhce->bhde', kt, v_new)
        return S, o

    xs = tuple(jnp.moveaxis(t, 2, 0) for t in
               (q_decay, k_cumdecay, value, attn_intra, k_tail, chunk_decay))
    S0 = jnp.zeros((B, H, Dk, Dv), f32)
    _, o = lax.scan(step, S0, xs)
    return jnp.transpose(o, (1, 0, 3, 2, 4)).reshape(B, L, H, Dv)

def second_inputs(seed: int = 0) -> dict:
    key = jax.random.key(seed)
    ks = jax.random.split(key, 16)
    f32 = jnp.float32

    def nrm(k, shape, s):
        return jax.random.normal(k, shape, f32) * s

    x = nrm(ks[0], (BATCH, SEQ, D_MODEL), 1.0)
    mix_norm_gain = 1.0 + nrm(ks[1], (DEPTH_2, D_MODEL), 0.05)
    w_in = nrm(ks[2], (DEPTH_2, D_MODEL, IN_COLS), D_MODEL ** -0.5)
    att_q_gain = 1.0 + nrm(ks[3], (DEPTH_2, ATT_HEAD_DIM), 0.05)
    att_k_gain = 1.0 + nrm(ks[4], (DEPTH_2, ATT_HEAD_DIM), 0.05)
    rel_bias = nrm(ks[5], (DEPTH_2, ATT_HEADS, N_REL), 0.2)
    att_out_gain = 1.0 + nrm(ks[6], (DEPTH_2, ATT_WIDTH), 0.05)
    dn_conv_w = nrm(ks[7], (DEPTH_2, CONV_K, 3 * DN_WIDTH), CONV_K ** -0.5)
    dn_a_log = jnp.log(jax.random.uniform(ks[8], (DEPTH_2, DN_HEADS), f32, 1.0, 16.0))
    dt = jnp.exp(jax.random.uniform(ks[9], (DEPTH_2, DN_HEADS), f32,
                                    float(np.log(1e-3)), float(np.log(1e-1))))
    dn_dt_bias = dt + jnp.log(-jnp.expm1(-dt))
    dn_out_gain = 1.0 + nrm(ks[10], (DEPTH_2, DN_HEAD_DIM), 0.05)
    w_out = nrm(ks[11], (DEPTH_2, D_MODEL, D_MODEL), D_MODEL ** -0.5)
    ffn_norm_gain = 1.0 + nrm(ks[12], (DEPTH_2, D_MODEL), 0.05)
    w_ff1 = nrm(ks[13], (DEPTH_2, D_MODEL, D_FF_2), D_MODEL ** -0.5)
    w_ff2 = nrm(ks[14], (DEPTH_2, D_FF_2, D_MODEL), D_FF_2 ** -0.5)
    return {"x": x, "mix_norm_gain": mix_norm_gain, "w_in": w_in,
            "att_q_gain": att_q_gain, "att_k_gain": att_k_gain, "rel_bias": rel_bias,
            "att_out_gain": att_out_gain, "dn_conv_w": dn_conv_w, "dn_a_log": dn_a_log,
            "dn_dt_bias": dn_dt_bias, "dn_out_gain": dn_out_gain, "w_out": w_out,
            "ffn_norm_gain": ffn_norm_gain, "w_ff1": w_ff1, "w_ff2": w_ff2}

def second_block(x, mix_norm_gain, w_in, att_q_gain, att_k_gain, rel_bias, att_out_gain,
              dn_conv_w, dn_a_log, dn_dt_bias, dn_out_gain, w_out, ffn_norm_gain,
              w_ff1, w_ff2):
    B, L, _ = x.shape
    h = x
    for layer in range(DEPTH_2):
        u = rms_norm(h, mix_norm_gain[layer])
        proj = u @ w_in[layer]
        aq, ak, av, dqkv, dgate, da, db = jnp.split(proj, SPLITS, axis=-1)
        shp_a = (B, L, ATT_HEADS, ATT_HEAD_DIM)
        o_att = chunked_rel_attention(aq.reshape(shp_a), ak.reshape(shp_a), av.reshape(shp_a),
                                      att_q_gain[layer], att_k_gain[layer], rel_bias[layer])
        o_att = rms_norm(o_att, att_out_gain[layer])
        dqkv = causal_short_conv(dqkv, dn_conv_w[layer])
        dq, dk, dv = jnp.split(dqkv, 3, axis=-1)
        shp_d = (B, L, DN_HEADS, DN_HEAD_DIM)
        log_decay = -jnp.exp(dn_a_log[layer].astype(jnp.float32)) * jax.nn.softplus(
            da.astype(jnp.float32) + dn_dt_bias[layer].astype(jnp.float32))
        beta = jax.nn.sigmoid(db.astype(jnp.float32))
        o_dn = gated_delta_rule(dq.reshape(shp_d), dk.reshape(shp_d), dv.reshape(shp_d),
                                log_decay, beta)
        o_dn = rms_norm(o_dn, dn_out_gain[layer]) * jax.nn.silu(
            dgate.reshape(shp_d).astype(jnp.float32))
        o_dn = o_dn.reshape(B, L, DN_WIDTH).astype(h.dtype)
        mixed = jnp.concatenate([o_att, o_dn], axis=-1) @ w_out[layer]
        h = h + mixed
        z = rms_norm(h, ffn_norm_gain[layer]) @ w_ff1[layer]
        h = h + jnp.square(jax.nn.relu(z)) @ w_ff2[layer]
    return h


def setup_inputs(seed=0):
    out = dict(first_inputs(seed))
    for name, value in second_inputs(seed + 1).items():
        if name != "x":
            out[name + "_2"] = value
    return out


def reference(
    x, ffn1_norm, ffn1_w_in, ffn1_w_out, mix_norm, ffn2_norm, ffn2_w_in, ffn2_w_out, da_w_in,
    da_q_gain, da_k_gain, da_lambda, da_subln, da_w_out, rt_w_in, rt_subln, rt_w_out, sg_w_in,
    sg_v_gain, sg_w_s, sg_b_s, sg_w_out, lr_w_in, lr_conv_w, lr_conv_b, lr_w_a, lr_b_a, lr_w_x,
    lr_b_x, lr_lambda, lr_w_out, mix_norm_gain_2, w_in_2, att_q_gain_2, att_k_gain_2,
    rel_bias_2, att_out_gain_2, dn_conv_w_2, dn_a_log_2, dn_dt_bias_2, dn_out_gain_2, w_out_2,
    ffn_norm_gain_2, w_ff1_2, w_ff2_2,
):
    x = first_block(
        x, ffn1_norm, ffn1_w_in, ffn1_w_out, mix_norm, ffn2_norm, ffn2_w_in, ffn2_w_out,
        da_w_in, da_q_gain, da_k_gain, da_lambda, da_subln, da_w_out, rt_w_in, rt_subln,
        rt_w_out, sg_w_in, sg_v_gain, sg_w_s, sg_b_s, sg_w_out, lr_w_in, lr_conv_w, lr_conv_b,
        lr_w_a, lr_b_a, lr_w_x, lr_b_x, lr_lambda, lr_w_out,
    )
    return second_block(
        x, mix_norm_gain_2, w_in_2, att_q_gain_2, att_k_gain_2, rel_bias_2, att_out_gain_2,
        dn_conv_w_2, dn_a_log_2, dn_dt_bias_2, dn_out_gain_2, w_out_2, ffn_norm_gain_2, w_ff1_2,
        w_ff2_2,
    )


_drawn_inputs = setup_inputs


def setup_inputs(seed=0):
    import zlib

    import numpy as np

    out = dict(_drawn_inputs(seed))
    spreads = {}
    factors = {'ffn1_norm': 2.981,
     'ffn2_norm': 4.856,
     'da_q_gain': 2.907,
     'da_k_gain': 2.851,
     'da_subln': 3.195,
     'rt_subln': 32.218,
     'att_q_gain_2': 3.797,
     'att_k_gain_2': 3.771,
     'att_out_gain_2': 21.867,
     'dn_out_gain_2': 32.512,
     'rel_bias_2': 7.787,
     'dn_a_log_2': 5.125,
     'ffn_norm_gain_2': 8.0}
    for name, (base, spread) in spreads.items():
        noise = np.random.default_rng([zlib.crc32(name.encode()), seed]).standard_normal(out[name].shape)
        drawn = base * np.exp(spread * noise) if base else spread * noise
        out[name] = __import__('jax').numpy.asarray(drawn.astype(out[name].dtype))
    for name, factor in factors.items():
        out[name] = (out[name] * factor).astype(out[name].dtype)
    return out
```

```python
from contextlib import ExitStack

import numpy as np

import concourse.bass as bass
from concourse import mybir

ALU = mybir.AluOpType
ACT = mybir.ActivationFunctionType
AX_X = mybir.AxisListType.X
F32 = mybir.dt.float32
F32R = mybir.dt.float32r

P = 128
T = 256
D = 1024
KD = D // P
EPS = 1e-6
RING = 3
BLOCK = 2048

FF = 2816
FFC = FF // 256
DA_H, DA_DH = 8, 64
LAM_INIT = 0.8 - 0.6 * float(np.exp(-0.3 * 0))
RT_H, RT_DK, RT_DV = 4, 256, 512
AT_H, AT_DH, N_REL, MAX_REL = 8, 64, 513, 256
CHUNK = 64
DN_H, DN_D, CONV_K = 4, 128, 4
FF2 = 4096
FF2C = FF2 // 512
LEVELS = 6
MASKED = -1e30

C_IDENT = 0
C_CUM = C_IDENT + P
C_LAST = C_CUM + P
C_LEVEL = C_LAST + P
C_END = C_LEVEL + LEVELS * P


def constants():
    j = np.arange(P)[:, None]
    i = np.arange(P)[None, :]
    table = np.zeros((P, C_END), np.float32)
    table[:, C_IDENT:C_IDENT + P] = i == j
    table[:, C_CUM:C_CUM + P] = (j <= i) & (j // CHUNK == i // CHUNK)
    table[:, C_LAST:C_LAST + P] = j == (i // CHUNK) * CHUNK + CHUNK - 1
    for n in range(LEVELS):
        half = 1 << n
        table[:, C_LEVEL + n * P:C_LEVEL + (n + 1) * P] = (
            (j // (2 * half) == i // (2 * half)) & (j // half % 2 == 0) & (i // half % 2 == 1))
    dist = np.arange(T)[None, :] - j
    slopes = 2.0 ** (-8.0 * np.arange(1, DA_H + 1) / DA_H)
    alibi = np.where(dist[:, None, :] >= 0, -slopes[None, :, None] * dist[:, None, :], MASKED)
    gamma = 1.0 - 2.0 ** (-5.0 - np.arange(RT_H, dtype=np.float64))
    decay = np.where(dist[:, None, :] >= 0, gamma[None, :, None] ** np.maximum(dist, 0)[:, None, :], 0.0)
    return {
        "c_table": table,
        "c_flip": np.ascontiguousarray(table[:, C_IDENT:C_IDENT + P][:, ::-1]),
        "c_alibi": alibi.astype(np.float32).reshape(P, DA_H * T),
        "c_decay": decay.astype(np.float32).reshape(P, RT_H * T),
    }


def first_then_second_block(nc, A, out, stop=99):
    ctx = ExitStack()
    with ctx:
        def sb(name, shape, dt=F32):
            return ctx.enter_context(nc.sbuf_tensor(name, shape, dt))

        def sem(name):
            return ctx.enter_context(nc.semaphore(name))

        raw = sb("raw", [P, RING, BLOCK])
        w_hi = sb("w_hi", [P, RING, BLOCK], F32R)
        w_lo = sb("w_lo", [P, RING, BLOCK], F32R)
        x = sb("x", [P, 2, D])
        xg = sb("xg", [P, 2, D])
        xT_hi = sb("xT_hi", [P, KD, T], F32R)
        xT_lo = sb("xT_lo", [P, KD, T], F32R)
        gains = sb("gains", [P, 2, D])
        sumsq = sb("sumsq", [P, 2])
        meansq = sb("meansq", [P, 2])
        rstd = sb("rstd", [P, 2])
        neghalf = sb("neghalf", [P, 64])
        relu = sb("relu", [P, 2, 512])
        silu_a = relu[:, :, 0:256]
        hid = sb("hid", [P, 2, 512])
        square = hid[:, :, :].rearrange("p t n -> p (t n)")
        hT_hi = sb("hT_hi", [P, 4, T], F32R)
        hT_lo = sb("hT_lo", [P, 4, T], F32R)
        table = sb("table", [P, C_END])
        room = sb("room", [P, 2 * 6144])

        qT = sb("qT", [P, 8, T])
        kT = sb("kT", [P, 8, T])
        bias = sb("bias", [P, 8, T])
        da_gain = sb("da_gain", [P, 2])
        lam_exp = sb("lam_exp", [P, 4])
        lam = sb("lam", [P, 1])
        qk_ss = sb("qk_ss", [P, 4, 16])
        qk_rstd = sb("qk_rstd", [P, 4, 16])
        neg_max = sb("neg_max", [P, 2, 4])
        p_sum = sb("p_sum", [P, 2, 4])
        p_recip = sb("p_recip", [P, 4])
        recip_lam = sb("recip_lam", [P, 2])
        head_ss = sb("head_ss", [P, 2])
        head_rstd = sb("head_rstd", [P, 2])

        def carve(at, *dims):
            size = int(np.prod(dims))
            view = room[:, at:at + size]
            names = " ".join("abcd"[:len(dims)])
            if len(dims) > 1:
                view = view.rearrange(f"p ({names}) -> p {names}", **dict(zip("abcd", dims)))
            return view, at + size

        da_proj, at = carve(0, 2, 3072)
        prob, at = carve(at, 2, 2, 384)
        prob1, at = carve(at, 384)
        mixed, at = carve(at, 2, 384)
        mixT, at = carve(at, 384)
        head_out, at = carve(at, 2, P)
        da_lam, at = carve(at, 4, DA_DH)
        lam_prod, at = carve(at, 2, DA_DH)
        subln, at = carve(at, P)

        rt_q, at = carve(0, 2, D)
        rt_k, at = carve(at, 2, D)
        rt_v, at = carve(at, 2, RT_H * RT_DV)
        rt_g, at = carve(at, 2, RT_H * RT_DV)
        rt_att, _ = carve(0, 2, 384)
        rt_chunk = [part[:, :, m * 512:m * 512 + 512] for part, n in ((rt_q, 2), (rt_k, 2), (rt_v, 4), (rt_g, 4))
                    for m in range(n)]
        MX_SMALL = 16 * 11
        rt_pair = [m % 3 for m in range(6)] + [0, 1] * 3

        mx_dn, at = carve(0, 3, 2, 512)
        mx_gate, at = carve(at, 2, 512)
        mx_att, at = carve(at, 3, 2, 512)
        free = at
        conv_in, at = carve(at, 12, CONV_K - 1 + T)
        conv_v, at = carve(at, 4, T)
        conv_out = [qT[:, 4:8, :], kT[:, 4:8, :], conv_v]
        dn_qhT, dn_khT = qT[:, 4:8, :], kT[:, 4:8, :]
        prob_a, _ = carve(at, 2, 384)
        probT = relu[:, 0, 0:384]
        flip = relu[:, 1, 0:P]

        def by_pair(ap):
            return ap.rearrange("p (u n) -> p u n", u=8)

        def flat(ap):
            return ap.rearrange("p a b -> p (a b)")

        dn_tok = [by_pair(room[:, s * 1024:s * 1024 + 1024]) for s in range(3)]
        dn_kbe, dn_ktail, dn_vbeta = dn_tok
        dn_AT = by_pair(room[:, free:free + 1024])
        dn_attT = by_pair(room[:, free + 1024:free + 2048])
        dn_X = by_pair(room[:, free + 2048:free + 3072])
        dn_XT = by_pair(flat(conv_v))
        dn_LT = by_pair(xg[:, 0, :])
        dn_MT = dn_LT
        dn_exprow = by_pair(xg[:, 1, :])
        dn_Y = by_pair(flat(dn_khT))
        dn_val = dn_AT
        dn_kcT = dn_X
        dn_state, dn_vnew = xg[:, 0, 0:512], xg[:, 0, 512:1024]
        dn_y = room[:, 0:1024].rearrange("p (t n) -> p t n", t=2)
        sq8 = by_pair(square)
        att_y = mx_att[:, 0, :, :]
        out_gain = gains[:, 0, 0:512]
        conv_row = gains[0:CONV_K * 12, 0, 512:640]
        dn_gain = gains[:, 0, 640:768]
        conv_w = sb("conv_w", [P, CONV_K * 12])
        a_log = sb("a_log", [P, DN_H])
        dt_bias = sb("dt_bias", [P, DN_H])
        att_gain = sb("att_gain", [P, 2])
        tail_w = sb("tail_w", [P, KD, 8])
        tail_hi = sb("tail_hi", [P, KD, 8], F32R)
        tail_lo = sb("tail_lo", [P, KD, 8], F32R)
        small = sb("small", [P, 24, 8])
        (ab, zz, ez, uu, ln, dd, gg, beta, dec, etail, edec, bed, dn_ss, dn_rstd, att_ss, att_rs) = (
            [small[:, n, :] for n in range(12)] + [small[:, n:n + 2, :] for n in (12, 14)]
            + [small[:, n:n + 4, :].rearrange("p a b -> p (a b)") for n in (16, 20)])
        tail_ab = sb("tail_ab", [P, 2, 8])
        ea = sb("ea", [P, DN_H])
        att_max = sb("att_max", [P, 8, 2])
        att_sum = sb("att_sum", [P, 2, 8])
        att_recip = sb("att_recip", [P, 2, 8])

        bank = [ctx.enter_context(nc.psum_tensor(f"bank{i}", [P, 512], F32)) for i in range(8)]
        ident = table[:, C_IDENT:C_IDENT + P]

        raw_full = [sem(f"raw_full{s}") for s in range(RING)]
        hi_ready = sem("hi_ready")
        lo_ready = sem("lo_ready")
        wt_used = sem("wt_used")
        x_full = sem("x_full")
        table_full = sem("table_full")
        gain_full = [sem("gain_full0"), sem("gain_full1")]
        acc_done = sem("acc_done")
        resid_done = sem("resid_done")
        xg_ready = sem("xg_ready")
        xt_psum = sem("xt_psum")
        xt_hi_ready = sem("xt_hi_ready")
        xt_lo_ready = sem("xt_lo_ready")
        ss_ready = sem("ss_ready")
        rstd_ready = sem("rstd_ready")
        pool_chain = sem("pool_chain")
        dve_chain = sem("dve_chain")
        in_done = sem("in_done")
        silu_ready = sem("silu_ready")
        hid_ready = sem("hid_ready")
        ht_psum = sem("ht_psum")
        ht_hi_ready = sem("ht_hi_ready")
        ht_lo_ready = sem("ht_lo_ready")
        x_stored = sem("x_stored")
        proj_done = sem("proj_done")
        proj_read = sem("proj_read")
        da_small = sem("da_small")
        da_square = sem("da_square")
        da_sumsq = sem("da_sumsq")
        da_rstd = sem("da_rstd")
        da_normed = sem("da_normed")
        da_turned = sem("da_turned")
        da_qT = sem("da_qT")
        da_kT = sem("da_kT")
        da_lamsum = sem("da_lamsum")
        da_lamexp = sem("da_lamexp")
        bias_full = sem("bias_full")
        da_scores = sem("da_scores")
        da_max = sem("da_max")
        da_exp = sem("da_exp")
        da_mixed = sem("da_mixed")
        da_mixT_psum = sem("da_mixT_psum")
        da_mixT = sem("da_mixT")
        da_o = sem("da_o")
        da_oss = sem("da_oss")
        da_orstd = sem("da_orstd")
        da_normed_o = sem("da_normed_o")
        da_oT_psum = sem("da_oT_psum")
        da_oT_hi = sem("da_oT_hi")
        da_oT_lo = sem("da_oT_lo")
        in2_done = sem("in2_done")
        relu_ready = sem("relu_ready")
        sq_ready = sem("sq_ready")
        ht2_psum = sem("ht2_psum")
        ht2_hi_ready = sem("ht2_hi_ready")
        ht2_lo_ready = sem("ht2_lo_ready")
        (mx_small, mx_bias, mx_tail_hi, mx_tail_lo, mx_tail, mx_ab, mx_abs, mx_exp, mx_onep, mx_ln, mx_beta, mx_g,
         mx_cum, mx_dec, mx_last, mx_last_diff, mx_etail, mx_rows, mx_diff, mx_exprow, mx_LT, mx_masked,
         mx_convw_psum, mx_convw, mx_conv_psum, mx_conv_in, mx_zero, mx_conv, mx_silu, mx_tok_psum, mx_tok,
         mx_dnsq, mx_dnss, mx_dnr, mx_dnn, mx_ktail, mx_back_psum, mx_back, mx_gram, mx_A, mx_attT, mx_N0, mx_N0T,
         mx_inv0, mx_MT, mx_Y, mx_Ysb, mx_Z, mx_inv, mx_val, mx_valsb, mx_qd, mx_KS, mx_vnew, mx_O, mx_SU, mx_state,
         mx_osq, mx_oss, mx_or, mx_gate_gain, mx_y, mx_asq, mx_ass, mx_ars, mx_an, mx_aT_psum, mx_aq, mx_ak,
         mx_S, mx_max, mx_P, mx_PT_psum, mx_PT, mx_AV, mx_ao, mx_yT_psum, mx_yT_hi, mx_yT_lo, mx_vbeta,
         mx_arecip, mx_aoss, mx_aor, mx_ay) = [
            sem("mx_" + name) for name in (
                "small bias tail_hi tail_lo tail ab abs exp onep ln beta g cum dec last last_diff etail rows diff "
                "exprow LT masked convw_psum convw conv_psum conv_in zero conv silu tok_psum tok dnsq dnss dnr dnn "
                "ktail back_psum back gram A attT N0 N0T inv0 MT Y Ysb Z inv val valsb qd KS vnew O SU state osq oss "
                "or gate_gain y asq ass ars an aT_psum aq ak S max P PT_psum PT AV ao yT_psum yT_hi yT_lo vbeta "
                "arecip aoss aor ay").split()]
        rt_small = sem("rt_small")
        rt_turned = sem("rt_turned")
        rt_qT = sem("rt_qT")
        rt_kT = sem("rt_kT")
        rt_scores = sem("rt_scores")
        rt_decayed = sem("rt_decayed")
        rt_o = sem("rt_o")
        rt_oss = sem("rt_oss")
        rt_orstd = sem("rt_orstd")
        rt_gate = sem("rt_gate")
        rt_y = sem("rt_y")
        rt_yT_psum = sem("rt_yT_psum")
        rt_yT_hi = sem("rt_yT_hi")
        rt_yT_lo = sem("rt_yT_lo")

        FFN_BLOCKS = 3 * FFC
        first = {}
        total = 0
        PHASES = [("ffn0", FFN_BLOCKS), ("da_in", 12), ("da_out", 4), ("ffn1", FFN_BLOCKS),
                  ("ffn2", FFN_BLOCKS), ("rt_in", 24), ("rt_out", 8), ("ffn3", FFN_BLOCKS),
                  ("mix_in", 14), ("mix_out", 4), ("ff2", 4 * FF2C)]
        for name, blocks in PHASES:
            first[name] = total
            total += blocks
            if name == stop:
                break
        live = set(first)
        total += 2 if stop != 99 else 0
        ffn_weights = [(A["ffn1_w_in"][0], A["ffn1_w_out"][0]), (A["ffn2_w_in"][0], A["ffn2_w_out"][0]),
                       (A["ffn1_w_in"][1], A["ffn1_w_out"][1]), (A["ffn2_w_in"][1], A["ffn2_w_out"][1])]
        norm_gains = [A["ffn1_norm"][0], A["mix_norm"][0], A["ffn2_norm"][0], A["ffn1_norm"][1],
                      A["mix_norm"][1], A["ffn2_norm"][1], A["mix_norm_gain_2"][0],
                      A["ffn_norm_gain_2"][0]]
        NORM_OF = {"ffn0": 0, "da_in": 1, "ffn1": 2, "ffn2": 3, "rt_in": 4, "ffn3": 5, "mix_in": 6, "ff2": 7}
        PROJ_NORM = {0: 1, 6: 4, 18: 6}
        norms = sum(name in live for name in NORM_OF)

        def piece(tensor, q):
            return tensor[:, q % 2, (q // 2) * 512:(q // 2) * 512 + 512]

        def turned(tensor, q):
            return tensor[:, 4 * (q // 2):4 * (q // 2) + 4, (q % 2) * P:(q % 2) * P + P]

        def by_four(ap):
            return ap.rearrange("p (k n) -> p k n", k=4)

        last_out = [first[a] + b - 1 for a, b in PHASES
                    if a in live and a not in ("da_in", "rt_in", "mix_in")]

        level = [table[:, C_LEVEL + n * P:C_LEVEL + n * P + P].unsqueeze(1).to_broadcast([P, 8, P])
                 for n in range(LEVELS)]
        cum = table[:, C_CUM:C_CUM + P]
        last_row = table[:, C_LAST:C_LAST + P]
        sum_mask = cum.unsqueeze(1).to_broadcast([P, 8, P])
        two_idents = ident.unsqueeze(1).to_broadcast([P, 4, P])

        def quarter(ap, b):
            return ap[:, 4 * b:4 * b + 4, :]

        def wide(ap):
            return ap.unsqueeze(2).to_broadcast([P, ap.shape[1], P])

        def used(eng, n, turns=0):
            eng.wait_ge(wt_used, RING + n + 1 + RING * turns)

        block = ctx.enter_context(nc.Block())

        @block.sync
        def _(sp):
            def claim(n, turns):
                sp.wait_ge(lo_ready, n + 1 + RING * turns)

            def load_in_pair(n, w, j, c, turns=0):
                claim(n, turns)
                rows = w.rearrange("(j k p) n -> j p k n", k=4, p=P)[j]
                dst = raw[:, n % RING, :].rearrange("p (k h n) -> p k h n", k=4, h=2)
                for h in range(2):
                    sp.dma_start(dst[:, :, h, :], rows[:, :, bass.ds(c * 256 + h * FF, 256)])\
                        .then_inc(raw_full[n % RING], 16)

            def load_in(n, w, j, col, turns=0):
                claim(n, turns)
                rows = w.rearrange("(j k p) n -> j p k n", k=4, p=P)[j]
                dst = raw[:, n % RING, :].rearrange("p (k n) -> p k n", k=4)
                for h in range(2):
                    sp.dma_start(dst[:, 2 * h:2 * h + 2, :], rows[:, 2 * h:2 * h + 2, bass.ds(col, 512)])\
                        .then_inc(raw_full[n % RING], 16)

            def load_out(n, w, r, turns=0):
                claim(n, turns)
                for h in range(2):
                    sp.dma_start(raw[:, n % RING, h * D:(h + 1) * D], w[bass.ds(r * 256 + h * P, P), :])\
                        .then_inc(raw_full[n % RING], 16)

            def load_gain(g):
                if g >= norms:
                    return
                if g >= 2:
                    sp.wait_ge(xg_ready, 4 * (g - 1))
                sp.dma_start(gains[:, g % 2, :], norm_gains[g].partition_broadcast(P)).then_inc(gain_full[g % 2], 16)

            def ffn(f, n0):
                w_in, w_out = ffn_weights[f]
                for j in range(2):
                    load_in_pair(n0 + j, w_in, j, 0)
                with sp.Fori(0, FFC - 1) as i:
                    for j in range(2):
                        load_in_pair(n0 + 2 + j, w_in, j, i + 1, turns=i)
                    load_out(n0 + 4, w_out, i, turns=i)
                load_out(n0 + FFN_BLOCKS - 1, w_out, FFC - 1)

            def project(n0, w, chunks):
                with sp.Fori(0, chunks // 3) as i:
                    for u in range(6):
                        load_in(n0 + u, w, u % 2, i * 1536 + u // 2 * 512, turns=2 * i)
                for u in range(chunks // 3 * 6, chunks * 2):
                    load_in(n0 + u, w, u % 2, u // 2 * 512)

            def out_blocks(n0, w, count):
                for r in range(count):
                    load_out(n0 + r, w, r)

            def ff2(n0):
                w_in, w_out = A["w_ff1_2"][0], A["w_ff2_2"][0]

                def chunk(c, n, turns=0):
                    for j in range(2):
                        load_in(n + j, w_in, j, c * 512, turns)
                    for r in range(2):
                        load_out(n + 2 + r, w_out, c * 2 + (r - 2), turns)

                for j in range(2):
                    load_in(n0 + j, w_in, j, 0)
                with sp.Fori(0, 2) as i:
                    for u in range(3):
                        chunk(3 * i + (1 + u), n0 + 2 + 4 * u, turns=4 * i)
                chunk(FF2C - 1, n0 + 4 * FF2C - 6)
                for r in range(2):
                    load_out(n0 + 4 * FF2C - 2 + r, w_out, FF2C * 2 - 2 + r)

            load_gain(1)
            ffn(0, first["ffn0"])
            if "da_in" in live:
                load_gain(2)
                project(first["da_in"], A["da_w_in"][0], 6)
                out_blocks(first["da_out"], A["da_w_out"][0], 4)
            if "ffn1" in live:
                load_gain(3)
                ffn(1, first["ffn1"])
            if "ffn2" in live:
                load_gain(4)
                ffn(2, first["ffn2"])
            if "rt_in" in live:
                load_gain(5)
                project(first["rt_in"], A["rt_w_in"][0], 12)
                out_blocks(first["rt_out"], A["rt_w_out"][0], 8)
            if "ffn3" in live:
                load_gain(6)
                ffn(3, first["ffn3"])
            if "mix_in" in live:
                load_gain(7)
                for u in range(14):
                    load_in(first["mix_in"] + u, A["w_in_2"][0], u % 2, (1536 + u // 2 * 512) if u < 8 else (u // 2 - 4) * 512)
                out_blocks(first["mix_out"], A["w_out_2"][0], 4)
            if "ff2" in live:
                ff2(first["ff2"])
            if stop != 99:
                load_out(total - 2, A["ffn1_w_out"][0], 0)
                load_out(total - 1, A["ffn1_w_out"][0], 0)
            sp.wait_ge(x_stored, 64)

        @block.scalar
        def _(act):
            def split(n, turns=0):
                if n >= total and isinstance(turns, int):
                    return
                act.wait_ge(raw_full[n % RING], 32 * (n // RING + 1) + 32 * turns)
                used(act, n - RING, turns)
                act.activation(w_hi[:, n % RING, :], raw[:, n % RING, :], ACT.Copy).then_inc(hi_ready, 1)

            def norm(g):
                for q in range(4):
                    act.wait_ge(xt_psum, 4 * g + q + 1)
                    act.activation(turned(xT_hi, q), by_four(bank[4 + q][:, :]), ACT.Copy)\
                        .then_inc(xt_hi_ready, 1)
                    if q >= 2:
                        if g:
                            act.wait_ge(resid_done, 4 * (g - 1) + q + 1)
                        else:
                            act.wait_ge(x_full, 16)
                        if 2 * g + q > 2:
                            act.wait_ge(ss_ready, 2 * g + q - 2)
                        act.activation(square[:, :], x[:, q - 2, :], ACT.Square,
                                       accum_out=sumsq[:, q - 2:q - 1]).then_inc(ss_ready, 1)

            def ffn(f, n0):
                cb = FFC * f

                def silu(c, i=0):
                    for t in range(2):
                        if t == 0:
                            act.wait_ge(in_done, cb + c + 1 + i)
                        else:
                            used(act, n0 + (1 if c == 0 else 3), i)
                        if c == 0 and t == 0:
                            act.wait_ge(rstd_ready, NORM_OF[f"ffn{f}"] + 1)
                        act.activation(silu_a[:, t, :], bank[4 + t][:, 0:256], ACT.Silu, scale=rstd[:, t:t + 1])\
                            .then_inc(silu_ready, 1)

                def turn_hidden(c, i=0):
                    act.wait_ge(ht_psum, cb + c + 1 + i)
                    act.activation(hT_hi[:, 0:2, :], bank[6][:, :].rearrange("p (k n) -> p k n", k=2), ACT.Copy)\
                        .then_inc(ht_hi_ready, 1)

                split(n0 + 2)
                split(n0 + 3)
                silu(0)
                with act.Fori(0, FFC - 1) as i:
                    turn_hidden(0, i)
                    split(n0 + 4, turns=i)
                    split(n0 + 5, turns=i)
                    silu(1, i)
                    split(n0 + 6, turns=i)
                turn_hidden(FFC - 1)
                split(n0 + FFN_BLOCKS + 1)

            def ff2(n0):
                def take_relu(c, n, i=0, turns=0):
                    for t in range(2):
                        if t == 0:
                            act.wait_ge(in2_done, c + 1 + i)
                            if c == 0:
                                act.wait_ge(rstd_ready, 8)
                        else:
                            used(act, n, turns)
                        act.activation(relu[:, t, :], bank[4 + t][:, :], ACT.Relu, scale=rstd[:, t:t + 1])\
                            .then_inc(relu_ready, 1)

                def turn_hidden(c, i=0):
                    for b in range(2):
                        act.wait_ge(ht2_psum, 2 * c + b + 1 + 2 * i)
                        act.activation(flat(hT_hi[:, 2 * b:2 * b + 2, :]), bank[6 + b][:, :], ACT.Copy)\
                            .then_inc(ht2_hi_ready, 1)

                def chunk(c, n, i=0, turns=0):
                    turn_hidden(c - 1, i)
                    split(n + 2, turns)
                    split(n + 3, turns)
                    take_relu(c, n + 1, i, turns)
                    split(n + 4, turns)
                    split(n + 5, turns)

                split(n0 + 2)
                split(n0 + 3)
                take_relu(0, n0 + 1)
                with act.Fori(0, 2) as i:
                    for u in range(3):
                        chunk(1 + u, n0 + 2 + 4 * u, 3 * i, 4 * i)
                chunk(FF2C - 1, n0 + 4 * FF2C - 6)
                turn_hidden(FF2C - 1)

            def read_chunk(n0, m0, m, dst, func=ACT.Copy, pair=None):
                for t in range(2):
                    if t == 0:
                        act.wait_ge(proj_done, m0 + m + 1)
                        if m == 0:
                            act.wait_ge(rstd_ready, PROJ_NORM[m0] + 1)
                    else:
                        used(act, n0 + 2 * m + 1)
                    act.activation(dst[:, t, :], bank[(m % 3 if pair is None else pair) * 2 + t][:, :], func, scale=rstd[:, t:t + 1])\
                        .then_inc(proj_read, 1)

            def load_da():
                for s, name in enumerate(("da_q_gain", "da_k_gain")):
                    for m in range(2):
                        act.dma_start(da_gain[m * DA_DH:(m + 1) * DA_DH, s:s + 1],
                                      A[name].rearrange("a d -> d a")).then_inc(da_small, 16)
                act.dma_start(da_lam[:, :, :], A["da_lambda"][0].partition_broadcast(P)).then_inc(da_small, 16)
                act.dma_start(subln[:, :], A["da_subln"][0].partition_broadcast(P)).then_inc(da_small, 16)
                act.dma_start(bias[:, :, :].rearrange("p h n -> p (h n)"), A["c_alibi"]).then_inc(bias_full, 16)

            def da():
                n0, n1 = first["da_in"], first["da_out"]
                norm(1)
                for m in range(6):
                    split(n0 + 2 * m + 2)
                    split(n0 + 2 * m + 3)
                    read_chunk(n0, 0, m, da_proj[:, :, m * 512:m * 512 + 512])
                    if m == 0:
                        act.wait_ge(da_lamsum, 1)
                        act.activation(lam_exp[:, 0:2], lam_exp[:, 2:4], ACT.Exp).then_inc(da_lamexp, 1)
                for c in range(4):
                    act.wait_ge(da_turned, 2 * c + 1)
                    act.activation(qT[:, 2 * c:2 * c + 2, :].rearrange("p h n -> p (h n)"), bank[2 * c][:, :], ACT.Copy,
                                   scale=da_gain[:, 0:1]).then_inc(da_qT, 1)
                for i in range(DA_H + 3):
                    if i < DA_H:
                        act.wait_ge(da_max, 4 * i + 4)
                        if i >= 2:
                            act.wait_ge(da_mixed, 2 * (i - 1))
                        for m in range(2):
                            for b in range(2):
                                cols = slice(0, P) if b == 0 else slice(P, 384)
                                act.activation(prob[:, i % 2, m, cols], bank[4 + m][:, cols], ACT.Exp,
                                               bias=neg_max[:, i % 2, 2 * m + b:2 * m + b + 1],
                                               accum_out=p_sum[:, i % 2, 2 * m + b:2 * m + b + 1]).then_inc(da_exp, 1)
                    if 1 <= i <= DA_H:
                        act.wait_ge(da_mixT_psum, i)
                        if i >= 2:
                            act.wait_ge(da_o, i - 1)
                        act.activation(mixT[:, :], bank[6][:, 0:384], ACT.Copy).then_inc(da_mixT, 1)
                        act.wait_ge(da_o, i)
                        for t in range(2):
                            if i >= 2 or t:
                                act.wait_ge(da_oss, 2 * (i - 1) + t)
                            if i >= 2:
                                act.wait_ge(da_orstd, i - 1)
                            act.activation(square[:, 0:P], bank[7][:, t * P:t * P + P], ACT.Square,
                                           accum_out=head_ss[:, t:t + 1]).then_inc(da_oss, 1)
                    if 2 <= i <= DA_H + 1:
                        h = i - 2
                        act.wait_ge(da_oT_psum, h + 1)
                        act.activation(xT_hi[:, h, :], bank[6][:, 0:T], ACT.Copy).then_inc(da_oT_hi, 1)
                    if i >= 4 and i % 2 == 0:
                        split(n1 + (i - 4) // 2 + 2)

            def rt():
                n0, n1 = first["rt_in"], first["rt_out"]
                act.wait_ge(da_scores, 2 * DA_H)
                act.dma_start(bias[:, 0:RT_H, :].rearrange("p h n -> p (h n)"), A["c_decay"]).then_inc(rt_small, 16)
                norm(4)
                act.wait_ge(xt_psum, 4 * 5)
                act.dma_start(xg[:, :, :], A["rt_subln"][0].rearrange("(a h) v -> a (h v)", a=2).partition_broadcast(P))\
                    .then_inc(rt_small, 16)
                for m in range(12):
                    split(n0 + 2 * m + 2)
                    if m in (6, 7):
                        for c in range(2 * (m - 6), 2 * (m - 6) + 2):
                            act.wait_ge(rt_turned, 2 * c + 1)
                            act.activation(qT[:, 2 * c:2 * c + 2, :].rearrange("p h n -> p (h n)"), bank[6][:, :],
                                           ACT.Copy).then_inc(rt_qT, 1)
                    split(n0 + 2 * m + 3)
                    read_chunk(n0, 6, m, rt_chunk[m], ACT.Silu if m >= 8 else ACT.Copy, rt_pair[m])
                    if m >= 8:
                        h = m - 8
                        act.wait_ge(rt_o, h + 1)
                        for t in range(2):
                            if h:
                                act.wait_ge(rt_oss, 2 * h)
                                act.wait_ge(rt_orstd, h)
                            act.activation(square[:, t * 512:t * 512 + 512], bank[4 + t][:, :], ACT.Square,
                                           accum_out=head_ss[:, t:t + 1]).then_inc(rt_oss, 1)

                def turned_y(h):
                    for t in range(2):
                        act.wait_ge(rt_yT_psum, 2 * h + t + 1)
                        act.activation(xT_hi[:, h % 2 * 4:h % 2 * 4 + 4, t * P:t * P + P], by_four(bank[6 + t][:, :]),
                                       ACT.Copy).then_inc(rt_yT_hi, 1)

                turned_y(0)
                turned_y(1)
                for h in range(RT_H):
                    split(n1 + 2 * h + 2)
                    split(n1 + 2 * h + 3)
                    if h < 2:
                        turned_y(h + 2)

            def load_mix():
                w = A["w_in_2"][0].rearrange("(k p) n -> p k n", p=P)
                act.dma_start(tail_w[:, :, :], w[:, :, 3584:3592]).then_inc(mx_small, 16)
                for dst, src in ((a_log, A["dn_a_log_2"][0]), (dt_bias, A["dn_dt_bias_2"][0])):
                    act.dma_start(dst[:, :], src.partition_broadcast(P)).then_inc(mx_small, 16)
                for s, name in enumerate(("att_q_gain_2", "att_k_gain_2")):
                    for m in range(2):
                        act.dma_start(att_gain[m * AT_DH:(m + 1) * AT_DH, s:s + 1],
                                      A[name].rearrange("a d -> d a")).then_inc(mx_small, 16)

            def mix():
                n0, n1 = first["mix_in"], first["mix_out"]
                act.wait_ge(rt_decayed, 2 * RT_H)
                act.dma_start(bias[:, :, :], bass.AP(A["rel_bias_2"].tensor, MAX_REL - (P - 1), [[1, P], [N_REL, AT_H], [1, T]]))\
                    .then_inc(mx_bias, 16)
                norm(6)
                act.wait_ge(xg_ready, 28)
                act.dma_start(flip, A["c_flip"]).then_inc(mx_small, 16)
                act.dma_start(conv_row, A["dn_conv_w_2"][0].rearrange("j (c p) -> (j c) p", p=P)).then_inc(mx_small, 16)
                act.dma_start(dn_gain, A["dn_out_gain_2"][0].partition_broadcast(P)).then_inc(mx_small, 16)
                act.dma_start(out_gain, A["att_out_gain_2"][0].partition_broadcast(P)).then_inc(mx_small, 16)
                act.wait_ge(mx_small, MX_SMALL)
                act.activation(tail_hi[:, :, :], tail_w[:, :, :], ACT.Copy).then_inc(mx_tail_hi, 1)
                dst = [mx_dn[:, m, :, :] for m in range(3)] + [mx_gate] + [mx_att[:, m, :, :] for m in range(3)]
                for m in range(7):
                    split(n0 + 2 * m + 2)
                    split(n0 + 2 * m + 3)
                    read_chunk(n0, 18, m, dst[m], ACT.Silu if m == 3 else ACT.Copy)
                act.wait_ge(mx_tail, 1)
                for t in range(2):
                    act.activation(tail_ab[:, t, :], bank[6][:, t * 8:t * 8 + 8], ACT.Copy, scale=rstd[:, t:t + 1])\
                        .then_inc(mx_ab, 1)
                act.wait_ge(mx_convw_psum, 1)
                act.activation(conv_w[:, :], bank[7][:, 0:48], ACT.Copy).then_inc(mx_convw, 1)
                act.wait_ge(mx_abs, 1)
                act.activation(ez, uu, ACT.Exp, scale=-1.0).then_inc(mx_exp, 1)
                act.activation(dd.rearrange("p (t h) -> p t h", t=2), tail_ab[:, :, 4:8], ACT.Exp, scale=-1.0)\
                    .then_inc(mx_exp, 1)
                act.activation(ea[:, :], a_log[:, :], ACT.Exp).then_inc(mx_exp, 1)
                act.wait_ge(mx_onep, 1)
                act.activation(ln, uu, ACT.Ln).then_inc(mx_ln, 1)
                act.wait_ge(mx_zero, 1)
                for c in range(0, 6, 2):
                    act.wait_ge(mx_conv_psum, c + 1)
                    act.activation(conv_in[:, 2 * c:2 * c + 2, 3:3 + T],
                                   bank[c][:, :].rearrange("p (k n) -> p k n", k=2), ACT.Copy).then_inc(mx_conv_in, 1)
                act.wait_ge(mx_dec, 1)
                act.activation(edec, dec, ACT.Exp).then_inc(mx_etail, 1)
                act.wait_ge(mx_last_diff, 1)
                act.activation(etail, etail, ACT.Exp).then_inc(mx_etail, 1)
                act.wait_ge(mx_rows, 1)
                act.wait_ge(mx_diff, 8)
                for b in range(2):
                    act.activation(flat(quarter(dn_exprow, b)), bank[b][:, :], ACT.Exp).then_inc(mx_exprow, 1)
                act.activation(flat(dn_LT), flat(dn_LT), ACT.Exp).then_inc(mx_exprow, 1)
                for s in range(3):
                    act.wait_ge(mx_conv, 4 * s + 4)
                    act.activation(flat(conv_out[s]), flat(conv_out[s]), ACT.Silu).then_inc(mx_silu, 1)
                for s in range(2):
                    for t in range(2):
                        act.wait_ge(mx_tok_psum, 2 * s + t + 1)
                        act.activation(flat(quarter(dn_tok[s], t)), bank[4 + s * 2 + t][:, :], ACT.Copy).then_inc(mx_tok, 1)
                for s in range(2):
                    if s:
                        act.wait_ge(mx_dnss, 1)
                    act.wait_ge(mx_tok, 2 * s + 2)
                    act.activation(flat(sq8), flat(dn_tok[s]), ACT.Square).then_inc(mx_dnsq, 1)
                for s in range(2):
                    for t in range(2):
                        act.wait_ge(mx_back_psum, 2 * s + t + 1)
                        act.activation((dn_qhT, dn_khT)[s][:, :, t * P:t * P + P], by_four(bank[4 + s * 2 + t][:, :]),
                                       ACT.Copy).then_inc(mx_back, 1)
                for n in range(1, LEVELS):
                    for b in range(2):
                        act.wait_ge(mx_Y, 2 * (n - 1) + b + 1)
                        act.activation(flat(quarter(dn_Y, b)), bank[b][:, :], ACT.Copy).then_inc(mx_Ysb, 1)
                act.wait_ge(mx_val, 1)
                for b in range(2):
                    act.activation(flat(quarter(dn_val, b)), bank[b][:, :], ACT.Copy).then_inc(mx_valsb, 1)
                for t in range(2):
                    act.wait_ge(mx_O, 2 * t + 2)
                    if t == 0:
                        act.wait_ge(mx_dnss, 2)
                    act.activation(square[:, t * 512:t * 512 + 512], bank[4 + t][:, :], ACT.Square).then_inc(mx_osq, 1)
                for c in range(2):
                    act.wait_ge(mx_aT_psum, 2 * c + 1)
                    act.activation(flat(qT[:, 2 * c:2 * c + 2, :]), bank[2 * c][:, :], ACT.Copy, scale=att_gain[:, 0:1])\
                        .then_inc(mx_aq, 1)
                for i in range(AT_H + 1):
                    if i < AT_H:
                        act.wait_ge(mx_max, 2 * i + 2)
                        if i >= 2:
                            act.wait_ge(mx_PT_psum, i - 1)
                        for b in range(2):
                            cols = slice(0, P) if b == 0 else slice(P, 384)
                            act.activation(prob_a[:, i % 2, cols], bank[i % 2][:, cols], ACT.Exp,
                                           bias=att_max[:, i, b:b + 1], accum_out=att_sum[:, b, i:i + 1]).then_inc(mx_P, 1)
                    if i:
                        h = i - 1
                        act.wait_ge(mx_PT_psum, h + 1)
                        if h:
                            act.wait_ge(mx_AV, h)
                        act.activation(probT, bank[2 + h % 2][:, 0:384], ACT.Copy).then_inc(mx_PT, 1)
                for t in range(2):
                    act.wait_ge(mx_ao, t + 1)
                    act.activation(square[:, t * 512:t * 512 + 512], att_y[:, t, :], ACT.Square,
                                   accum_out=head_ss[:, t:t + 1]).then_inc(mx_aoss, 1)
                for p in range(2):
                    for t in range(2):
                        act.wait_ge(mx_yT_psum, 2 * p + t + 1)
                        k0 = 4 - 4 * p
                        act.activation(xT_hi[:, k0:k0 + 4, t * P:t * P + P], by_four(bank[6 + t][:, :]), ACT.Copy)\
                            .then_inc(mx_yT_hi, 1)
                for r in range(4):
                    split(n1 + r + 2)
            act.sem_inc(proj_read, 6)
            act.dma_start(x[:, :, :], A["x"][0].rearrange("(t p) d -> p t d", p=P)).then_inc(x_full, 16)
            act.dma_start(gains[:, 0, :], norm_gains[0].partition_broadcast(P)).then_inc(gain_full[0], 16)
            act.dma_start(table[:, :], A["c_table"]).then_inc(table_full, 16)
            split(0)
            split(1)
            norm(0)
            load_da()
            load_mix()
            ffn(0, first["ffn0"])
            if "da_in" in live:
                da()
            if "ffn1" in live:
                norm(2)
                ffn(1, first["ffn1"])
            if "ffn2" in live:
                norm(3)
                ffn(2, first["ffn2"])
            if "rt_in" in live:
                rt()
            if "ffn3" in live:
                norm(5)
                ffn(3, first["ffn3"])
            if "mix_in" in live:
                mix()
            if "ff2" in live:
                norm(7)
                ff2(first["ff2"])
            for q in range(4):
                act.wait_ge(resid_done, 4 * (len(last_out) - 1) + q + 1)
                act.dma_start(out[0].rearrange("(t p) d -> p t d", p=P)[:, q % 2, q // 2 * 512:q // 2 * 512 + 512],
                              piece(x, q)).then_inc(x_stored, 16)

        @block.gpsimd
        def _(pool):
            chain = [0]

            def link(ins):
                chain[0] += 1
                ins.then_inc(pool_chain, 1)
                pool.wait_ge(pool_chain, chain[0])

            def norm(g):
                pool.wait_ge(ss_ready, 2 * (g + 1))
                link(pool.tensor_scalar(meansq[:, :], sumsq[:, :], 1.0 / D, EPS, ALU.mult, ALU.add))
                pool.tensor_tensor(rstd[:, :], meansq[:, :], neghalf[:, 0:2], ALU.pow).then_inc(rstd_ready, 1)

            def da():
                pool.wait_ge(da_small, 16 * 6)
                link(pool.tensor_scalar(da_gain[:, 0:1], da_gain[:, 0:1], DA_DH ** -0.5, None, ALU.mult))
                pool.tensor_scalar(subln[:, :], subln[:, :], 1.0 - LAM_INIT, None, ALU.mult).then_inc(da_small, 16)
                norm(1)
                for s in range(2):
                    pool.wait_ge(proj_read, 6 + 4 * (s + 1))
                    for t in range(2):
                        qk = da_proj[:, t, s * D:s * D + D]
                        if s:
                            pool.wait_ge(da_sumsq, t + 1)
                        pool.tensor_tensor(xg[:, t, :], qk, qk, ALU.mult).then_inc(da_square, 1)
                    for t in range(2):
                        u = 2 * s + t
                        pool.wait_ge(da_sumsq, u + 1)
                        link(pool.tensor_scalar(qk_ss[:, u, :], qk_ss[:, u, :], 1.0 / DA_DH, EPS, ALU.mult, ALU.add))
                        pool.tensor_tensor(qk_rstd[:, u, :], qk_ss[:, u, :], neghalf[:, 0:16], ALU.pow).then_inc(da_rstd, 1)
                for h in range(DA_H):
                    pool.wait_ge(da_oss, 2 * h + 2)
                    link(pool.tensor_scalar(meansq[:, :], head_ss[:, :], 1.0 / P, EPS, ALU.mult, ALU.add))
                    if h:
                        pool.wait_ge(da_normed_o, 2 * h)
                    pool.tensor_tensor(head_rstd[:, :], meansq[:, :], neghalf[:, 0:2], ALU.pow).then_inc(da_orstd, 1)

            def rt():
                norm(4)
                pool.wait_ge(rt_small, 32)
                for h in range(RT_H):
                    pool.wait_ge(proj_read, 6 + 2 * (6 + 8 + h + 1))
                    for t in range(2):
                        gate = rt_g[:, t, h * 512:h * 512 + 512]
                        pool.tensor_tensor(gate, gate, xg[:, h // 2, h % 2 * 512:h % 2 * 512 + 512], ALU.mult)\
                            .then_inc(rt_gate, 1)
                    pool.wait_ge(rt_oss, 2 * h + 2)
                    link(pool.tensor_scalar(meansq[:, :], head_ss[:, :], 1.0 / RT_DV, EPS, ALU.mult, ALU.add))
                    if h:
                        pool.wait_ge(rt_y, 2 * h)
                    pool.tensor_tensor(head_rstd[:, :], meansq[:, :], neghalf[:, 0:2], ALU.pow).then_inc(rt_orstd, 1)

            def mix():
                pool.wait_ge(mx_small, MX_SMALL)
                link(pool.tensor_scalar(att_gain[:, 0:1], att_gain[:, 0:1], AT_DH ** -0.5, None, ALU.mult))
                norm(6)
                pool.wait_ge(mx_bias, 16)
                pool.wait_ge(rstd_ready, 7)
                pool.memset(bias[0:CHUNK, :, 0:CHUNK], MASKED).then_inc(mx_bias, 1)
                pool.wait_ge(mx_bias, 17)
                for s in range(2):
                    pool.wait_ge(mx_dnss, s + 1)
                    link(pool.tensor_scalar(dn_ss[:, s, :], dn_ss[:, s, :], EPS, None, ALU.add))
                    ins = pool.tensor_tensor(dn_rstd[:, s, :], dn_ss[:, s, :], neghalf[:, 0:8], ALU.pow)
                    if s == 0:
                        link(ins)
                        ins = pool.tensor_scalar(dn_rstd[:, 0, :], dn_rstd[:, 0, :], DN_D ** -0.5, None, ALU.mult)
                    ins.then_inc(mx_dnr, 1)
                pool.wait_ge(mx_back_psum, 4)
                pool.tensor_tensor(dn_kbe, dn_tok[1], wide(bed), ALU.mult).then_inc(mx_ktail, 1)
                pool.wait_ge(mx_ktail, 1)
                pool.tensor_tensor(dn_ktail, dn_tok[1], wide(etail), ALU.mult).then_inc(mx_ktail, 1)
                pool.wait_ge(mx_gram, 2)
                pool.tensor_tensor(dn_qhT[:, :, 0:P], dn_qhT[:, :, 0:P], quarter(dn_exprow, 0), ALU.mult)\
                    .then_inc(mx_ktail, 1)
                pool.tensor_tensor(dn_qhT[:, :, P:T], dn_qhT[:, :, P:T], quarter(dn_exprow, 1), ALU.mult)\
                    .then_inc(mx_qd, 1)
                for t in range(2):
                    pool.tensor_tensor(by_four(mx_gate[:, t, :]), by_four(mx_gate[:, t, :]),
                                       dn_gain[:, :].unsqueeze(1).to_broadcast([P, 4, P]), ALU.mult).then_inc(mx_gate_gain, 1)
                pool.wait_ge(mx_oss, 2)
                link(pool.tensor_scalar(dn_ss[:, 0, :], dn_ss[:, 0, :], 1.0 / DN_D, EPS, ALU.mult, ALU.add))
                pool.tensor_tensor(dn_rstd[:, 0, :], dn_ss[:, 0, :], neghalf[:, 0:8], ALU.pow).then_inc(mx_or, 1)
                for s in range(2):
                    for t in range(2):
                        u = 2 * s + t
                        if s:
                            pool.wait_ge(mx_ass, t + 1)
                        pool.tensor_tensor(square[:, t * 512:t * 512 + 512], mx_att[:, s, t, :], mx_att[:, s, t, :],
                                           ALU.mult).then_inc(mx_asq, 1)
                    pool.wait_ge(mx_ass, 2 * s + 2)
                    at = slice(16 * s, 16 * s + 16)
                    link(pool.tensor_scalar(att_ss[:, at], att_ss[:, at], 1.0 / AT_DH, EPS, ALU.mult, ALU.add))
                    pool.tensor_tensor(att_rs[:, at], att_ss[:, at], neghalf[:, 0:16], ALU.pow).then_inc(mx_ars, 1)
                pool.wait_ge(mx_aoss, 2)
                link(pool.tensor_scalar(meansq[:, :], head_ss[:, :], 1.0 / 512, EPS, ALU.mult, ALU.add))
                pool.tensor_tensor(head_rstd[:, :], meansq[:, :], neghalf[:, 0:2], ALU.pow).then_inc(mx_aor, 1)
            link(pool.memset(neghalf[:, :], -0.5))
            norm(0)
            if "da_in" in live:
                da()
            if "ffn1" in live:
                norm(2)
            if "ffn2" in live:
                norm(3)
            if "rt_in" in live:
                rt()
            if "ffn3" in live:
                norm(5)
            if "mix_in" in live:
                mix()
            if "ff2" in live:
                norm(7)

        @block.vector
        def _(dve):
            chain = [0]

            def link(ins):
                chain[0] += 1
                ins.then_inc(dve_chain, 1)
                dve.wait_ge(dve_chain, chain[0])

            def split(n, turns=0):
                if n >= total and isinstance(turns, int):
                    return
                dve.wait_ge(hi_ready, n + 1 + RING * turns)
                dve.tensor_tensor(w_lo[:, n % RING, :], raw[:, n % RING, :], w_hi[:, n % RING, :].bitcast(F32),
                                  ALU.subtract).then_inc(lo_ready, 1)

            def ff2(n0):
                def square_relu(c, i=0):
                    for t in range(2):
                        dve.wait_ge(relu_ready, 2 * c + t + 1 + 2 * i)
                        dve.tensor_tensor(hid[:, t, :], relu[:, t, :], relu[:, t, :], ALU.mult).then_inc(sq_ready, 1)

                def turn_hidden(c, i=0):
                    for b in range(2):
                        dve.wait_ge(ht2_hi_ready, 2 * c + b + 1 + 2 * i)
                        dve.tensor_tensor(flat(hT_lo[:, 2 * b:2 * b + 2, :]), bank[6 + b][:, :],
                                          flat(hT_hi[:, 2 * b:2 * b + 2, :]).bitcast(F32), ALU.subtract)\
                            .then_inc(ht2_lo_ready, 1)

                def chunk(c, n, i=0, turns=0):
                    turn_hidden(c - 1, i)
                    split(n + 2, turns)
                    split(n + 3, turns)
                    square_relu(c, i)
                    split(n + 4, turns)
                    split(n + 5, turns)

                split(n0 + 2)
                split(n0 + 3)
                square_relu(0)
                with dve.Fori(0, 2) as i:
                    for u in range(3):
                        chunk(1 + u, n0 + 2 + 4 * u, 3 * i, 4 * i)
                chunk(FF2C - 1, n0 + 4 * FF2C - 6)
                turn_hidden(FF2C - 1)

            def residual(phase, q, scale):
                if q < 3:
                    dve.wait_ge(acc_done, 3 * phase + q + 1)
                else:
                    used(dve, last_out[phase])
                dve.scalar_tensor_tensor(piece(x, q), bank[q][:, :], scale, piece(x, q), ALU.mult, ALU.add)\
                    .then_inc(resid_done, 1)
                dve.wait_ge(resid_done, 4 * phase + q + 1)

            def norm(g, scale=None):
                def lo(q):
                    dve.wait_ge(xt_hi_ready, 4 * g + q + 1)
                    dve.tensor_tensor(turned(xT_lo, q), by_four(bank[4 + q][:, :]), turned(xT_hi, q).bitcast(F32),
                                      ALU.subtract).then_inc(xt_lo_ready, 1)

                dve.wait_ge(gain_full[g % 2], 16 * (g // 2 + 1))
                for q in range(4):
                    if g:
                        residual(g - 1, q, scale)
                    else:
                        dve.wait_ge(x_full, 16)
                    dve.tensor_tensor(piece(xg, q), piece(x, q), gains[:, g % 2, q // 2 * 512:q // 2 * 512 + 512], ALU.mult).then_inc(xg_ready, 1)
                    if q >= 2:
                        lo(q - 2)
                lo(2)
                lo(3)

            def ffn(f, n0):
                cb = FFC * f

                def times_b(c, i=0):
                    for t in range(2):
                        dve.wait_ge(silu_ready, 2 * (cb + c) + t + 1 + 2 * i)
                        dve.scalar_tensor_tensor(hid[:, t, 0:256], bank[4 + t][:, 256:512], rstd[:, t:t + 1],
                                                 silu_a[:, t, :], ALU.mult, ALU.mult).then_inc(hid_ready, 1)

                def turn_hidden(c, i=0):
                    dve.wait_ge(ht_hi_ready, cb + c + 1 + i)
                    dve.tensor_tensor(hT_lo[:, 0:2, :], bank[6][:, :].rearrange("p (k n) -> p k n", k=2),
                                      hT_hi[:, 0:2, :].bitcast(F32), ALU.subtract).then_inc(ht_lo_ready, 1)

                split(n0 + 2)
                split(n0 + 3)
                times_b(0)
                with dve.Fori(0, FFC - 1) as i:
                    turn_hidden(0, i)
                    split(n0 + 4, turns=i)
                    split(n0 + 5, turns=i)
                    times_b(1, i)
                    split(n0 + 6, turns=i)
                turn_hidden(FFC - 1)
                split(n0 + FFN_BLOCKS + 1)

            def da():
                n0, n1 = first["da_in"], first["da_out"]
                norm(1, 0.5)
                for m in range(6):
                    split(n0 + 2 * m + 2)
                    split(n0 + 2 * m + 3)
                    if m == 0:
                        dve.wait_ge(da_small, 16 * 6)
                        link(dve.tensor_tensor(lam_prod[:, :, :], da_lam[:, 0::2, :], da_lam[:, 1::2, :], ALU.mult))
                        dve.tensor_reduce(lam_exp[:, 2:4], lam_prod[:, :, :], AX_X, ALU.add).then_inc(da_lamsum, 1)
                    if m == 1:
                        dve.wait_ge(da_lamexp, 1)
                        link(dve.scalar_tensor_tensor(lam[:, :], lam_exp[:, 0:1], LAM_INIT, lam_exp[:, 1:2],
                                                      ALU.add, ALU.subtract))
                    if m in (2, 4):
                        s = m // 2 - 1
                        for t in range(2):
                            u = 2 * s + t
                            dve.wait_ge(da_square, u + 1)
                            dve.tensor_reduce(qk_ss[:, u, :], xg[:, t, :].rearrange("p (g d) -> p g d", d=DA_DH),
                                              AX_X, ALU.add).then_inc(da_sumsq, 1)
                    if m in (3, 5):
                        s = m // 2 - 1
                        for t in range(2):
                            u = 2 * s + t
                            dve.wait_ge(da_rstd, u + 1)
                            qk = da_proj[:, t, s * D:s * D + D].rearrange("p (g d) -> p g d", d=DA_DH)
                            dve.tensor_tensor(qk, qk, qk_rstd[:, u, :].unsqueeze(2).to_broadcast([P, 16, DA_DH]),
                                              ALU.mult).then_inc(da_normed, 1)
                for c in range(4):
                    dve.wait_ge(da_turned, 2 * c + 2)
                    dve.tensor_scalar(kT[:, 2 * c:2 * c + 2, :].rearrange("p h n -> p (h n)"), bank[2 * c + 1][:, :],
                                      da_gain[:, 1:2], None, ALU.mult).then_inc(da_kT, 1)
                for i in range(DA_H + 3):
                    if i < DA_H:
                        for m in range(2):
                            dve.wait_ge(da_scores, 2 * i + m + 1)
                            if i >= 2 and m == 0:
                                dve.wait_ge(da_exp, 4 * (i - 1))
                            for b in range(2):
                                cols = slice(0, P) if b == 0 else slice(P, 384)
                                dve.tensor_reduce(neg_max[:, i % 2, 2 * m + b:2 * m + b + 1], bank[4 + m][:, cols],
                                                  AX_X, ALU.max, negate=True).then_inc(da_max, 1)
                    if 1 <= i <= DA_H:
                        h = i - 1
                        dve.wait_ge(da_exp, 4 * h + 4)
                        if h >= 2:
                            dve.wait_ge(da_mixT_psum, h - 1)
                        link(dve.reciprocal(p_recip[:, :], p_sum[:, h % 2, :]))
                        link(dve.tensor_scalar(recip_lam[:, :], p_recip[:, 2:4], lam[:, :], None, ALU.mult))
                        for b in range(2):
                            cols = slice(0, P) if b == 0 else slice(P, 384)
                            last = dve.tensor_scalar(prob1[:, cols], prob[:, h % 2, 1, cols], recip_lam[:, b:b + 1],
                                                     None, ALU.mult)
                            if b:
                                link(last)
                        for b in range(2):
                            cols = slice(0, P) if b == 0 else slice(P, 384)
                            dve.scalar_tensor_tensor(mixed[:, h % 2, cols], prob[:, h % 2, 0, cols], p_recip[:, b:b + 1],
                                                     prob1[:, cols], ALU.mult, ALU.subtract).then_inc(da_mixed, 1)
                        dve.wait_ge(da_mixed, 2 * h + 2)
                    if 2 <= i <= DA_H + 1:
                        h = i - 2
                        dve.wait_ge(da_orstd, h + 1)
                        if h:
                            dve.wait_ge(da_oT_psum, h)
                        for t in range(2):
                            dve.scalar_tensor_tensor(head_out[:, t, 0:P], bank[7][:, t * P:t * P + P],
                                                     head_rstd[:, t:t + 1], subln[:, :], ALU.mult, ALU.mult)\
                                .then_inc(da_normed_o, 1)
                        dve.wait_ge(da_oT_hi, h + 1)
                        dve.tensor_tensor(xT_lo[:, h, :], bank[6][:, 0:T], xT_hi[:, h, :].bitcast(F32),
                                          ALU.subtract).then_inc(da_oT_lo, 1)
                    if i >= 4 and i % 2 == 0:
                        split(n1 + (i - 4) // 2 + 2)

            def rt():
                n0, n1 = first["rt_in"], first["rt_out"]

                def gated(h):
                    dve.wait_ge(rt_orstd, h + 1)
                    dve.wait_ge(rt_gate, 2 * h + 2)
                    for t in range(2):
                        gate = rt_g[:, t, h * 512:h * 512 + 512]
                        dve.scalar_tensor_tensor(gate, bank[4 + t][:, :], head_rstd[:, t:t + 1], gate, ALU.mult, ALU.mult)\
                            .then_inc(rt_y, 1)

                def turned_y(h):
                    for t in range(2):
                        dve.wait_ge(rt_yT_hi, 2 * h + t + 1)
                        at = (slice(None), slice(h % 2 * 4, h % 2 * 4 + 4), slice(t * P, t * P + P))
                        dve.tensor_tensor(xT_lo[at], by_four(bank[6 + t][:, :]), xT_hi[at].bitcast(F32), ALU.subtract)\
                            .then_inc(rt_yT_lo, 1)

                norm(4, 0.5)
                for m in range(12):
                    split(n0 + 2 * m + 2)
                    if m in (6, 7):
                        for c in range(2 * (m - 6), 2 * (m - 6) + 2):
                            dve.wait_ge(rt_turned, 2 * c + 2)
                            dve.tensor_copy(kT[:, 2 * c:2 * c + 2, :].rearrange("p h n -> p (h n)"), bank[7][:, :])\
                                .then_inc(rt_kT, 1)
                    if m >= 8:
                        h = m - 8
                        dve.wait_ge(rt_scores, h + 1)
                        dve.wait_ge(rt_small, 32)
                        if h >= 2:
                            dve.wait_ge(rt_o, h - 1)
                        for cols, decay in ((slice(0, T), bias[:, h, :]), (slice(T, 384), bias[:, h, 0:P])):
                            dve.scalar_tensor_tensor(rt_att[:, h % 2, cols], bank[6][:, cols], RT_DK ** -0.5, decay,
                                                     ALU.mult, ALU.mult).then_inc(rt_decayed, 1)
                        if h:
                            gated(h - 1)
                    split(n0 + 2 * m + 3)
                turned_y(0)
                gated(3)
                turned_y(1)
                for h in range(RT_H):
                    split(n1 + 2 * h + 2)
                    split(n1 + 2 * h + 3)
                    if h < 2:
                        turned_y(h + 2)

            def mix():
                n0, n1 = first["mix_in"], first["mix_out"]
                norm(6, 0.5)
                dve.wait_ge(mx_tail_hi, 1)
                dve.tensor_tensor(tail_lo[:, :, :], tail_w[:, :, :], tail_hi[:, :, :].bitcast(F32), ALU.subtract)\
                    .then_inc(mx_tail_lo, 1)
                for m in range(7):
                    split(n0 + 2 * m + 2)
                    split(n0 + 2 * m + 3)
                dve.memset(conv_in[:, :, 0:3], 0.0).then_inc(mx_zero, 1)
                by_t = lambda ap: ap.rearrange("p (t h) -> p t h", t=2)
                each_t = lambda ap: ap.unsqueeze(1).to_broadcast([P, 2, DN_H])
                dve.wait_ge(mx_ab, 2)
                link(dve.tensor_tensor(by_t(zz), tail_ab[:, :, 0:4], each_t(dt_bias[:, :]), ALU.add))
                dve.scalar_tensor_tensor(uu, zz, -1.0, zz, ALU.mult, ALU.max).then_inc(mx_abs, 1)
                dve.wait_ge(mx_exp, 3)
                dve.tensor_scalar(uu, ez, 1.0, None, ALU.add).then_inc(mx_onep, 1)
                link(dve.tensor_scalar(beta, dd, 1.0, None, ALU.add))
                dve.reciprocal(beta, beta).then_inc(mx_beta, 1)
                dve.wait_ge(mx_beta, 1)
                link(dve.scalar_tensor_tensor(dd, uu, -1.0, ez, ALU.add, ALU.subtract))
                link(dve.reciprocal(ez, uu))
                link(dve.tensor_tensor(dd, dd, ez, ALU.mult))
                dve.wait_ge(mx_ln, 1)
                link(dve.tensor_tensor(dd, ln, dd, ALU.subtract))
                link(dve.scalar_tensor_tensor(dd, zz, 0.0, dd, ALU.max, ALU.add))
                dve.scalar_tensor_tensor(by_t(gg), by_t(dd), -1.0, each_t(ea[:, :]), ALU.mult, ALU.mult).then_inc(mx_g, 1)
                for c in range(1, 6, 2):
                    dve.wait_ge(mx_conv_psum, c + 1)
                    dve.tensor_copy(conv_in[:, 2 * c:2 * c + 2, 3:3 + T],
                                    bank[c][:, :].rearrange("p (k n) -> p k n", k=2)).then_inc(mx_conv_in, 1)
                dve.wait_ge(mx_cum, 1)
                dve.tensor_copy(dec, bank[6][:, 16:24]).then_inc(mx_dec, 1)
                dve.wait_ge(mx_dec, 1)
                dve.wait_ge(mx_last, 1)
                dve.tensor_tensor(etail, bank[6][:, 24:32], dec, ALU.subtract).then_inc(mx_last_diff, 1)
                dve.wait_ge(mx_rows, 1)
                for u in range(8):
                    dve.tensor_scalar(dn_LT[:, u, :], bank[u // 4][:, u % 4 * P:u % 4 * P + P], dec[:, u:u + 1], 0.0,
                                      ALU.subtract, ALU.min).then_inc(mx_diff, 1)
                dve.wait_ge(mx_convw, 1)
                dve.wait_ge(mx_conv_in, 6)
                for c in range(12):
                    dst = conv_out[c // 4][:, c % 4, :]
                    last = dve.tensor_scalar(dst, conv_in[:, c, 0:T], conv_w[:, c:c + 1], None, ALU.mult)
                    for j in range(1, CONV_K):
                        link(last)
                        last = dve.scalar_tensor_tensor(dst, conv_in[:, c, j:j + T], conv_w[:, 12 * j + c:12 * j + c + 1],
                                                        dst, ALU.mult, ALU.add)
                    last.then_inc(mx_conv, 1)
                dve.wait_ge(mx_etail, 2)
                link(dve.tensor_tensor(bed, beta, edec, ALU.mult))
                dve.wait_ge(mx_exprow, 3)
                link(dve.tensor_tensor(dn_LT, dn_LT, sum_mask, ALU.mult))
                dve.wait_ge(mx_rows, 2)
                for b in range(2):
                    dve.tensor_tensor(flat(quarter(dn_AT, b)), flat(quarter(dn_LT, b)), bank[2 + b][:, :], ALU.mult)\
                        .then_inc(mx_masked, 1)
                for t in range(2):
                    dve.wait_ge(mx_tok_psum, 4 + t + 1)
                    dve.tensor_tensor(quarter(dn_vbeta, t), by_four(bank[4 + t][:, :]), wide(beta[:, 4 * t:4 * t + 4]), ALU.mult)\
                        .then_inc(mx_vbeta, 1)
                for s in range(2):
                    dve.wait_ge(mx_dnsq, s + 1)
                    dve.tensor_reduce(dn_ss[:, s, :], sq8, AX_X, ALU.add).then_inc(mx_dnss, 1)
                for s in range(2):
                    dve.wait_ge(mx_dnr, s + 1)
                    dve.wait_ge(mx_tok, 4)
                    dve.tensor_tensor(dn_tok[s], dn_tok[s], wide(dn_rstd[:, s, :]), ALU.mult).then_inc(mx_dnn, 1)
                dve.wait_ge(mx_masked, 2)
                for b in range(2):
                    dve.wait_ge(mx_gram, 1)
                    dve.tensor_tensor(flat(quarter(dn_AT, b)), flat(quarter(dn_AT, b)), bank[4 + b][:, :], ALU.mult)\
                        .then_inc(mx_A, 1)
                dve.wait_ge(mx_gram, 2)
                for b in range(2):
                    dve.tensor_tensor(flat(quarter(dn_attT, b)), flat(quarter(dn_LT, b)), bank[6 + b][:, :], ALU.mult)\
                        .then_inc(mx_attT, 1)
                dve.wait_ge(mx_A, 2)
                dve.tensor_tensor(dn_X, dn_AT, level[0], ALU.mult).then_inc(mx_N0, 1)
                dve.wait_ge(mx_N0, 1)
                for b in range(2):
                    last = dve.tensor_tensor(quarter(dn_XT, b), two_idents, quarter(dn_X, b), ALU.subtract)
                link(last)
                dve.wait_ge(mx_N0T, 1)
                for b in range(2):
                    dve.tensor_tensor(quarter(dn_X, b), two_idents, by_four(bank[b][:, :]), ALU.subtract).then_inc(mx_inv0, 1)
                dve.wait_ge(mx_attT, 2)
                for n in range(1, LEVELS):
                    for b in range(2):
                        if n > 1:
                            dve.wait_ge(mx_Y, 2 * (n - 2) + b + 1)
                        dve.tensor_tensor(quarter(dn_MT, b), quarter(dn_AT, b), level[n][:, 4 * b:4 * b + 4, :], ALU.mult)\
                            .then_inc(mx_MT, 1)
                    for b in range(2):
                        dve.wait_ge(mx_Z, 2 * (n - 1) + b + 1)
                        if n > 1:
                            dve.wait_ge(mx_inv, 4 * (n - 2) + 2 * b + 2)
                        for dst, src in ((dn_X, bank[2 + b]), (dn_XT, bank[4 + b])):
                            dve.tensor_tensor(flat(quarter(dst, b)), flat(quarter(dst, b)), src[:, :], ALU.subtract)\
                                .then_inc(mx_inv, 1)
                dve.wait_ge(mx_val, 1)
                dve.wait_ge(mx_inv, 4 * (LEVELS - 1))
                for b in range(2):
                    dve.tensor_copy(flat(quarter(dn_kcT, b)), bank[2 + b][:, :]).then_inc(mx_valsb, 1)
                for n in range(4):
                    t, r = n // 2, slice(n % 2 * CHUNK, n % 2 * CHUNK + CHUNK)
                    val = flat(quarter(dn_val, t))[r, :]
                    if n == 0:
                        dve.wait_ge(mx_valsb, 4)
                        dve.tensor_copy(dn_vnew[r, :], val).then_inc(mx_vnew, 1)
                    else:
                        dve.wait_ge(mx_KS, n)
                        if n >= 2:
                            dve.wait_ge(mx_SU, n - 1)
                        dve.tensor_tensor(dn_vnew[r, :], val, bank[0][r, :], ALU.subtract).then_inc(mx_vnew, 1)
                    if n == 0:
                        dve.wait_ge(mx_SU, 1)
                        dve.tensor_copy(dn_state, bank[2][:, :]).then_inc(mx_state, 1)
                    elif n < 3:
                        dve.wait_ge(mx_SU, n + 1)
                        for h in range(4):
                            at = slice(h * P, h * P + P)
                            dve.wait_ge(mx_state, 4 * (n - 1) + 1)
                            decay = dn_exprow[:, 4 * t + h, r.stop - 1:r.stop]
                            dve.scalar_tensor_tensor(dn_state[:, at], dn_state[:, at], decay, bank[2][:, at],
                                                     ALU.mult, ALU.add).then_inc(mx_state, 1)
                for t in range(2):
                    dve.wait_ge(mx_osq, t + 1)
                    dve.tensor_reduce(dn_ss[:, 0, 4 * t:4 * t + 4], by_four(square[:, t * 512:t * 512 + 512]), AX_X,
                                      ALU.add).then_inc(mx_oss, 1)
                dve.wait_ge(mx_or, 1)
                dve.wait_ge(mx_gate_gain, 2)
                for t in range(2):
                    dve.tensor_tensor(by_four(dn_y[:, t, :]), by_four(bank[4 + t][:, :]), wide(dn_rstd[:, 0, 4 * t:4 * t + 4]),
                                      ALU.mult).then_inc(mx_y, 1)
                    dve.wait_ge(mx_y, 2 * t + 1)
                    dve.tensor_tensor(dn_y[:, t, :], dn_y[:, t, :], mx_gate[:, t, :], ALU.mult).then_inc(mx_y, 1)
                for s in range(2):
                    for t in range(2):
                        u = 2 * s + t
                        dve.wait_ge(mx_asq, u + 1)
                        dve.tensor_reduce(att_ss[:, 8 * u:8 * u + 8],
                                          square[:, t * 512:t * 512 + 512].rearrange("p (g d) -> p g d", d=AT_DH),
                                          AX_X, ALU.add).then_inc(mx_ass, 1)
                for s in range(2):
                    dve.wait_ge(mx_ars, s + 1)
                    for t in range(2):
                        u = 2 * s + t
                        qk = mx_att[:, s, t, :].rearrange("p (g d) -> p g d", d=AT_DH)
                        dve.tensor_tensor(qk, qk, att_rs[:, 8 * u:8 * u + 8].unsqueeze(2).to_broadcast([P, 8, AT_DH]),
                                          ALU.mult).then_inc(mx_an, 1)
                for c in range(2):
                    dve.wait_ge(mx_aT_psum, 2 * c + 2)
                    dve.tensor_scalar(flat(kT[:, 2 * c:2 * c + 2, :]), bank[2 * c + 1][:, :], att_gain[:, 1:2], None,
                                      ALU.mult).then_inc(mx_ak, 1)
                for i in range(AT_H):
                    dve.wait_ge(mx_S, i + 1)
                    for b in range(2):
                        cols = slice(0, P) if b == 0 else slice(P, 384)
                        dve.tensor_reduce(att_max[:, i, b:b + 1], bank[i % 2][:, cols], AX_X, ALU.max, negate=True)\
                            .then_inc(mx_max, 1)
                dve.wait_ge(mx_P, 2 * AT_H)
                link(dve.reciprocal(flat(att_recip), flat(att_sum)))
                dve.wait_ge(mx_AV, AT_H)
                for t in range(2):
                    dve.tensor_tensor(att_y[:, t, :].rearrange("p (g d) -> p g d", d=AT_DH),
                                      bank[4 + t][:, :].rearrange("p (g d) -> p g d", d=AT_DH),
                                      att_recip[:, t, :].unsqueeze(2).to_broadcast([P, 8, AT_DH]), ALU.mult)\
                        .then_inc(mx_ao, 1)
                dve.wait_ge(mx_aor, 1)
                dve.wait_ge(mx_ao, 2)
                for t in range(2):
                    dve.scalar_tensor_tensor(att_y[:, t, :], att_y[:, t, :], head_rstd[:, t:t + 1], out_gain[:, :],
                                             ALU.mult, ALU.mult).then_inc(mx_ay, 1)
                for p in range(2):
                    for t in range(2):
                        dve.wait_ge(mx_yT_hi, 2 * p + t + 1)
                        k0 = 4 - 4 * p
                        at = (slice(None), slice(k0, k0 + 4), slice(t * P, t * P + P))
                        dve.tensor_tensor(xT_lo[at], by_four(bank[6 + t][:, :]), xT_hi[at].bitcast(F32), ALU.subtract)\
                            .then_inc(mx_yT_lo, 1)
                for r in range(4):
                    split(n1 + r + 2)
            dve.sem_inc(lo_ready, RING)
            split(0)
            split(1)
            norm(0)
            ffn(0, first["ffn0"])
            if "da_in" in live:
                da()
            if "ffn1" in live:
                norm(2, 1.0)
                ffn(1, first["ffn1"])
            if "ffn2" in live:
                norm(3, 0.5)
                ffn(2, first["ffn2"])
            if "rt_in" in live:
                rt()
            if "ffn3" in live:
                norm(5, 1.0)
                ffn(3, first["ffn3"])
            if "mix_in" in live:
                mix()
            if "ff2" in live:
                norm(7, 1.0)
                ff2(first["ff2"])
            for q in range(4):
                residual(len(last_out) - 1, q, 1.0 if stop in ("da_out", "rt_out", "mix_out", 99) else 0.5)

        @block.tensor
        def _(pe):
            def split_product(dst, lT_hi, lT_lo, r_hi, r_lo, start, stop):
                pe.matmul(dst, lT_hi, r_hi, start=start, stop=False)
                pe.matmul(dst, lT_hi, r_lo, start=False, stop=False)
                return pe.matmul(dst, lT_lo, r_hi, start=False, stop=stop)

            def wait_block(n, turns):
                pe.wait_ge(lo_ready, n + 1 + RING + RING * turns)

            def in_block(n, j, banks, turns=0, norm=None, done=None):
                wait_block(n, turns)
                hi, lo = by_four(w_hi[:, n % RING, :]), by_four(w_lo[:, n % RING, :])
                for t in range(2):
                    if norm is not None:
                        pe.wait_ge(xt_lo_ready, 4 * norm + 2 * j + t + 1)
                    tok = slice(t * P, t * P + P)
                    for k in range(4):
                        mm = split_product(bank[banks + t][:, :], xT_hi[:, 4 * j + k, tok], xT_lo[:, 4 * j + k, tok],
                                           hi[:, k, :], lo[:, k, :], j == 0 and k == 0, j == 1 and k == 3)
                    if j == 1 and t == 0:
                        mm.then_inc(done, 1)
                mm.then_inc(wt_used, 1)

            def out_block(n, lhs, k0, start, stop, turns=0):
                wait_block(n, turns)
                hi = w_hi[:, n % RING, :].rearrange("p (k n) -> p k n", k=2)
                lo = w_lo[:, n % RING, :].rearrange("p (k n) -> p k n", k=2)
                for q in range(4):
                    tok = slice(q % 2 * P, q % 2 * P + P)
                    cols = slice(q // 2 * 512, q // 2 * 512 + 512)
                    for k in range(2):
                        mm = split_product(bank[q][:, :], lhs[0][:, k0 + k, tok], lhs[1][:, k0 + k, tok],
                                           hi[:, k, cols], lo[:, k, cols], start and k == 0, stop and k == 1)
                    if stop and q < 3:
                        mm.then_inc(acc_done, 1)
                mm.then_inc(wt_used, 1)

            def norm(g):
                for q in range(4):
                    pe.wait_ge(xg_ready, 4 * g + q + 1)
                    for k in range(4):
                        at = (q // 2) * 512 + k * P
                        tr = pe.transpose(bank[4 + q][:, k * P:k * P + P], xg[:, q % 2, at:at + P], ident)
                    tr.then_inc(xt_psum, 1)

            def ffn(f, n0):
                g = NORM_OF[f"ffn{f}"]
                cb = FFC * f

                def turn_hidden(c, i=0):
                    pe.wait_ge(hid_ready, 2 * (cb + c + 1) + 2 * i)
                    for t in range(2):
                        for k in range(2):
                            tr = pe.transpose(bank[6][:, k * T + t * P:k * T + t * P + P],
                                              hid[:, t, k * P:k * P + P], ident)
                    tr.then_inc(ht_psum, 1)

                in_block(n0, 0, 4, norm=g)
                in_block(n0 + 1, 1, 4, norm=g, done=in_done)
                turn_hidden(0)

                def chunk(c, i, start):
                    in_block(n0 + 2, 0, 4, turns=i)
                    in_block(n0 + 3, 1, 4, turns=i, done=in_done)
                    pe.wait_ge(ht_lo_ready, cb + c + i)
                    out_block(n0 + 4, (hT_hi, hT_lo), 0, start, False, turns=i)
                    turn_hidden(c, i)

                chunk(1, 0, True)
                with pe.Fori(1, FFC - 1) as i:
                    chunk(1, i, False)
                pe.wait_ge(ht_lo_ready, cb + FFC)
                out_block(n0 + FFN_BLOCKS - 1, (hT_hi, hT_lo), 0, False, True)

            def ff2(n0):
                def turn_hidden(c, i=0):
                    pe.wait_ge(sq_ready, 2 * c + 2 + 2 * i)
                    for b in range(2):
                        for k in range(2):
                            for t in range(2):
                                at = (2 * b + k) * P
                                tr = pe.transpose(bank[6 + b][:, k * T + t * P:k * T + t * P + P],
                                                  hid[:, t, at:at + P], ident)
                        tr.then_inc(ht2_psum, 1)

                def out(c, n, start, stop, i=0, turns=0):
                    for b in range(2):
                        pe.wait_ge(ht2_lo_ready, 2 * c + b + 1 + 2 * i)
                        out_block(n + b, (hT_hi, hT_lo), 2 * b, start and b == 0, stop and b == 1, turns)

                def chunk(c, n, start=False, i=0, turns=0):
                    in_block(n, 0, 4, turns)
                    in_block(n + 1, 1, 4, turns, done=in2_done)
                    out(c - 1, n + 2, start, False, i, turns)
                    turn_hidden(c, i)

                in_block(n0, 0, 4, norm=7)
                in_block(n0 + 1, 1, 4, norm=7, done=in2_done)
                turn_hidden(0)
                for u in range(3):
                    chunk(1 + u, n0 + 2 + 4 * u, u == 0)
                with pe.Fori(1, 2) as i:
                    for u in range(3):
                        chunk(1 + u, n0 + 2 + 4 * u, False, 3 * i, 4 * i)
                chunk(FF2C - 1, n0 + 4 * FF2C - 6)
                out(FF2C - 1, n0 + 4 * FF2C - 2, False, True)

            def project(n0, m0, g, chunks):
                def chunk(u, turns=0, norm=None):
                    pe.wait_ge(proj_read, 2 * (m0 + u + 1) + 3 * turns)
                    in_block(n0 + 2 * u, 0, u % 3 * 2, turns=turns, norm=norm)
                    in_block(n0 + 2 * u + 1, 1, u % 3 * 2, turns=turns, norm=norm, done=proj_done)

                chunk(0, norm=g)
                chunk(1)
                chunk(2)
                if chunks // 3 > 1:
                    with pe.Fori(1, chunks // 3) as i:
                        for u in range(3):
                            chunk(u, turns=2 * i)
                for u in range(chunks // 3 * 3, chunks):
                    chunk(u)

            def da():
                norm(1)
                project(first["da_in"], 0, 1, 6)
                pe.wait_ge(proj_read, 6 + 12)
                pe.wait_ge(da_normed, 4)
                for c in range(4):
                    for s in range(2):
                        for h in range(2):
                            for t in range(2):
                                at = s * D + (2 * c + h) * P
                                tr = pe.transpose(bank[2 * c + s][:, h * T + t * P:h * T + t * P + P],
                                                  da_proj[:, t, at:at + P], ident)
                        tr.then_inc(da_turned, 1)
                pe.wait_ge(bias_full, 16)
                for i in range(DA_H + 3):
                    if i < DA_H:
                        if i == 0:
                            pe.wait_ge(da_qT, 4)
                            pe.wait_ge(da_kT, 4)
                        else:
                            pe.wait_ge(da_exp, 4 * i)
                        for m in range(2):
                            rows = slice(m * DA_DH, (m + 1) * DA_DH)
                            S = bank[4 + m]
                            pe.matmul(S[:, 0:P], qT[rows, i, 0:P], kT[rows, i, 0:P], start=True, stop=False)
                            pe.matmul(S[:, 0:P], bias[:, i, 0:P], ident, start=False, stop=True)
                            pe.matmul(S[:, P:384], qT[rows, i, P:T], kT[rows, i, :], start=True, stop=False)
                            pe.matmul(S[:, P:T], bias[:, i, P:T], ident, start=False, stop=False)
                            pe.matmul(S[:, T:384], bias[:, i, 0:P], ident, start=False, stop=True)\
                                .then_inc(da_scores, 1)
                    if 1 <= i <= DA_H:
                        h = i - 1
                        pe.wait_ge(da_mixed, 2 * h + 2)
                        if h:
                            pe.wait_ge(da_mixT, h)
                        for b in range(3):
                            tr = pe.transpose(bank[6][:, b * P:b * P + P], mixed[:, h % 2, b * P:b * P + P], ident)
                        tr.then_inc(da_mixT_psum, 1)
                    if i >= 4 and i % 2 == 0:
                        r = (i - 4) // 2
                        pe.wait_ge(da_oT_lo, 2 * r + 2)
                        out_block(first["da_out"] + r, (xT_hi, xT_lo), 2 * r, r == 0, r == 3)
                    if 1 <= i <= DA_H:
                        h = i - 1
                        v = da_proj[:, :, 2 * D + h * P:2 * D + h * P + P]
                        pe.wait_ge(da_mixT, h + 1)
                        if h:
                            pe.wait_ge(da_normed_o, 2 * h)
                        pe.matmul(bank[7][:, 0:P], mixT[:, 0:P], v[:, 0, :], start=True, stop=True)
                        pe.matmul(bank[7][:, P:T], mixT[:, P:T], v[:, 0, :], start=True, stop=False)
                        pe.matmul(bank[7][:, P:T], mixT[:, T:384], v[:, 1, :], start=False, stop=True)\
                            .then_inc(da_o, 1)
                    if 2 <= i <= DA_H + 1:
                        h = i - 2
                        pe.wait_ge(da_normed_o, 2 * h + 2)
                        if h:
                            pe.wait_ge(da_oT_lo, h)
                        for t in range(2):
                            tr = pe.transpose(bank[6][:, t * P:t * P + P], head_out[:, t, 0:P], ident)
                        tr.then_inc(da_oT_psum, 1)

            def rt():
                n0, n1 = first["rt_in"], first["rt_out"]
                norm(4)
                project(n0, 6, 4, 6)
                for m in range(6, 12):
                    h = m - 8
                    pe.wait_ge(proj_read, 6 + 2 * (6 + (m - 1 if m >= 8 else 3 + m - 5)))
                    for j in range(2):
                        in_block(n0 + 2 * m + j, j, 2 * rt_pair[m], done=proj_done)
                        if h < 0:
                            c = 2 * (m - 6) + j
                            for s, src in enumerate((rt_q, rt_k)):
                                if c:
                                    pe.wait_ge((rt_qT, rt_kT)[s], c)
                                for k in range(2):
                                    for t in range(2):
                                        at = (2 * c + k) * P
                                        tr = pe.transpose(bank[6 + s][:, k * T + t * P:k * T + t * P + P],
                                                          src[:, t, at:at + P], ident)
                                tr.then_inc(rt_turned, 1)
                        elif j == 0:
                            if h == 0:
                                pe.wait_ge(rt_qT, 4)
                                pe.wait_ge(rt_kT, 4)
                            else:
                                pe.wait_ge(rt_decayed, 2 * h)
                            for cols, keys, queries in ((slice(0, T), slice(0, P), slice(0, T)),
                                                        (slice(T, 384), slice(P, T), slice(P, T))):
                                for k in range(2):
                                    mm = pe.matmul(bank[6][:, cols], kT[:, 2 * h + k, keys], qT[:, 2 * h + k, queries],
                                                   start=k == 0, stop=k == 1)
                            mm.then_inc(rt_scores, 1)
                        else:
                            pe.wait_ge(rt_decayed, 2 * h + 2)
                            if h:
                                pe.wait_ge(rt_y, 2 * h)
                            v = rt_v[:, :, h * 512:h * 512 + 512]
                            att = rt_att[:, h % 2, :]
                            pe.matmul(bank[4][:, :], att[:, 0:P], v[:, 0, :], start=True, stop=True)
                            pe.matmul(bank[5][:, :], att[:, P:T], v[:, 0, :], start=True, stop=False)
                            pe.matmul(bank[5][:, :], att[:, T:384], v[:, 1, :], start=False, stop=True).then_inc(rt_o, 1)

                def turn_y(h):
                    pe.wait_ge(rt_y, 2 * h + 2)
                    if h:
                        pe.wait_ge(rt_yT_lo, 2 * h)
                    for t in range(2):
                        for k in range(4):
                            at = h * 512 + k * P
                            tr = pe.transpose(bank[6 + t][:, k * P:k * P + P], rt_g[:, t, at:at + P], ident)
                        tr.then_inc(rt_yT_psum, 1)

                turn_y(0)
                turn_y(1)
                pe.wait_ge(proj_read, 6 + 2 * 18)
                for h in range(RT_H):
                    pe.wait_ge(rt_yT_lo, 2 * h + 2)
                    for r in range(2):
                        out_block(n1 + 2 * h + r, (xT_hi, xT_lo), h % 2 * 4 + 2 * r, h == 0 and r == 0, h == 3 and r == 1)
                    if h < 2:
                        turn_y(h + 2)

            def mix():
                n0, n1 = first["mix_in"], first["mix_out"]
                norm(6)
                project(n0, 18, 6, 7)
                pe.wait_ge(mx_tail_lo, 1)
                for t in range(2):
                    tok = slice(t * P, t * P + P)
                    for k in range(KD):
                        mm = split_product(bank[6][:, t * 8:t * 8 + 8], xT_hi[:, k, tok], xT_lo[:, k, tok],
                                           tail_hi[:, k, :], tail_lo[:, k, :], k == 0, k == KD - 1)
                mm.then_inc(mx_tail, 1)
                pe.wait_ge(mx_small, MX_SMALL)
                pe.transpose(bank[7][:, 0:48], conv_row, ident[0:48, 0:48]).then_inc(mx_convw_psum, 1)
                pe.wait_ge(proj_read, 6 + 2 * 25)
                for c in range(6):
                    for k in range(2):
                        for t in range(2):
                            at = (c % 2 * 2 + k) * P
                            tr = pe.transpose(bank[c][:, k * T + t * P:k * T + t * P + P],
                                              mx_dn[:, c // 2, t, at:at + P], ident)
                    tr.then_inc(mx_conv_psum, 1)
                pe.wait_ge(mx_g, 1)
                pe.matmul(bank[6][:, 16:24], cum, gg, start=True, stop=True).then_inc(mx_cum, 1)
                pe.wait_ge(mx_dec, 1)
                pe.matmul(bank[6][:, 24:32], last_row, dec, start=True, stop=True).then_inc(mx_last, 1)
                pe.wait_ge(mx_conv_in, 6)
                for b, src in ((0, dec), (2, beta)):
                    for u in range(8):
                        mm = pe.matmul(bank[b + u // 4][:, u % 4 * P:u % 4 * P + P],
                                       src[:, u:u + 1].to_broadcast([P, P]), ident, start=True, stop=True)
                    mm.then_inc(mx_rows, 1)
                pe.wait_ge(mx_etail, 1)
                pe.wait_ge(mx_convw, 1)
                for s in range(3):
                    pe.wait_ge(mx_silu, s + 1)
                    if s == 2:
                        pe.wait_ge(mx_tok, 2)
                    for t in range(2):
                        for h in range(4):
                            tr = pe.transpose(bank[4 + s % 2 * 2 + t][:, h * P:h * P + P],
                                              conv_out[s][:, h, t * P:t * P + P], ident)
                        tr.then_inc(mx_tok_psum, 1)
                pe.wait_ge(mx_tok, 4)
                pe.wait_ge(mx_vbeta, 2)
                for s in range(2):
                    pe.wait_ge(mx_dnn, s + 1)
                    for t in range(2):
                        for h in range(4):
                            tr = pe.transpose(bank[4 + s * 2 + t][:, h * P:h * P + P], dn_tok[s][:, 4 * t + h, :], ident)
                        tr.then_inc(mx_back_psum, 1)
                pe.wait_ge(mx_back, 4)
                pe.wait_ge(mx_masked, 2)
                for b, rhs in ((4, dn_khT), (6, dn_qhT)):
                    for u in range(8):
                        tok = slice(u // 4 * P, u // 4 * P + P)
                        mm = pe.matmul(bank[b + u // 4][:, u % 4 * P:u % 4 * P + P], dn_khT[:, u % 4, tok],
                                       rhs[:, u % 4, tok], start=True, stop=True)
                    mm.then_inc(mx_gram, 1)
                pe.wait_ge(mx_N0, 1)
                for u in range(8):
                    tr = pe.transpose(bank[u // 4][:, u % 4 * P:u % 4 * P + P], dn_X[:, u, :], ident)
                tr.then_inc(mx_N0T, 1)
                pe.wait_ge(mx_inv0, 2)
                for n in range(1, LEVELS):
                    for b in range(2):
                        pe.wait_ge(mx_MT, 2 * (n - 1) + b + 1)
                        if n > 1:
                            pe.wait_ge(mx_inv, 4 * (n - 2) + 2 * b + 2)
                        for u in range(4 * b, 4 * b + 4):
                            mm = pe.matmul(bank[b][:, u % 4 * P:u % 4 * P + P], dn_MT[:, u, :], dn_X[:, u, :],
                                           start=True, stop=True)
                        mm.then_inc(mx_Y, 1)
                    for b in range(2):
                        pe.wait_ge(mx_Ysb, 2 * (n - 1) + b + 1)
                        for u in range(4 * b, 4 * b + 4):
                            at = slice(u % 4 * P, u % 4 * P + P)
                            pe.matmul(bank[2 + b][:, at], dn_XT[:, u, :], dn_Y[:, u, :], start=True, stop=True)
                            mm = pe.matmul(bank[4 + b][:, at], dn_Y[:, u, :], dn_XT[:, u, :], start=True, stop=True)
                        mm.then_inc(mx_Z, 1)
                pe.wait_ge(mx_inv, 4 * (LEVELS - 1))
                pe.wait_ge(mx_ktail, 2)
                for u in range(8):
                    at = slice(u % 4 * P, u % 4 * P + P)
                    pe.matmul(bank[u // 4][:, at], dn_XT[:, u, :], dn_vbeta[:, u, :], start=True, stop=True)
                    mm = pe.matmul(bank[2 + u // 4][:, at], dn_kbe[:, u, :], dn_XT[:, u, :], start=True, stop=True)
                mm.then_inc(mx_val, 1)
                for n in range(4):
                    t, r = n // 2, slice(n % 2 * CHUNK, n % 2 * CHUNK + CHUNK)
                    if n:
                        pe.wait_ge(mx_state, 4 * (n - 1) + 1)
                        for h in range(4):
                            mm = pe.matmul(bank[0][r, h * P:h * P + P], dn_kcT[:, 4 * t + h, r],
                                           dn_state[:, h * P:h * P + P], start=True, stop=True)
                        mm.then_inc(mx_KS, 1)
                    else:
                        pe.wait_ge(mx_valsb, 4)
                        pe.wait_ge(mx_qd, 1)
                    pe.wait_ge(mx_vnew, n + 1)
                    for h in range(4):
                        at = slice(h * P, h * P + P)
                        tok = slice(t * P + n % 2 * CHUNK, t * P + n % 2 * CHUNK + CHUNK)
                        if n:
                            pe.matmul(bank[4 + t][r, at], dn_qhT[:, h, tok], dn_state[:, at], start=True, stop=False)
                        mm = pe.matmul(bank[4 + t][r, at], dn_attT[r, 4 * t + h, r], dn_vnew[r, at],
                                       start=not n, stop=True)
                    mm.then_inc(mx_O, 1)
                    if n < 3:
                        for h in range(4):
                            mm = pe.matmul(bank[2][:, h * P:h * P + P], dn_ktail[r, 4 * t + h, :],
                                           dn_vnew[r, h * P:h * P + P], start=True, stop=True)
                        mm.then_inc(mx_SU, 1)

                pe.wait_ge(mx_an, 4)
                pe.wait_ge(mx_vnew, 3)
                pe.wait_ge(mx_state, 9)
                for c in range(2):
                    for s in range(2):
                        for k in range(2):
                            for t in range(2):
                                at = (2 * c + k) * P
                                tr = pe.transpose(bank[2 * c + s][:, k * T + t * P:k * T + t * P + P],
                                                  mx_att[:, s, t, at:at + P], ident)
                        tr.then_inc(mx_aT_psum, 1)
                pe.wait_ge(mx_bias, 17)
                pe.wait_ge(mx_y, 3)
                for i in range(AT_H + 1):
                    if i < AT_H:
                        if i == 0:
                            pe.wait_ge(mx_aq, 2)
                            pe.wait_ge(mx_ak, 2)
                        if i >= 2:
                            pe.wait_ge(mx_P, 2 * (i - 1))
                        rows = slice(i % 2 * AT_DH, (i % 2 + 1) * AT_DH)
                        q, k, S = qT[rows, i // 2, :], kT[rows, i // 2, :], bank[i % 2]
                        pe.matmul(S[:, 0:P], q[:, 0:P], k[:, 0:P], start=True, stop=False)
                        pe.matmul(S[:, 0:P], bias[:, i, 0:P], flip, start=False, stop=True)
                        pe.matmul(S[:, P:384], q[:, P:T], k, start=True, stop=False)
                        pe.matmul(S[:, P:T], bias[:, i, P:T], flip, start=False, stop=False)
                        pe.matmul(S[:, T:384], bias[:, i, 0:P], flip, start=False, stop=True).then_inc(mx_S, 1)
                    if i:
                        h = i - 1
                        pe.wait_ge(mx_P, 2 * h + 2)
                        if h >= 2:
                            pe.wait_ge(mx_PT, h - 1)
                        for b in range(3):
                            tr = pe.transpose(bank[2 + h % 2][:, b * P:b * P + P], prob_a[:, h % 2, b * P:b * P + P], ident)
                        tr.then_inc(mx_PT_psum, 1)
                        pe.wait_ge(mx_PT, h + 1)
                        at = slice(h * AT_DH, h * AT_DH + AT_DH)
                        v = mx_att[:, 2, :, at]
                        pe.matmul(bank[4][:, at], probT[:, 0:P], v[:, 0, :], start=True, stop=True)
                        pe.matmul(bank[5][:, at], probT[:, P:T], v[:, 0, :], start=True, stop=False)
                        pe.matmul(bank[5][:, at], probT[:, T:384], v[:, 1, :], start=False, stop=True).then_inc(mx_AV, 1)

                for p, (src, ready, need) in enumerate(((dn_y, mx_y, 4), (att_y, mx_ay, 2))):
                    pe.wait_ge(ready, need)
                    for t in range(2):
                        for k in range(4):
                            tr = pe.transpose(bank[6 + t][:, k * P:k * P + P], src[:, t, k * P:k * P + P], ident)
                        tr.then_inc(mx_yT_psum, 1)
                    pe.wait_ge(mx_yT_lo, 2 * p + 2)
                for r in range(4):
                    out_block(n1 + r, (xT_hi, xT_lo), 2 * r, r == 0, r == 3)
            pe.sem_inc(wt_used, RING)
            pe.wait_ge(table_full, 16)
            norm(0)
            ffn(0, first["ffn0"])
            if "da_in" in live:
                da()
            if "ffn1" in live:
                norm(2)
                ffn(1, first["ffn1"])
            if "ffn2" in live:
                norm(3)
                ffn(2, first["ffn2"])
            if "rt_in" in live:
                rt()
            if "ffn3" in live:
                norm(5)
                ffn(3, first["ffn3"])
            if "mix_in" in live:
                mix()
            if "ff2" in live:
                norm(7)
                ff2(first["ff2"])


USED = ["x", "ffn1_norm", "ffn1_w_in", "ffn1_w_out", "mix_norm", "ffn2_norm", "ffn2_w_in", "ffn2_w_out",
        "da_w_in", "da_q_gain", "da_k_gain", "da_lambda", "da_subln", "da_w_out", "rt_w_in", "rt_subln",
        "rt_w_out", "mix_norm_gain_2", "w_in_2", "att_q_gain_2", "att_k_gain_2", "rel_bias_2",
        "att_out_gain_2", "dn_conv_w_2", "dn_a_log_2", "dn_dt_bias_2", "dn_out_gain_2", "w_out_2",
        "ffn_norm_gain_2", "w_ff1_2", "w_ff2_2"]


def program(nc, shapes, stop=99):
    A = {}
    for name, (shape, dtype) in shapes.items():
        A[name] = nc.dram_tensor(f"in_{name}", shape, dtype, kind="ExternalInput").ap()
    out = nc.dram_tensor("out", (1, T, D), F32, kind="ExternalOutput").ap()
    first_then_second_block(nc, A, out, stop)


def kernel(**inputs):
    import concourse.bacc as bacc
    from concourse.bass_utils import run_bass_kernel_spmd

    arrays = {name: np.ascontiguousarray(inputs[name]) for name in USED} | constants()
    nc = bacc.Bacc("TRN2", target_bir_lowering=False, num_devices=1)
    program(nc, {k: (v.shape, mybir.dt.from_np(v.dtype)) for k, v in arrays.items()})
    r = run_bass_kernel_spmd(nc, [{f"in_{k}": v for k, v in arrays.items()}], core_ids=[0])
    return r.results[0]["out"]
```

```python
from contextlib import ExitStack

import numpy as np

import concourse.bass as bass
from concourse import mybir

ALU = mybir.AluOpType
ACT = mybir.ActivationFunctionType
AX_X = mybir.AxisListType.X
F32 = mybir.dt.float32
F32R = mybir.dt.float32r

P = 128
T = 256
D = 1024
KD = D // P
EPS = 1e-6
RING = 3
BLOCK = 2048

FF = 2816
FFC = FF // 256
DA_H, DA_DH = 8, 64
LAM_INIT = 0.8 - 0.6 * float(np.exp(-0.3 * 0))
RT_H, RT_DK, RT_DV = 4, 256, 512
AT_H, AT_DH, N_REL, MAX_REL = 8, 64, 513, 256
CHUNK = 64
DN_H, DN_D, CONV_K = 4, 128, 4
FF2 = 4096
FF2C = FF2 // 512
LEVELS = 6
MASKED = -1e30

C_IDENT = 0
C_CUM = C_IDENT + P
C_LAST = C_CUM + P
C_LEVEL = C_LAST + P
C_END = C_LEVEL + LEVELS * P


def constants():
    j = np.arange(P)[:, None]
    i = np.arange(P)[None, :]
    table = np.zeros((P, C_END), np.float32)
    table[:, C_IDENT:C_IDENT + P] = i == j
    table[:, C_CUM:C_CUM + P] = (j <= i) & (j // CHUNK == i // CHUNK)
    table[:, C_LAST:C_LAST + P] = j == (i // CHUNK) * CHUNK + CHUNK - 1
    for n in range(LEVELS):
        half = 1 << n
        table[:, C_LEVEL + n * P:C_LEVEL + (n + 1) * P] = (
            (j // (2 * half) == i // (2 * half)) & (j // half % 2 == 0) & (i // half % 2 == 1))
    dist = np.arange(T)[None, :] - j
    slopes = 2.0 ** (-8.0 * np.arange(1, DA_H + 1) / DA_H)
    alibi = np.where(dist[:, None, :] >= 0, -slopes[None, :, None] * dist[:, None, :], MASKED)
    gamma = 1.0 - 2.0 ** (-5.0 - np.arange(RT_H, dtype=np.float64))
    decay = np.where(dist[:, None, :] >= 0, gamma[None, :, None] ** np.maximum(dist, 0)[:, None, :], 0.0)
    return {
        "c_table": table,
        "c_flip": np.ascontiguousarray(table[:, C_IDENT:C_IDENT + P][:, ::-1]),
        "c_alibi": alibi.astype(np.float32).reshape(P, DA_H * T),
        "c_decay": decay.astype(np.float32).reshape(P, RT_H * T),
    }


def first_then_second_block(nc, A, out):
    ctx = ExitStack()
    with ctx:
        def sb(name, shape, dt=F32):
            return ctx.enter_context(nc.sbuf_tensor(name, shape, dt))

        def sem(name):
            return ctx.enter_context(nc.semaphore(name))

        raw = sb("raw", [P, RING, BLOCK])
        w_hi = sb("w_hi", [P, RING, BLOCK], F32R)
        w_lo = sb("w_lo", [P, RING, BLOCK], F32R)
        x = sb("x", [P, 2, D])
        xg = sb("xg", [P, 2, D])
        xT_hi = sb("xT_hi", [P, KD, T], F32R)
        xT_lo = sb("xT_lo", [P, KD, T], F32R)
        gains = sb("gains", [P, 2, D])
        sumsq = sb("sumsq", [P, 2])
        meansq = sb("meansq", [P, 2])
        rstd = sb("rstd", [P, 2])
        neghalf = sb("neghalf", [P, 64])
        relu = sb("relu", [P, 2, 512])
        silu_a = relu[:, :, 0:256]
        hid = sb("hid", [P, 2, 512])
        square = hid[:, :, :].rearrange("p t n -> p (t n)")
        hT_hi = sb("hT_hi", [P, 4, T], F32R)
        hT_lo = sb("hT_lo", [P, 4, T], F32R)
        ident_r = hT_lo[:, 0, 0:P]
        diag_bias = hT_hi[:, :, :].rearrange("p a (b n) -> p (a b) n", b=2)
        table = sb("table", [P, C_END])
        room = sb("room", [P, 2 * 6144])

        qT = sb("qT", [P, 8, T])
        kT = sb("kT", [P, 8, T])
        bias = sb("bias", [P, 8, T])
        da_gain = sb("da_gain", [P, 2])
        lam_exp = sb("lam_exp", [P, 4])
        lam = sb("lam", [P, 1])
        qk_ss = sb("qk_ss", [P, 4, 16])
        qk_rstd = sb("qk_rstd", [P, 4, 16])
        neg_max = sb("neg_max", [P, 2, 4])
        p_sum = sb("p_sum", [P, 2, 4])
        p_recip = sb("p_recip", [P, 4])
        recip_lam = sb("recip_lam", [P, 2])
        head_ss = sb("head_ss", [P, 2])
        head_rstd = sb("head_rstd", [P, 2])

        def carve(at, *dims):
            size = int(np.prod(dims))
            view = room[:, at:at + size]
            names = " ".join("abcd"[:len(dims)])
            if len(dims) > 1:
                view = view.rearrange(f"p ({names}) -> p {names}", **dict(zip("abcd", dims)))
            return view, at + size

        da_proj, at = carve(0, 2, 3072)
        prob, at = carve(at, 2, 2, 384)
        prob1, at = carve(at, 384)
        mixed, at = carve(at, 2, 384)
        mixT, at = carve(at, 384)
        head_out, at = carve(at, 2, P)
        da_lam, at = carve(at, 4, DA_DH)
        lam_prod, at = carve(at, 2, DA_DH)
        subln, at = carve(at, P)

        rt_q, at = carve(0, 2, D)
        rt_k, at = carve(at, 2, D)
        rt_v, at = carve(at, 2, RT_H * RT_DV)
        rt_g, at = carve(at, 2, RT_H * RT_DV)
        rt_att, _ = carve(0, 2, 384)
        rt_chunk = [part[:, :, m * 512:m * 512 + 512] for part, n in ((rt_q, 2), (rt_k, 2), (rt_v, 4), (rt_g, 4))
                    for m in range(n)]
        mx_pair = [0, 1, 2, 0, 0, 0, 0]
        MX_SMALL = 16 * 11
        rt_pair = [m % 3 for m in range(6)] + [0, 1] * 3

        mx_dn, at = carve(0, 3, 2, 512)
        mx_gate, at = carve(at, 2, 512)
        mx_att, at = carve(at, 3, 2, 512)
        free = at
        conv_in, at = carve(at, 12, CONV_K - 1 + T)
        conv_v, at = carve(at, 4, T)
        conv_out = [qT[:, 4:8, :], kT[:, 4:8, :], conv_v]
        dn_qhT, dn_khT = qT[:, 4:8, :], kT[:, 4:8, :]
        prob_a, _ = carve(at, 2, 384)
        probT = relu[:, 0, 0:384]
        att_square = relu[:, 0, :]
        tail_row = relu[0:8, 1, 256:512]
        flip = relu[:, 1, 0:P]

        def by_pair(ap):
            return ap.rearrange("p (u n) -> p u n", u=8)

        def flat(ap):
            return ap.rearrange("p a b -> p (a b)")

        dn_tok = [by_pair(room[:, s * 1024:s * 1024 + 1024]) for s in range(3)]
        dn_kbe, dn_ktail, dn_vbeta = dn_tok
        dn_AT = by_pair(room[:, free:free + 1024])
        dn_attT = by_pair(room[:, free + 1024:free + 2048])
        dn_X = by_pair(room[:, free + 2048:free + 3072])
        dn_XT = by_pair(flat(conv_v))
        dn_LT = by_pair(xg[:, 0, :])
        dn_MT = dn_LT
        dn_exprow = by_pair(xg[:, 1, :])
        dn_Y = by_pair(flat(dn_khT))
        dn_val = dn_AT
        dn_kcT = dn_X
        dn_state, dn_vnew = [xg[:, 0, 0:512], flat(kT[:, 4:6, :])], xg[:, 0, 512:1024]
        dn_y = room[:, 0:1024].rearrange("p (t n) -> p t n", t=2)
        sq8 = by_pair(square)
        att_y = mx_att[:, 0, :, :]
        out_gain = gains[:, 0, 0:512]
        conv_row = gains[0:CONV_K * 12, 0, 512:640]
        dn_gain = gains[:, 0, 640:768]
        conv_w = sb("conv_w", [P, CONV_K * 12])
        a_log = sb("a_log", [P, DN_H])
        dt_bias = sb("dt_bias", [P, DN_H])
        att_gain = sb("att_gain", [P, 2])
        tail_w = sb("tail_w", [P, KD, 8])
        tail_hi = sb("tail_hi", [P, KD, 8], F32R)
        tail_lo = sb("tail_lo", [P, KD, 8], F32R)
        small = sb("small", [P, 24, 8])
        (ab, zz, ez, uu, ln, dd, gg, beta, dec, etail, edec, bed, dn_ss, dn_rstd, att_ss, att_rs) = (
            [small[:, n, :] for n in range(12)] + [small[:, n:n + 2, :] for n in (12, 14)]
            + [small[:, n:n + 4, :].rearrange("p a b -> p (a b)") for n in (16, 20)])
        tail_ab = sb("tail_ab", [P, 2, 8])
        ea = sb("ea", [P, DN_H])
        att_max = sb("att_max", [P, 8, 2])
        att_sum = sb("att_sum", [P, 2, 8])
        att_recip = sb("att_recip", [P, 2, 8])

        bank = [ctx.enter_context(nc.psum_tensor(f"bank{i}", [P, 512], F32)) for i in range(8)]
        ident = table[:, C_IDENT:C_IDENT + P]

        raw_full = [sem(f"raw_full{s}") for s in range(RING)]
        hi_ready = sem("hi_ready")
        lo_ready = sem("lo_ready")
        wt_used = sem("wt_used")
        x_full = sem("x_full")
        table_full = sem("table_full")
        gain_full = [sem("gain_full0"), sem("gain_full1")]
        acc_done = sem("acc_done")
        resid_done = sem("resid_done")
        xg_ready = sem("xg_ready")
        xt_psum = sem("xt_psum")
        xt_hi_ready = sem("xt_hi_ready")
        xt_lo_ready = sem("xt_lo_ready")
        ss_ready = sem("ss_ready")
        rstd_ready = sem("rstd_ready")
        pool_chain = sem("pool_chain")
        dve_chain = sem("dve_chain")
        in_done = sem("in_done")
        silu_ready = sem("silu_ready")
        hid_ready = sem("hid_ready")
        ht_psum = sem("ht_psum")
        ht_hi_ready = sem("ht_hi_ready")
        ht_lo_ready = sem("ht_lo_ready")
        x_stored = sem("x_stored")
        proj_done = sem("proj_done")
        proj_read = sem("proj_read")
        da_small = sem("da_small")
        da_square = sem("da_square")
        da_sumsq = sem("da_sumsq")
        da_rstd = sem("da_rstd")
        da_normed = sem("da_normed")
        da_turned = sem("da_turned")
        da_qT = sem("da_qT")
        da_kT = sem("da_kT")
        da_lamsum = sem("da_lamsum")
        da_lamexp = sem("da_lamexp")
        bias_full = sem("bias_full")
        da_scores = sem("da_scores")
        da_max = sem("da_max")
        da_exp = sem("da_exp")
        da_mixed = sem("da_mixed")
        da_mixT_psum = sem("da_mixT_psum")
        da_mixT = sem("da_mixT")
        da_o = sem("da_o")
        da_oss = sem("da_oss")
        da_orstd = sem("da_orstd")
        da_normed_o = sem("da_normed_o")
        da_oT_psum = sem("da_oT_psum")
        da_oT_hi = sem("da_oT_hi")
        da_oT_lo = sem("da_oT_lo")
        in2_done = sem("in2_done")
        relu_ready = sem("relu_ready")
        sq_ready = sem("sq_ready")
        ht2_psum = sem("ht2_psum")
        ht2_hi_ready = sem("ht2_hi_ready")
        ht2_lo_ready = sem("ht2_lo_ready")
        mx_small = sem("mx_small")
        mx_bias = sem("mx_bias")
        mx_tail_hi = sem("mx_tail_hi")
        mx_tail_lo = sem("mx_tail_lo")
        mx_tail = sem("mx_tail")
        mx_ab = sem("mx_ab")
        mx_abs = sem("mx_abs")
        mx_exp = sem("mx_exp")
        mx_onep = sem("mx_onep")
        mx_ln = sem("mx_ln")
        mx_beta = sem("mx_beta")
        mx_g = sem("mx_g")
        mx_cum = sem("mx_cum")
        mx_dec = sem("mx_dec")
        mx_last = sem("mx_last")
        mx_last_diff = sem("mx_last_diff")
        mx_etail = sem("mx_etail")
        mx_rows = sem("mx_rows")
        mx_diff = sem("mx_diff")
        mx_exprow = sem("mx_exprow")
        mx_masked = sem("mx_masked")
        mx_convw_psum = sem("mx_convw_psum")
        mx_convw = sem("mx_convw")
        mx_conv_psum = sem("mx_conv_psum")
        mx_conv_in = sem("mx_conv_in")
        mx_zero = sem("mx_zero")
        mx_conv = sem("mx_conv")
        mx_silu = sem("mx_silu")
        mx_tok_psum = sem("mx_tok_psum")
        mx_tok = sem("mx_tok")
        mx_dnsq = sem("mx_dnsq")
        mx_dnss = sem("mx_dnss")
        mx_dnr = sem("mx_dnr")
        mx_dnn = sem("mx_dnn")
        mx_ktail = sem("mx_ktail")
        mx_back_psum = sem("mx_back_psum")
        mx_back = sem("mx_back")
        mx_gram = sem("mx_gram")
        mx_attT = sem("mx_attT")
        mx_N0 = sem("mx_N0")
        mx_N0T = sem("mx_N0T")
        mx_inv0 = sem("mx_inv0")
        mx_MT = sem("mx_MT")
        mx_Y = sem("mx_Y")
        mx_Ysb = sem("mx_Ysb")
        mx_Z = sem("mx_Z")
        mx_inv = sem("mx_inv")
        mx_val = sem("mx_val")
        mx_valsb = sem("mx_valsb")
        mx_qd = sem("mx_qd")
        mx_KS = sem("mx_KS")
        mx_vnew = sem("mx_vnew")
        mx_O = sem("mx_O")
        mx_SU = sem("mx_SU")
        mx_state = sem("mx_state")
        mx_osq = sem("mx_osq")
        mx_oss = sem("mx_oss")
        mx_or = sem("mx_or")
        mx_gate_gain = sem("mx_gate_gain")
        mx_y = sem("mx_y")
        mx_asq = sem("mx_asq")
        mx_ass = sem("mx_ass")
        mx_ars = sem("mx_ars")
        mx_an = sem("mx_an")
        mx_aT_psum = sem("mx_aT_psum")
        mx_aq = sem("mx_aq")
        mx_ak = sem("mx_ak")
        mx_S = sem("mx_S")
        mx_max = sem("mx_max")
        mx_P = sem("mx_P")
        mx_PT_psum = sem("mx_PT_psum")
        mx_PT = sem("mx_PT")
        mx_AV = sem("mx_AV")
        mx_ao = sem("mx_ao")
        mx_yT_psum = sem("mx_yT_psum")
        mx_yT_hi = sem("mx_yT_hi")
        mx_yT_lo = sem("mx_yT_lo")
        mx_vbeta = sem("mx_vbeta")
        mx_tap = sem("mx_tap")
        mx_conv_in2 = sem("mx_conv_in2")
        mx_aoss = sem("mx_aoss")
        mx_aor = sem("mx_aor")
        mx_ay = sem("mx_ay")
        mx_tail_sb = sem("mx_tail_sb")
        rt_small = sem("rt_small")
        rt_turned = sem("rt_turned")
        rt_qT = sem("rt_qT")
        rt_kT = sem("rt_kT")
        rt_scores = sem("rt_scores")
        rt_decayed = sem("rt_decayed")
        rt_o = sem("rt_o")
        rt_oss = sem("rt_oss")
        rt_orstd = sem("rt_orstd")
        rt_gate = sem("rt_gate")
        rt_y = sem("rt_y")
        rt_yT_psum = sem("rt_yT_psum")
        rt_yT_hi = sem("rt_yT_hi")
        rt_yT_lo = sem("rt_yT_lo")

        FFN_BLOCKS = 3 * FFC
        first = {}
        total = 0
        PHASES = [("ffn0", FFN_BLOCKS), ("da_in", 12), ("da_out", 4), ("ffn1", FFN_BLOCKS),
                  ("ffn2", FFN_BLOCKS), ("rt_in", 24), ("rt_out", 8), ("ffn3", FFN_BLOCKS),
                  ("mix_in", 14), ("mix_out", 4), ("ff2", 4 * FF2C)]
        for name, blocks in PHASES:
            first[name] = total
            total += blocks
        ffn_weights = [(A["ffn1_w_in"][0], A["ffn1_w_out"][0]), (A["ffn2_w_in"][0], A["ffn2_w_out"][0]),
                       (A["ffn1_w_in"][1], A["ffn1_w_out"][1]), (A["ffn2_w_in"][1], A["ffn2_w_out"][1])]
        norm_gains = [A["ffn1_norm"][0], A["mix_norm"][0], A["ffn2_norm"][0], A["ffn1_norm"][1],
                      A["mix_norm"][1], A["ffn2_norm"][1], A["mix_norm_gain_2"][0],
                      A["ffn_norm_gain_2"][0]]
        NORM_OF = {"ffn0": 0, "da_in": 1, "ffn1": 2, "ffn2": 3, "rt_in": 4, "ffn3": 5, "mix_in": 6, "ff2": 7}
        PROJ_NORM = {0: 1, 6: 4, 18: 6}

        def piece(tensor, q):
            return tensor[:, q % 2, (q // 2) * 512:(q // 2) * 512 + 512]

        def turned(tensor, q):
            return tensor[:, 4 * (q // 2):4 * (q // 2) + 4, (q % 2) * P:(q % 2) * P + P]

        def by_four(ap):
            return ap.rearrange("p (k n) -> p k n", k=4)

        last_out = [first[a] + b - 1 for a, b in PHASES
                    if a not in ("da_in", "rt_in", "mix_in")]

        level = [table[:, C_LEVEL + n * P:C_LEVEL + n * P + P].unsqueeze(1).to_broadcast([P, 8, P])
                 for n in range(LEVELS)]
        cum = table[:, C_CUM:C_CUM + P]
        last_row = table[:, C_LAST:C_LAST + P]
        sum_mask = cum.unsqueeze(1).to_broadcast([P, 8, P])
        two_idents = ident.unsqueeze(1).to_broadcast([P, 4, P])

        def quarter(ap, b):
            return ap[:, 4 * b:4 * b + 4, :]

        def wide(ap):
            return ap.unsqueeze(2).to_broadcast([P, ap.shape[1], P])

        def used(eng, n, turns=0):
            eng.wait_ge(wt_used, RING + n + 1 + RING * turns)

        block = ctx.enter_context(nc.Block())

        @block.sync
        def _(sp):
            def claim(n, turns):
                sp.wait_ge(lo_ready, n + 1 + RING * turns)

            def load_in_pair(n, w, j, c, turns=0):
                claim(n, turns)
                rows = w.rearrange("(j k p) n -> j p k n", k=4, p=P)[j]
                dst = raw[:, n % RING, :].rearrange("p (k h n) -> p k h n", k=4, h=2)
                for h in range(2):
                    sp.dma_start(dst[:, :, h, :], rows[:, :, bass.ds(c * 256 + h * FF, 256)])\
                        .then_inc(raw_full[n % RING], 16)

            def load_in(n, w, j, col, turns=0):
                claim(n, turns)
                rows = w.rearrange("(j k p) n -> j p k n", k=4, p=P)[j]
                dst = raw[:, n % RING, :].rearrange("p (k n) -> p k n", k=4)
                for h in range(2):
                    sp.dma_start(dst[:, 2 * h:2 * h + 2, :], rows[:, 2 * h:2 * h + 2, bass.ds(col, 512)])\
                        .then_inc(raw_full[n % RING], 16)

            def load_out(n, w, r, turns=0):
                claim(n, turns)
                for h in range(2):
                    sp.dma_start(raw[:, n % RING, h * D:(h + 1) * D], w[bass.ds(r * 256 + h * P, P), :])\
                        .then_inc(raw_full[n % RING], 16)

            def load_gain(g):
                if g >= 2:
                    sp.wait_ge(xg_ready, 4 * (g - 1))
                sp.dma_start(gains[:, g % 2, :], norm_gains[g].partition_broadcast(P)).then_inc(gain_full[g % 2], 16)

            def ffn(f, n0):
                w_in, w_out = ffn_weights[f]
                for j in range(2):
                    load_in_pair(n0 + j, w_in, j, 0)
                with sp.Fori(0, FFC - 1) as i:
                    for j in range(2):
                        load_in_pair(n0 + 2 + j, w_in, j, i + 1, turns=i)
                    load_out(n0 + 4, w_out, i, turns=i)
                load_out(n0 + FFN_BLOCKS - 1, w_out, FFC - 1)

            def project(n0, w, chunks):
                with sp.Fori(0, chunks // 3) as i:
                    for u in range(6):
                        load_in(n0 + u, w, u % 2, i * 1536 + u // 2 * 512, turns=2 * i)
                for u in range(chunks // 3 * 6, chunks * 2):
                    load_in(n0 + u, w, u % 2, u // 2 * 512)

            def out_blocks(n0, w, count):
                for r in range(count):
                    load_out(n0 + r, w, r)

            def ff2(n0):
                w_in, w_out = A["w_ff1_2"][0], A["w_ff2_2"][0]

                def chunk(c, n, turns=0):
                    for j in range(2):
                        load_in(n + j, w_in, j, c * 512, turns)
                    for r in range(2):
                        load_out(n + 2 + r, w_out, c * 2 + (r - 2), turns)

                for j in range(2):
                    load_in(n0 + j, w_in, j, 0)
                with sp.Fori(0, 2) as i:
                    for u in range(3):
                        chunk(3 * i + (1 + u), n0 + 2 + 4 * u, turns=4 * i)
                chunk(FF2C - 1, n0 + 4 * FF2C - 6)
                for r in range(2):
                    load_out(n0 + 4 * FF2C - 2 + r, w_out, FF2C * 2 - 2 + r)

            def load_da():
                for s, name in enumerate(("da_q_gain", "da_k_gain")):
                    for m in range(2):
                        sp.dma_start(da_gain[m * DA_DH:(m + 1) * DA_DH, s:s + 1],
                                      A[name].rearrange("a d -> d a")).then_inc(da_small, 16)
                sp.dma_start(da_lam[:, :, :], A["da_lambda"][0].partition_broadcast(P)).then_inc(da_small, 16)
                sp.dma_start(subln[:, :], A["da_subln"][0].partition_broadcast(P)).then_inc(da_small, 16)
                sp.dma_start(bias[:, :, :].rearrange("p h n -> p (h n)"), A["c_alibi"]).then_inc(bias_full, 16)

            def load_mix():
                w = A["w_in_2"][0].rearrange("(k p) n -> p k n", p=P)
                sp.dma_start(tail_w[:, :, :], w[:, :, 3584:3592]).then_inc(mx_small, 16)
                for dst, src in ((a_log, A["dn_a_log_2"][0]), (dt_bias, A["dn_dt_bias_2"][0])):
                    sp.dma_start(dst[:, :], src.partition_broadcast(P)).then_inc(mx_small, 16)
                for s, name in enumerate(("att_q_gain_2", "att_k_gain_2")):
                    for m in range(2):
                        sp.dma_start(att_gain[m * AT_DH:(m + 1) * AT_DH, s:s + 1],
                                      A[name].rearrange("a d -> d a")).then_inc(mx_small, 16)

            for t in range(2):
                sp.dma_start(x[:, t, :], A["x"][0, t * P:t * P + P, :]).then_inc(x_full, 16)
            ffn(0, first["ffn0"])
            load_gain(1)
            load_da()
            load_gain(2)
            project(first["da_in"], A["da_w_in"][0], 6)
            out_blocks(first["da_out"], A["da_w_out"][0], 4)
            load_gain(3)
            ffn(1, first["ffn1"])
            load_gain(4)
            ffn(2, first["ffn2"])
            load_mix()
            load_gain(5)
            project(first["rt_in"], A["rt_w_in"][0], 12)
            out_blocks(first["rt_out"], A["rt_w_out"][0], 8)
            load_gain(6)
            ffn(3, first["ffn3"])
            load_gain(7)
            for u in range(14):
                load_in(first["mix_in"] + u, A["w_in_2"][0], u % 2, (1536, 2048, 2560, 0, 512, 1024, 3072)[u // 2])
            out_blocks(first["mix_out"], A["w_out_2"][0], 4)
            ff2(first["ff2"])
            sp.wait_ge(x_stored, 64)

        @block.scalar
        def _(act):
            def split(n, turns=0):
                act.wait_ge(raw_full[n % RING], 32 * (n // RING + 1) + 32 * turns)
                used(act, n - RING, turns)
                act.activation(w_hi[:, n % RING, :], raw[:, n % RING, :], ACT.Copy).then_inc(hi_ready, 1)

            def norm(g):
                def squares(t):
                    if g:
                        act.wait_ge(resid_done, 4 * (g - 1) + t + 3)
                    if 2 * g + t:
                        act.wait_ge(ss_ready, 2 * g + t)
                    act.activation(square[:, :], x[:, t, :], ACT.Square, accum_out=sumsq[:, t:t + 1]).then_inc(ss_ready, 1)

                for q in range(4):
                    act.wait_ge(xt_psum, 4 * g + q + 1)
                    act.activation(turned(xT_hi, q), by_four(bank[4 + q][:, :]), ACT.Copy)\
                        .then_inc(xt_hi_ready, 1)
                    if q >= 2 and g:
                        squares(q - 2)
                if g == 0:
                    split(0)
                    split(1)
                    act.wait_ge(x_full, 32)
                    squares(0)
                    squares(1)

            def ffn(f, n0):
                cb = FFC * f

                def silu(c, i=0, first_chunk=False):
                    for t in range(2):
                        if t == 0:
                            act.wait_ge(in_done, cb + c + 1 + i)
                        else:
                            used(act, n0 + (1 if c == 0 else 3), i)
                        if c == 0 and t == 0:
                            act.wait_ge(rstd_ready, NORM_OF[f"ffn{f}"] + 1)
                        src = bank[t if first_chunk else 4 + t]
                        act.activation(silu_a[:, t, :], src[:, 0:256], ACT.Silu, scale=rstd[:, t:t + 1])\
                            .then_inc(silu_ready, 1)

                def turn_hidden(c, i=0):
                    act.wait_ge(ht_psum, cb + c + 1 + i)
                    act.activation(hT_hi[:, 0:2, :], bank[6][:, :].rearrange("p (k n) -> p k n", k=2), ACT.Copy)\
                        .then_inc(ht_hi_ready, 1)

                split(n0 + 2)
                split(n0 + 3)
                silu(0, first_chunk=True)
                with act.Fori(0, FFC - 1) as i:
                    turn_hidden(0, i)
                    split(n0 + 4, turns=i)
                    split(n0 + 5, turns=i)
                    silu(1, i)
                    split(n0 + 6, turns=i)
                turn_hidden(FFC - 1)
                split(n0 + FFN_BLOCKS + 1)

            def ff2(n0):
                def take_relu(c, n, i=0, turns=0, first_chunk=False):
                    for t in range(2):
                        if t == 0:
                            act.wait_ge(in2_done, c + 1 + i)
                            if c == 0:
                                act.wait_ge(rstd_ready, 8)
                        else:
                            used(act, n, turns)
                        src = bank[t if first_chunk else 4 + t]
                        act.activation(relu[:, t, :], src[:, :], ACT.Relu, scale=rstd[:, t:t + 1])\
                            .then_inc(relu_ready, 1)

                def turn_hidden(c, i=0):
                    for b in range(2):
                        act.wait_ge(ht2_psum, 2 * c + b + 1 + 2 * i)
                        act.activation(flat(hT_hi[:, 2 * b:2 * b + 2, :]), bank[6 + b][:, :], ACT.Copy)\
                            .then_inc(ht2_hi_ready, 1)

                def chunk(c, n, i=0, turns=0):
                    turn_hidden(c - 1, i)
                    split(n + 2, turns)
                    split(n + 3, turns)
                    take_relu(c, n + 1, i, turns)
                    split(n + 4, turns)
                    split(n + 5, turns)

                split(n0 + 2)
                split(n0 + 3)
                take_relu(0, n0 + 1, first_chunk=True)
                with act.Fori(0, 2) as i:
                    for u in range(3):
                        chunk(1 + u, n0 + 2 + 4 * u, 3 * i, 4 * i)
                chunk(FF2C - 1, n0 + 4 * FF2C - 6)
                turn_hidden(FF2C - 1)

            def read_chunk(n0, m0, m, dst, func=ACT.Copy, pair=None):
                for t in range(2):
                    if t == 0:
                        act.wait_ge(proj_done, m0 + m + 1)
                        if m == 0:
                            act.wait_ge(rstd_ready, PROJ_NORM[m0] + 1)
                    else:
                        used(act, n0 + 2 * m + 1)
                    act.activation(dst[:, t, :], bank[(m % 3 if pair is None else pair) * 2 + t][:, :], func, scale=rstd[:, t:t + 1])\
                        .then_inc(proj_read, 1)

            def da():
                n0, n1 = first["da_in"], first["da_out"]
                norm(1)
                for m in range(6):
                    split(n0 + 2 * m + 2)
                    split(n0 + 2 * m + 3)
                    read_chunk(n0, 0, m, da_proj[:, :, m * 512:m * 512 + 512])
                    if m == 0:
                        act.wait_ge(da_lamsum, 1)
                        act.activation(lam_exp[:, 0:2], lam_exp[:, 2:4], ACT.Exp).then_inc(da_lamexp, 1)
                for c in range(4):
                    act.wait_ge(da_turned, 2 * c + 1)
                    act.activation(qT[:, 2 * c:2 * c + 2, :].rearrange("p h n -> p (h n)"), bank[2 * c][:, :], ACT.Copy,
                                   scale=da_gain[:, 0:1]).then_inc(da_qT, 1)
                for i in range(DA_H + 3):
                    if i >= 3:
                        h = i - 3
                        act.wait_ge(da_oT_psum, h + 1)
                        act.activation(xT_hi[:, h, :], bank[6][:, 0:T], ACT.Copy).then_inc(da_oT_hi, 1)
                    for m in range(2):
                        if i < DA_H:
                            act.wait_ge(da_max, 4 * i + 2 * m + 2)
                            if i >= 2:
                                act.wait_ge(da_mixed, 2 * (i - 1))
                            for b in range(2):
                                cols = slice(0, P) if b == 0 else slice(P, 384)
                                act.activation(prob[:, i % 2, m, cols], bank[4 + m][:, cols], ACT.Exp,
                                               bias=neg_max[:, i % 2, 2 * m + b:2 * m + b + 1],
                                               accum_out=p_sum[:, i % 2, 2 * m + b:2 * m + b + 1]).then_inc(da_exp, 1)
                        if 1 <= i <= DA_H and m == 0:
                            act.wait_ge(da_mixT_psum, i)
                            if i >= 2:
                                act.wait_ge(da_o, i - 1)
                            act.activation(mixT[:, :], bank[6][:, 0:384], ACT.Copy).then_inc(da_mixT, 1)
                    if 1 <= i <= DA_H:
                        act.wait_ge(da_o, i)
                        for t in range(2):
                            if i >= 2 or t:
                                act.wait_ge(da_oss, 2 * (i - 1) + t)
                            if i >= 2:
                                act.wait_ge(da_orstd, i - 1)
                            act.activation(square[:, 0:P], bank[7][:, t * P:t * P + P], ACT.Square,
                                           accum_out=head_ss[:, t:t + 1]).then_inc(da_oss, 1)
                    if i >= 4 and i % 2 == 0:
                        split(n1 + (i - 4) // 2 + 2)

            def rt():
                n0, n1 = first["rt_in"], first["rt_out"]
                act.wait_ge(da_scores, 2 * DA_H)
                act.dma_start(bias[:, 0:RT_H, :].rearrange("p h n -> p (h n)"), A["c_decay"]).then_inc(rt_small, 16)
                norm(4)
                act.wait_ge(xt_psum, 4 * 5)
                act.dma_start(xg[:, :, :], A["rt_subln"][0].rearrange("(a h) v -> a (h v)", a=2).partition_broadcast(P))\
                    .then_inc(rt_small, 16)
                for m in range(12):
                    split(n0 + 2 * m + 2)
                    if m in (6, 7):
                        for c in range(2 * (m - 6), 2 * (m - 6) + 2):
                            act.wait_ge(rt_turned, 2 * c + 1)
                            act.activation(qT[:, 2 * c:2 * c + 2, :].rearrange("p h n -> p (h n)"), bank[6][:, :],
                                           ACT.Copy).then_inc(rt_qT, 1)
                    split(n0 + 2 * m + 3)
                    read_chunk(n0, 6, m, rt_chunk[m], ACT.Silu if m >= 8 else ACT.Copy, rt_pair[m])
                    if m >= 8:
                        h = m - 8
                        act.wait_ge(rt_o, h + 1)
                        for t in range(2):
                            if h:
                                act.wait_ge(rt_oss, 2 * h)
                                act.wait_ge(rt_orstd, h)
                            act.activation(square[:, t * 512:t * 512 + 512], bank[4 + t][:, :], ACT.Square,
                                           accum_out=head_ss[:, t:t + 1]).then_inc(rt_oss, 1)

                def turned_y(h):
                    for t in range(2):
                        act.wait_ge(rt_yT_psum, 2 * h + t + 1)
                        act.activation(xT_hi[:, h % 2 * 4:h % 2 * 4 + 4, t * P:t * P + P], by_four(bank[6 + t][:, :]),
                                       ACT.Copy).then_inc(rt_yT_hi, 1)

                turned_y(0)
                turned_y(1)
                for h in range(RT_H):
                    split(n1 + 2 * h + 2)
                    split(n1 + 2 * h + 3)
                    if h < 2:
                        turned_y(h + 2)

            def mix():
                n0, n1 = first["mix_in"], first["mix_out"]

                def take_conv(c):
                    act.wait_ge(mx_conv_psum, c + 1)
                    act.activation(conv_in[:, 2 * c:2 * c + 2, 3:3 + T],
                                   bank[2 + c % 4][:, :].rearrange("p (k n) -> p k n", k=2), ACT.Copy).then_inc(mx_conv_in, 1)

                def tap(s):
                    act.wait_ge(mx_conv_in, s + 1)
                    act.wait_ge(mx_conv_in2, s + 1)
                    for k in range(4):
                        c = 4 * s + k
                        act.activation(conv_out[s][:, k, :], conv_in[:, c, 0:T], ACT.Copy, scale=conv_w[:, c:c + 1])\
                            .then_inc(mx_tap, 1)

                def silu(s):
                    act.wait_ge(mx_conv, 12 * s + 12)
                    act.activation(flat(conv_out[s]), flat(conv_out[s]), ACT.Silu).then_inc(mx_silu, 1)

                def tokens(s):
                    for t in range(2):
                        act.wait_ge(mx_tok_psum, 2 * s + t + 1)
                        act.activation(flat(quarter(dn_tok[s], t)), bank[4 + s * 2 + t][:, :], ACT.Copy).then_inc(mx_tok, 1)

                def squares(s):
                    if s:
                        act.wait_ge(mx_dnss, 1)
                    act.wait_ge(mx_tok, 2 * s + 2)
                    act.activation(flat(sq8), flat(dn_tok[s]), ACT.Square).then_inc(mx_dnsq, 1)

                def probabilities(i):
                    act.wait_ge(mx_max, 2 * i + 2)
                    if i >= 2:
                        act.wait_ge(mx_PT_psum, i - 1)
                    for b in range(2):
                        cols = slice(0, P) if b == 0 else slice(P, 384)
                        act.activation(prob_a[:, i % 2, cols], bank[i % 2][:, cols], ACT.Exp,
                                       bias=att_max[:, i, b:b + 1], accum_out=att_sum[:, b, i:i + 1]).then_inc(mx_P, 1)

                def turned_probabilities(h):
                    act.wait_ge(mx_PT_psum, h + 1)
                    if h:
                        act.wait_ge(mx_AV, h)
                    act.activation(probT, bank[2][:, 0:384], ACT.Copy).then_inc(mx_PT, 1)

                def turned_output(p, b):
                    for t in range(2):
                        act.wait_ge(mx_yT_psum, 2 * p + t + 1)
                        act.activation(xT_hi[:, 4 * p:4 * p + 4, t * P:t * P + P], by_four(bank[b + t][:, :]), ACT.Copy)\
                            .then_inc(mx_yT_hi, 1)

                act.wait_ge(rt_decayed, 2 * RT_H)
                act.dma_start(bias[:, :, :], bass.AP(A["rel_bias_2"].tensor, MAX_REL - (P - 1), [[1, P], [N_REL, AT_H], [1, T]]))\
                    .then_inc(mx_bias, 16)
                norm(6)
                act.wait_ge(xg_ready, 28)
                act.dma_start(flip, A["c_flip"]).then_inc(mx_small, 16)
                act.dma_start(conv_row, A["dn_conv_w_2"][0].rearrange("j (c p) -> (j c) p", p=P)).then_inc(mx_small, 16)
                act.dma_start(dn_gain, A["dn_out_gain_2"][0].partition_broadcast(P)).then_inc(mx_small, 16)
                act.dma_start(out_gain, A["att_out_gain_2"][0].partition_broadcast(P)).then_inc(mx_small, 16)
                dst = [mx_dn[:, m, :, :] for m in range(3)] + [mx_att[:, m, :, :] for m in range(3)] + [mx_gate]

                def read(m):
                    read_chunk(n0, 18, m, dst[m], ACT.Silu if m == 6 else ACT.Copy, mx_pair[m])

                for m in range(3):
                    split(n0 + 2 * m + 2)
                    split(n0 + 2 * m + 3)
                    if m == 0:
                        act.wait_ge(mx_small, MX_SMALL)
                        act.activation(tail_hi[:, :, :], tail_w[:, :, :], ACT.Copy).then_inc(mx_tail_hi, 1)
                    read(m)
                act.wait_ge(mx_tail, 1)
                act.activation(tail_row, bank[6][0:8, 0:T], ACT.Copy).then_inc(mx_tail_sb, 1)
                split(n0 + 8)
                act.wait_ge(mx_tail, 2)
                for t in range(2):
                    act.activation(tail_ab[:, t, :], bank[6][:, t * 8:t * 8 + 8], ACT.Copy, scale=rstd[:, t:t + 1])\
                        .then_inc(mx_ab, 1)
                act.wait_ge(mx_convw_psum, 1)
                act.activation(conv_w[:, :], bank[7][:, 0:48], ACT.Copy).then_inc(mx_convw, 1)
                act.wait_ge(mx_convw, 1)
                act.wait_ge(mx_abs, 1)
                act.activation(ez, uu, ACT.Exp, scale=-1.0).then_inc(mx_exp, 1)
                act.activation(dd.rearrange("p (t h) -> p t h", t=2), tail_ab[:, :, 4:8], ACT.Exp, scale=-1.0)\
                    .then_inc(mx_exp, 1)
                act.activation(ea[:, :], a_log[:, :], ACT.Exp).then_inc(mx_exp, 1)
                act.wait_ge(mx_onep, 1)
                act.activation(ln, uu, ACT.Ln).then_inc(mx_ln, 1)
                split(n0 + 9)
                act.wait_ge(mx_zero, 1)
                take_conv(0)
                take_conv(2)
                read(3)
                split(n0 + 10)
                tap(0)
                take_conv(4)
                tap(1)
                split(n0 + 11)
                tap(2)
                read(4)
                split(n0 + 12)
                silu(0)
                silu(1)
                act.wait_ge(mx_dec, 1)
                act.activation(edec, dec, ACT.Exp).then_inc(mx_etail, 1)
                act.wait_ge(mx_last_diff, 1)
                act.activation(etail, etail, ACT.Exp).then_inc(mx_etail, 1)
                act.wait_ge(mx_rows, 1)
                act.wait_ge(mx_diff, 8)
                for b in range(2):
                    act.activation(flat(quarter(dn_exprow, b)), bank[4 + b][:, :], ACT.Exp).then_inc(mx_exprow, 1)
                act.activation(flat(dn_LT), flat(dn_LT), ACT.Exp).then_inc(mx_exprow, 1)
                split(n0 + 13)
                tokens(0)
                read(5)
                silu(2)
                squares(0)
                tokens(1)
                squares(1)
                read(6)
                for c in range(2):
                    act.wait_ge(mx_aT_psum, 2 * c + 1)
                    act.activation(flat(qT[:, 2 * c:2 * c + 2, :]), bank[2 - 2 * c][:, :], ACT.Copy, scale=att_gain[:, 0:1])\
                        .then_inc(mx_aq, 1)
                for s in range(2):
                    for t in range(2):
                        act.wait_ge(mx_back_psum, 2 * s + t + 1)
                        act.activation((dn_qhT, dn_khT)[s][:, :, t * P:t * P + P], by_four(bank[4 + s * 2 + t][:, :]),
                                       ACT.Copy).then_inc(mx_back, 1)
                probabilities(0)
                turned_probabilities(0)
                probabilities(1)
                for n in range(1, LEVELS):
                    for b in range(2):
                        act.wait_ge(mx_Y, 2 * (n - 1) + b + 1)
                        act.activation(flat(quarter(dn_Y, b)), bank[4 + b][:, :], ACT.Copy).then_inc(mx_Ysb, 1)
                    if n <= 3:
                        split(n1 + n - 1)
                    turned_probabilities(n)
                    probabilities(n + 1)
                act.wait_ge(mx_val, 1)
                for b in range(2):
                    act.activation(flat(quarter(dn_val, b)), bank[4 + b][:, :], ACT.Copy).then_inc(mx_valsb, 1)
                turned_probabilities(6)
                probabilities(7)
                turned_probabilities(7)
                act.wait_ge(mx_ao, 4)
                for t in range(2):
                    act.activation(relu[:, 0, :], att_y[:, t, :], ACT.Square, accum_out=head_ss[:, t:t + 1]).then_inc(mx_aoss, 1)
                    act.wait_ge(mx_aoss, t + 1)
                act.wait_ge(mx_O, 2)
                act.wait_ge(mx_dnss, 2)
                act.activation(square[:, 0:512], bank[4][:, :], ACT.Square).then_inc(mx_osq, 1)
                turned_output(0, 0)
                act.wait_ge(mx_O, 4)
                act.activation(square[:, 512:1024], bank[5][:, :], ACT.Square).then_inc(mx_osq, 1)
                turned_output(1, 6)
                split(n1 + 3)
                split(n1 + 4)
                split(n1 + 5)
            act.sem_inc(proj_read, 6)
            act.dma_start(gains[:, 0, :], norm_gains[0].partition_broadcast(P)).then_inc(gain_full[0], 16)
            act.dma_start(ident, A["c_table"][:, C_IDENT:C_IDENT + P]).then_inc(table_full, 16)
            act.wait_ge(pool_chain, 1)
            act.activation(lam[:, :], neghalf[:, 0:1], ACT.Silu)
            norm(0)
            act.dma_start(table[:, P:], A["c_table"][:, P:]).then_inc(table_full, 16)
            ffn(0, first["ffn0"])
            da()
            norm(2)
            ffn(1, first["ffn1"])
            norm(3)
            ffn(2, first["ffn2"])
            rt()
            norm(5)
            ffn(3, first["ffn3"])
            mix()
            norm(7)
            ff2(first["ff2"])
            for q in range(4):
                act.wait_ge(resid_done, 4 * (len(last_out) - 1) + q + 1)
                act.dma_start(out[0].rearrange("(t p) d -> p t d", p=P)[:, q % 2, q // 2 * 512:q // 2 * 512 + 512],
                              piece(x, q)).then_inc(x_stored, 16)

        @block.gpsimd
        def _(pool):
            chain = [0]

            def link(ins):
                chain[0] += 1
                ins.then_inc(pool_chain, 1)
                pool.wait_ge(pool_chain, chain[0])

            def norm(g):
                pool.wait_ge(ss_ready, 2 * (g + 1))
                link(pool.tensor_scalar(meansq[:, :], sumsq[:, :], 1.0 / D, EPS, ALU.mult, ALU.add))
                pool.tensor_tensor(rstd[:, :], meansq[:, :], neghalf[:, 0:2], ALU.pow).then_inc(rstd_ready, 1)

            def split(n):
                pool.wait_ge(lo_ready, RING + n)
                pool.wait_ge(hi_ready, n + 1)
                pool.tensor_tensor(w_lo[:, n % RING, :], raw[:, n % RING, :], w_hi[:, n % RING, :].bitcast(F32),
                                   ALU.subtract).then_inc(lo_ready, 1)

            def da():
                pool.wait_ge(da_small, 16 * 6)
                link(pool.tensor_scalar(da_gain[:, 0:1], da_gain[:, 0:1], DA_DH ** -0.5, None, ALU.mult))
                pool.tensor_scalar(subln[:, :], subln[:, :], 1.0 - LAM_INIT, None, ALU.mult).then_inc(da_small, 16)
                norm(1)
                pool.wait_ge(bias_full, 16)
                pool.tensor_copy(ident_r, ident)
                pool.tensor_copy(diag_bias, bias[:, :, 0:P]).then_inc(bias_full, 1)
                pool.wait_ge(bias_full, 17)
                for s in range(2):
                    pool.wait_ge(proj_read, 6 + 4 * (s + 1))
                    for t in range(2):
                        qk = da_proj[:, t, s * D:s * D + D]
                        if s:
                            pool.wait_ge(da_sumsq, t + 1)
                        pool.tensor_tensor(xg[:, t, :], qk, qk, ALU.mult).then_inc(da_square, 1)
                    for t in range(2):
                        u = 2 * s + t
                        pool.wait_ge(da_sumsq, u + 1)
                        link(pool.tensor_scalar(qk_ss[:, u, :], qk_ss[:, u, :], 1.0 / DA_DH, EPS, ALU.mult, ALU.add))
                        pool.tensor_tensor(qk_rstd[:, u, :], qk_ss[:, u, :], neghalf[:, 0:16], ALU.pow).then_inc(da_rstd, 1)
                for h in range(DA_H):
                    pool.wait_ge(da_oss, 2 * h + 2)
                    link(pool.tensor_scalar(meansq[:, :], head_ss[:, :], 1.0 / P, EPS, ALU.mult, ALU.add))
                    if h:
                        pool.wait_ge(da_normed_o, 2 * h)
                    pool.tensor_tensor(head_rstd[:, :], meansq[:, :], neghalf[:, 0:2], ALU.pow).then_inc(da_orstd, 1)
                    if h in (3, 5, 7):
                        split(first["da_out"] + (h - 3) // 2 + 2)

            def rt():
                norm(4)
                pool.wait_ge(rt_small, 32)
                for h in range(RT_H):
                    pool.wait_ge(proj_read, 6 + 2 * (6 + 8 + h + 1))
                    for t in range(2):
                        gate = rt_g[:, t, h * 512:h * 512 + 512]
                        pool.tensor_tensor(gate, gate, xg[:, h // 2, h % 2 * 512:h % 2 * 512 + 512], ALU.mult)\
                            .then_inc(rt_gate, 1)
                    pool.wait_ge(rt_oss, 2 * h + 2)
                    link(pool.tensor_scalar(meansq[:, :], head_ss[:, :], 1.0 / RT_DV, EPS, ALU.mult, ALU.add))
                    if h:
                        pool.wait_ge(rt_y, 2 * h)
                    pool.tensor_tensor(head_rstd[:, :], meansq[:, :], neghalf[:, 0:2], ALU.pow).then_inc(rt_orstd, 1)

            def mix():
                pool.wait_ge(mx_small, MX_SMALL)
                link(pool.tensor_scalar(att_gain[:, 0:1], att_gain[:, 0:1], AT_DH ** -0.5, None, ALU.mult))
                norm(6)
                pool.wait_ge(mx_bias, 16)
                pool.wait_ge(rstd_ready, 7)
                pool.memset(bias[0:CHUNK, :, 0:CHUNK], MASKED).then_inc(mx_bias, 1)
                pool.wait_ge(mx_bias, 17)

                def att_squares(s):
                    pool.wait_ge(proj_read, 6 + 2 * (18 + 3 + s + 1))
                    for t in range(2):
                        if s or t:
                            pool.wait_ge(mx_ass, 2 * s + t)
                        pool.tensor_tensor(att_square, mx_att[:, s, t, :], mx_att[:, s, t, :], ALU.mult).then_inc(mx_asq, 1)
                    pool.wait_ge(mx_ass, 2 * s + 2)
                    at = slice(16 * s, 16 * s + 16)
                    link(pool.tensor_scalar(att_ss[:, at], att_ss[:, at], 1.0 / AT_DH, EPS, ALU.mult, ALU.add))
                    pool.tensor_tensor(att_rs[:, at], att_ss[:, at], neghalf[:, 0:16], ALU.pow).then_inc(mx_ars, 1)

                att_squares(0)
                att_squares(1)
                for s in range(2):
                    pool.wait_ge(mx_dnss, s + 1)
                    link(pool.tensor_scalar(dn_ss[:, s, :], dn_ss[:, s, :], EPS, None, ALU.add))
                    ins = pool.tensor_tensor(dn_rstd[:, s, :], dn_ss[:, s, :], neghalf[:, 0:8], ALU.pow)
                    if s == 0:
                        link(ins)
                        ins = pool.tensor_scalar(dn_rstd[:, 0, :], dn_rstd[:, 0, :], DN_D ** -0.5, None, ALU.mult)
                    ins.then_inc(mx_dnr, 1)
                pool.wait_ge(mx_back_psum, 4)
                pool.tensor_tensor(dn_kbe, dn_tok[1], wide(bed), ALU.mult).then_inc(mx_ktail, 1)
                pool.wait_ge(mx_ktail, 1)
                pool.tensor_tensor(dn_ktail, dn_tok[1], wide(etail), ALU.mult).then_inc(mx_ktail, 1)
                pool.wait_ge(mx_gram, 2)
                pool.tensor_tensor(dn_qhT[:, :, 0:P], dn_qhT[:, :, 0:P], quarter(dn_exprow, 0), ALU.mult)\
                    .then_inc(mx_ktail, 1)
                pool.tensor_tensor(dn_qhT[:, :, P:T], dn_qhT[:, :, P:T], quarter(dn_exprow, 1), ALU.mult)\
                    .then_inc(mx_qd, 1)
                pool.wait_ge(proj_read, 6 + 2 * 25)
                for t in range(2):
                    pool.tensor_tensor(by_four(mx_gate[:, t, :]), by_four(mx_gate[:, t, :]),
                                       dn_gain[:, :].unsqueeze(1).to_broadcast([P, 4, P]), ALU.mult).then_inc(mx_gate_gain, 1)
                pool.wait_ge(mx_aoss, 2)
                link(pool.tensor_scalar(meansq[:, :], head_ss[:, :], 1.0 / 512, EPS, ALU.mult, ALU.add))
                pool.tensor_tensor(head_rstd[:, :], meansq[:, :], neghalf[:, 0:2], ALU.pow).then_inc(mx_aor, 1)
                pool.wait_ge(mx_oss, 2)
                link(pool.tensor_scalar(dn_ss[:, 0, :], dn_ss[:, 0, :], 1.0 / DN_D, EPS, ALU.mult, ALU.add))
                pool.tensor_tensor(dn_rstd[:, 0, :], dn_ss[:, 0, :], neghalf[:, 0:8], ALU.pow).then_inc(mx_or, 1)
            link(pool.memset(neghalf[:, :], -0.5))
            norm(0)
            da()
            norm(2)
            norm(3)
            rt()
            norm(5)
            mix()
            norm(7)

        @block.vector
        def _(dve):
            chain = [0]

            def link(ins):
                chain[0] += 1
                ins.then_inc(dve_chain, 1)
                dve.wait_ge(dve_chain, chain[0])

            def split(n, turns=0):
                dve.wait_ge(hi_ready, n + 1 + RING * turns)
                dve.tensor_tensor(w_lo[:, n % RING, :], raw[:, n % RING, :], w_hi[:, n % RING, :].bitcast(F32),
                                  ALU.subtract).then_inc(lo_ready, 1)

            def ff2(n0):
                def square_relu(c, i=0):
                    for t in range(2):
                        dve.wait_ge(relu_ready, 2 * c + t + 1 + 2 * i)
                        dve.tensor_tensor(hid[:, t, :], relu[:, t, :], relu[:, t, :], ALU.mult).then_inc(sq_ready, 1)

                def turn_hidden(c, i=0):
                    for b in range(2):
                        dve.wait_ge(ht2_hi_ready, 2 * c + b + 1 + 2 * i)
                        dve.tensor_tensor(flat(hT_lo[:, 2 * b:2 * b + 2, :]), bank[6 + b][:, :],
                                          flat(hT_hi[:, 2 * b:2 * b + 2, :]).bitcast(F32), ALU.subtract)\
                            .then_inc(ht2_lo_ready, 1)

                def chunk(c, n, i=0, turns=0):
                    turn_hidden(c - 1, i)
                    split(n + 2, turns)
                    split(n + 3, turns)
                    square_relu(c, i)
                    split(n + 4, turns)
                    split(n + 5, turns)

                split(n0 + 2)
                split(n0 + 3)
                square_relu(0)
                with dve.Fori(0, 2) as i:
                    for u in range(3):
                        chunk(1 + u, n0 + 2 + 4 * u, 3 * i, 4 * i)
                chunk(FF2C - 1, n0 + 4 * FF2C - 6)
                turn_hidden(FF2C - 1)

            def residual(phase, q, scale):
                if q < 3:
                    dve.wait_ge(acc_done, 3 * phase + q + 1)
                else:
                    used(dve, last_out[phase])
                dve.scalar_tensor_tensor(piece(x, q), bank[q][:, :], scale, piece(x, q), ALU.mult, ALU.add)\
                    .then_inc(resid_done, 1)
                dve.wait_ge(resid_done, 4 * phase + q + 1)

            def norm(g, scale=None, n=None):
                def lo(q):
                    dve.wait_ge(xt_hi_ready, 4 * g + q + 1)
                    dve.tensor_tensor(turned(xT_lo, q), by_four(bank[4 + q][:, :]), turned(xT_hi, q).bitcast(F32),
                                      ALU.subtract).then_inc(xt_lo_ready, 1)

                dve.wait_ge(gain_full[g % 2], 16 * (g // 2 + 1))
                for q in range(4):
                    if g:
                        residual(g - 1, q, scale)
                    elif q < 2:
                        dve.wait_ge(x_full, 32)
                    dve.tensor_tensor(piece(xg, q), piece(x, q), gains[:, g % 2, q // 2 * 512:q // 2 * 512 + 512], ALU.mult).then_inc(xg_ready, 1)
                    if q >= 1:
                        lo(q - 1)
                    if q == 2 and g:
                        split(n)
                lo(3)

            def ffn(f, n0):
                cb = FFC * f

                def times_b(c, i=0, first_chunk=False):
                    for t in range(2):
                        dve.wait_ge(silu_ready, 2 * (cb + c) + t + 1 + 2 * i)
                        src = bank[t if first_chunk else 4 + t]
                        dve.scalar_tensor_tensor(hid[:, t, 0:256], src[:, 256:512], rstd[:, t:t + 1],
                                                 silu_a[:, t, :], ALU.mult, ALU.mult).then_inc(hid_ready, 1)

                def turn_hidden(c, i=0):
                    dve.wait_ge(ht_hi_ready, cb + c + 1 + i)
                    dve.tensor_tensor(hT_lo[:, 0:2, :], bank[6][:, :].rearrange("p (k n) -> p k n", k=2),
                                      hT_hi[:, 0:2, :].bitcast(F32), ALU.subtract).then_inc(ht_lo_ready, 1)

                split(n0 + 2)
                split(n0 + 3)
                times_b(0, first_chunk=True)
                with dve.Fori(0, FFC - 1) as i:
                    turn_hidden(0, i)
                    split(n0 + 4, turns=i)
                    split(n0 + 5, turns=i)
                    times_b(1, i)
                    split(n0 + 6, turns=i)
                turn_hidden(FFC - 1)

            def da():
                n0, n1 = first["da_in"], first["da_out"]
                norm(1, 0.5, n0 + 1)
                for m in range(6):
                    split(n0 + 2 * m + 2)
                    split(n0 + 2 * m + 3)
                    if m == 0:
                        dve.wait_ge(da_small, 16 * 6)
                        link(dve.tensor_tensor(lam_prod[:, :, :], da_lam[:, 0::2, :], da_lam[:, 1::2, :], ALU.mult))
                        dve.tensor_reduce(lam_exp[:, 2:4], lam_prod[:, :, :], AX_X, ALU.add).then_inc(da_lamsum, 1)
                    if m == 1:
                        dve.wait_ge(da_lamexp, 1)
                        link(dve.scalar_tensor_tensor(lam[:, :], lam_exp[:, 0:1], LAM_INIT, lam_exp[:, 1:2],
                                                      ALU.add, ALU.subtract))
                    if m in (2, 4):
                        s = m // 2 - 1
                        for t in range(2):
                            u = 2 * s + t
                            dve.wait_ge(da_square, u + 1)
                            dve.tensor_reduce(qk_ss[:, u, :], xg[:, t, :].rearrange("p (g d) -> p g d", d=DA_DH),
                                              AX_X, ALU.add).then_inc(da_sumsq, 1)
                    if m in (3, 5):
                        s = m // 2 - 1
                        for t in range(2):
                            u = 2 * s + t
                            dve.wait_ge(da_rstd, u + 1)
                            qk = da_proj[:, t, s * D:s * D + D].rearrange("p (g d) -> p g d", d=DA_DH)
                            dve.tensor_tensor(qk, qk, qk_rstd[:, u, :].unsqueeze(2).to_broadcast([P, 16, DA_DH]),
                                              ALU.mult).then_inc(da_normed, 1)
                for c in range(4):
                    dve.wait_ge(da_turned, 2 * c + 2)
                    dve.tensor_scalar(kT[:, 2 * c:2 * c + 2, :].rearrange("p h n -> p (h n)"), bank[2 * c + 1][:, :],
                                      da_gain[:, 1:2], None, ALU.mult).then_inc(da_kT, 1)
                for i in range(DA_H + 3):
                    if 1 <= i <= DA_H:
                        h = i - 1
                        dve.wait_ge(da_exp, 4 * h + 4)
                        if h >= 2:
                            dve.wait_ge(da_mixT_psum, h - 1)
                        link(dve.reciprocal(p_recip[:, :], p_sum[:, h % 2, :]))
                        link(dve.tensor_scalar(recip_lam[:, :], p_recip[:, 2:4], lam[:, :], None, ALU.mult))
                        for b in range(2):
                            cols = slice(0, P) if b == 0 else slice(P, 384)
                            last = dve.tensor_scalar(prob1[:, cols], prob[:, h % 2, 1, cols], recip_lam[:, b:b + 1],
                                                     None, ALU.mult)
                            if b:
                                link(last)
                        for b in range(2):
                            cols = slice(0, P) if b == 0 else slice(P, 384)
                            dve.scalar_tensor_tensor(mixed[:, h % 2, cols], prob[:, h % 2, 0, cols], p_recip[:, b:b + 1],
                                                     prob1[:, cols], ALU.mult, ALU.subtract).then_inc(da_mixed, 1)
                        dve.wait_ge(da_mixed, 2 * h + 2)
                    if i >= 3:
                        h = i - 3
                        dve.wait_ge(da_oT_hi, h + 1)
                        dve.tensor_tensor(xT_lo[:, h, :], bank[6][:, 0:T], xT_hi[:, h, :].bitcast(F32),
                                          ALU.subtract).then_inc(da_oT_lo, 1)
                    if 2 <= i <= DA_H + 1:
                        h = i - 2
                        dve.wait_ge(da_orstd, h + 1)
                        if h:
                            dve.wait_ge(da_oT_psum, h)
                        for t in range(2):
                            dve.scalar_tensor_tensor(head_out[:, t, 0:P], bank[7][:, t * P:t * P + P],
                                                     head_rstd[:, t:t + 1], subln[:, :], ALU.mult, ALU.mult)\
                                .then_inc(da_normed_o, 1)
                    if i < DA_H:
                        for m in range(2):
                            dve.wait_ge(da_scores, 2 * i + m + 1)
                            if i >= 2 and m == 0:
                                dve.wait_ge(da_exp, 4 * (i - 1))
                            for b in range(2):
                                cols = slice(0, P) if b == 0 else slice(P, 384)
                                dve.tensor_reduce(neg_max[:, i % 2, 2 * m + b:2 * m + b + 1], bank[4 + m][:, cols],
                                                  AX_X, ALU.max, negate=True).then_inc(da_max, 1)
                dve.wait_ge(lo_ready, RING + n1 + 5)

            def rt():
                n0, n1 = first["rt_in"], first["rt_out"]

                def gated(h):
                    dve.wait_ge(rt_orstd, h + 1)
                    dve.wait_ge(rt_gate, 2 * h + 2)
                    for t in range(2):
                        gate = rt_g[:, t, h * 512:h * 512 + 512]
                        dve.scalar_tensor_tensor(gate, bank[4 + t][:, :], head_rstd[:, t:t + 1], gate, ALU.mult, ALU.mult)\
                            .then_inc(rt_y, 1)

                def turned_y(h):
                    for t in range(2):
                        dve.wait_ge(rt_yT_hi, 2 * h + t + 1)
                        at = (slice(None), slice(h % 2 * 4, h % 2 * 4 + 4), slice(t * P, t * P + P))
                        dve.tensor_tensor(xT_lo[at], by_four(bank[6 + t][:, :]), xT_hi[at].bitcast(F32), ALU.subtract)\
                            .then_inc(rt_yT_lo, 1)

                norm(4, 0.5, n0 + 1)
                for m in range(12):
                    split(n0 + 2 * m + 2)
                    if m in (6, 7):
                        for c in range(2 * (m - 6), 2 * (m - 6) + 2):
                            dve.wait_ge(rt_turned, 2 * c + 2)
                            dve.tensor_copy(kT[:, 2 * c:2 * c + 2, :].rearrange("p h n -> p (h n)"), bank[7][:, :])\
                                .then_inc(rt_kT, 1)
                    if m >= 8:
                        h = m - 8
                        dve.wait_ge(rt_scores, h + 1)
                        dve.wait_ge(rt_small, 32)
                        if h >= 2:
                            dve.wait_ge(rt_o, h - 1)
                        for cols, decay in ((slice(0, T), bias[:, h, :]), (slice(T, 384), bias[:, h, 0:P])):
                            dve.scalar_tensor_tensor(rt_att[:, h % 2, cols], bank[6][:, cols], RT_DK ** -0.5, decay,
                                                     ALU.mult, ALU.mult).then_inc(rt_decayed, 1)
                        if h:
                            gated(h - 1)
                    split(n0 + 2 * m + 3)
                turned_y(0)
                gated(3)
                turned_y(1)
                for h in range(RT_H):
                    split(n1 + 2 * h + 2)
                    if h < 3:
                        split(n1 + 2 * h + 3)
                    if h < 2:
                        turned_y(h + 2)

            def mix():
                n0, n1 = first["mix_in"], first["mix_out"]
                by_t = lambda ap: ap.rearrange("p (t h) -> p t h", t=2)
                each_t = lambda ap: ap.unsqueeze(1).to_broadcast([P, 2, DN_H])

                def log_decay():
                    dve.wait_ge(mx_exp, 3)
                    dve.tensor_scalar(uu, ez, 1.0, None, ALU.add).then_inc(mx_onep, 1)
                    link(dve.tensor_scalar(beta, dd, 1.0, None, ALU.add))
                    dve.reciprocal(beta, beta).then_inc(mx_beta, 1)
                    dve.wait_ge(mx_beta, 1)
                    link(dve.scalar_tensor_tensor(dd, uu, -1.0, ez, ALU.add, ALU.subtract))
                    link(dve.reciprocal(ez, uu))
                    link(dve.tensor_tensor(dd, dd, ez, ALU.mult))
                    dve.wait_ge(mx_ln, 1)
                    link(dve.tensor_tensor(dd, ln, dd, ALU.subtract))
                    link(dve.scalar_tensor_tensor(dd, zz, 0.0, dd, ALU.max, ALU.add))
                    dve.scalar_tensor_tensor(by_t(gg), by_t(dd), -1.0, each_t(ea[:, :]), ALU.mult, ALU.mult).then_inc(mx_g, 1)

                def take_conv(c):
                    dve.wait_ge(mx_conv_psum, c + 1)
                    dve.tensor_copy(conv_in[:, 2 * c:2 * c + 2, 3:3 + T],
                                    bank[2 + c % 4][:, :].rearrange("p (k n) -> p k n", k=2)).then_inc(mx_conv_in2, 1)

                def convolve(s):
                    dve.wait_ge(mx_conv_in, s + 1)
                    dve.wait_ge(mx_conv_in2, s + 1)
                    for j in range(1, CONV_K):
                        for k in range(4):
                            c = 4 * s + k
                            if j == 1:
                                dve.wait_ge(mx_tap, c + 1)
                            else:
                                dve.wait_ge(mx_conv, 12 * s + 4 * (j - 2) + k + 1)
                            dst = conv_out[s][:, k, :]
                            dve.scalar_tensor_tensor(dst, conv_in[:, c, j:j + T], conv_w[:, 12 * j + c:12 * j + c + 1],
                                                     dst, ALU.mult, ALU.add).then_inc(mx_conv, 1)

                def att_sum_squares(u):
                    dve.wait_ge(mx_asq, u + 1)
                    dve.tensor_reduce(att_ss[:, 8 * u:8 * u + 8], att_square.rearrange("p (g d) -> p g d", d=AT_DH),
                                      AX_X, ALU.add).then_inc(mx_ass, 1)

                def att_normalise(s):
                    dve.wait_ge(mx_ars, s + 1)
                    for t in range(2):
                        u = 2 * s + t
                        qk = mx_att[:, s, t, :].rearrange("p (g d) -> p g d", d=AT_DH)
                        dve.tensor_tensor(qk, qk, att_rs[:, 8 * u:8 * u + 8].unsqueeze(2).to_broadcast([P, 8, AT_DH]),
                                          ALU.mult).then_inc(mx_an, 1)

                def sum_squares(s):
                    dve.wait_ge(mx_dnsq, s + 1)
                    dve.tensor_reduce(dn_ss[:, s, :], sq8, AX_X, ALU.add).then_inc(mx_dnss, 1)

                def level_mask(n, b):
                    if n > 1:
                        dve.wait_ge(mx_Y, 2 * (n - 2) + b + 1)
                    dve.tensor_tensor(quarter(dn_MT, b), quarter(dn_AT, b), level[n][:, 4 * b:4 * b + 4, :], ALU.mult)\
                        .then_inc(mx_MT, 1)

                def maxima(i):
                    dve.wait_ge(mx_S, i + 1)
                    for b in range(2):
                        cols = slice(0, P) if b == 0 else slice(P, 384)
                        dve.tensor_reduce(att_max[:, i, b:b + 1], bank[i % 2][:, cols], AX_X, ALU.max, negate=True)\
                            .then_inc(mx_max, 1)

                def att_out(g):
                    dve.wait_ge(mx_P, 8 * g + 8)
                    link(dve.reciprocal(att_recip[:, :, 4 * g:4 * g + 4], att_sum[:, :, 4 * g:4 * g + 4]))
                    dve.wait_ge(mx_AV, 4 * g + 4)
                    for t in range(2):
                        dve.tensor_tensor(att_y[:, t, g * 256:g * 256 + 256].rearrange("p (g d) -> p g d", d=AT_DH),
                                          bank[3][:, :].rearrange("p (h t d) -> p t h d", h=4, t=2)[:, t],
                                          att_recip[:, t, 4 * g:4 * g + 4].unsqueeze(2).to_broadcast([P, 4, AT_DH]),
                                          ALU.mult).then_inc(mx_ao, 1)

                def recur(n):
                    t, r = n // 2, slice(n % 2 * CHUNK, n % 2 * CHUNK + CHUNK)
                    val = flat(quarter(dn_val, t))[r, :]
                    if n == 0:
                        dve.wait_ge(mx_valsb, 4)
                        dve.tensor_copy(dn_vnew[r, :], val).then_inc(mx_vnew, 1)
                    else:
                        dve.wait_ge(mx_KS, n)
                        if n >= 2:
                            dve.wait_ge(mx_O, n - 1)
                        dve.tensor_tensor(dn_vnew[r, :], val, bank[6][r, :], ALU.subtract).then_inc(mx_vnew, 1)
                    if n == 0:
                        dve.wait_ge(mx_SU, 1)
                        dve.tensor_copy(dn_state[0], bank[7][:, :]).then_inc(mx_state, 1)
                    elif n < 3:
                        dve.wait_ge(mx_SU, n + 1)
                        dve.wait_ge(mx_O, n)
                        for h in range(4):
                            at = slice(h * P, h * P + P)
                            dve.wait_ge(mx_state, 4 * (n - 1) + 1)
                            decay = dn_exprow[:, 4 * t + h, r.stop - 1:r.stop]
                            dve.scalar_tensor_tensor(dn_state[n % 2][:, at], dn_state[(n - 1) % 2][:, at], decay, bank[7][:, at],
                                                     ALU.mult, ALU.add).then_inc(mx_state, 1)

                norm(6, 0.5, n0 + 1)
                dve.memset(conv_in[:, :, 0:3], 0.0).then_inc(mx_zero, 1)
                for u in range(6):
                    split(n0 + 2 + u)
                    if u == 1:
                        dve.wait_ge(mx_tail_hi, 1)
                        dve.tensor_tensor(tail_lo[:, :, :], tail_w[:, :, :], tail_hi[:, :, :].bitcast(F32), ALU.subtract)\
                            .then_inc(mx_tail_lo, 1)
                dve.wait_ge(mx_ab, 2)
                link(dve.tensor_tensor(by_t(zz), tail_ab[:, :, 0:4], each_t(dt_bias[:, :]), ALU.add))
                dve.scalar_tensor_tensor(uu, zz, -1.0, zz, ALU.mult, ALU.max).then_inc(mx_abs, 1)
                split(n0 + 8)
                log_decay()
                split(n0 + 9)
                take_conv(1)
                take_conv(3)
                split(n0 + 10)
                take_conv(5)
                convolve(0)
                split(n0 + 11)
                dve.wait_ge(mx_cum, 1)
                dve.tensor_copy(dec, bank[6][:, 16:24]).then_inc(mx_dec, 1)
                convolve(1)
                att_sum_squares(0)
                att_sum_squares(1)
                split(n0 + 12)
                dve.wait_ge(mx_dec, 1)
                dve.wait_ge(mx_last, 1)
                dve.tensor_tensor(etail, bank[6][:, 24:32], dec, ALU.subtract).then_inc(mx_last_diff, 1)
                dve.wait_ge(mx_rows, 1)
                for u in range(8):
                    dve.tensor_scalar(dn_LT[:, u, :], bank[4 + u // 4][:, u % 4 * P:u % 4 * P + P], dec[:, u:u + 1], 0.0,
                                      ALU.subtract, ALU.min).then_inc(mx_diff, 1)
                convolve(2)
                split(n0 + 13)
                dve.wait_ge(mx_etail, 2)
                link(dve.tensor_tensor(bed, beta, edec, ALU.mult))
                att_sum_squares(2)
                att_sum_squares(3)
                dve.wait_ge(table_full, 32)
                dve.wait_ge(mx_exprow, 3)
                link(dve.tensor_tensor(dn_LT, dn_LT, sum_mask, ALU.mult))
                dve.wait_ge(mx_rows, 2)
                dve.wait_ge(mx_conv, 36)
                for b in range(2):
                    dve.tensor_tensor(flat(quarter(dn_AT, b)), flat(quarter(dn_LT, b)), bank[2 + b][:, :], ALU.mult)\
                        .then_inc(mx_masked, 1)
                sum_squares(0)
                att_normalise(0)
                att_normalise(1)
                for t in range(2):
                    dve.wait_ge(mx_tok_psum, 4 + t + 1)
                    dve.tensor_tensor(quarter(dn_vbeta, t), by_four(bank[4 + t][:, :]), wide(beta[:, 4 * t:4 * t + 4]), ALU.mult)\
                        .then_inc(mx_vbeta, 1)
                sum_squares(1)
                for s in range(2):
                    dve.wait_ge(mx_dnr, s + 1)
                    dve.wait_ge(mx_tok, 4)
                    dve.tensor_tensor(dn_tok[s], dn_tok[s], wide(dn_rstd[:, s, :]), ALU.mult).then_inc(mx_dnn, 1)
                for c in range(2):
                    dve.wait_ge(mx_aT_psum, 2 * c + 2)
                    dve.tensor_scalar(flat(kT[:, 2 * c:2 * c + 2, :]), bank[3 - 2 * c][:, :], att_gain[:, 1:2], None,
                                      ALU.mult).then_inc(mx_ak, 1)
                dve.wait_ge(mx_masked, 2)
                dve.wait_ge(mx_gram, 1)
                for b in range(2):
                    last = dve.tensor_tensor(flat(quarter(dn_AT, b)), flat(quarter(dn_AT, b)), bank[4 + b][:, :], ALU.mult)
                link(last)
                dve.tensor_tensor(dn_X, dn_AT, level[0], ALU.mult).then_inc(mx_N0, 1)
                dve.wait_ge(mx_N0, 1)
                for b in range(2):
                    last = dve.tensor_tensor(quarter(dn_XT, b), two_idents, quarter(dn_X, b), ALU.subtract)
                link(last)
                dve.wait_ge(mx_gram, 2)
                for b in range(2):
                    dve.tensor_tensor(flat(quarter(dn_attT, b)), flat(quarter(dn_LT, b)), bank[6 + b][:, :], ALU.mult)\
                        .then_inc(mx_attT, 1)
                maxima(0)
                dve.wait_ge(mx_N0T, 1)
                for b in range(2):
                    dve.tensor_tensor(quarter(dn_X, b), two_idents, by_four(bank[4 + b][:, :]), ALU.subtract).then_inc(mx_inv0, 1)
                dve.wait_ge(mx_attT, 2)
                for b in range(2):
                    level_mask(1, b)
                maxima(1)
                for n in range(1, LEVELS):
                    if n + 1 < LEVELS:
                        for b in range(2):
                            level_mask(n + 1, b)
                    if n == 5:
                        att_out(0)
                    for b in range(2):
                        dve.wait_ge(mx_Z, 2 * (n - 1) + b + 1)
                        if n > 1:
                            dve.wait_ge(mx_inv, 4 * (n - 2) + 2 * b + 2)
                        for dst, src in ((dn_X, bank[4 + b]), (dn_XT, bank[6 + b]))[n // (LEVELS - 1):]:
                            dve.tensor_tensor(flat(quarter(dst, b)), flat(quarter(dst, b)), src[:, :], ALU.subtract)\
                                .then_inc(mx_inv, 1)
                        if b == 0:
                            maxima(n + 1)
                dve.wait_ge(mx_val, 1)
                dve.wait_ge(mx_inv, 4 * (LEVELS - 2) + 2)
                for b in range(2):
                    dve.tensor_copy(flat(quarter(dn_kcT, b)), bank[6 + b][:, :]).then_inc(mx_valsb, 1)
                recur(0)
                maxima(7)
                split(n1)
                recur(1)
                att_out(1)
                split(n1 + 1)
                recur(2)
                dve.wait_ge(mx_aor, 1)
                dve.wait_ge(mx_ao, 4)
                for t in range(2):
                    dve.scalar_tensor_tensor(att_y[:, t, :], att_y[:, t, :], head_rstd[:, t:t + 1], out_gain[:, :],
                                             ALU.mult, ALU.mult).then_inc(mx_ay, 1)
                recur(3)
                for t in range(2):
                    dve.wait_ge(mx_osq, t + 1)
                    dve.tensor_reduce(dn_ss[:, 0, 4 * t:4 * t + 4], by_four(square[:, t * 512:t * 512 + 512]), AX_X,
                                      ALU.add).then_inc(mx_oss, 1)

                def turned_output(p, b):
                    for t in range(2):
                        dve.wait_ge(mx_yT_hi, 2 * p + t + 1)
                        at = (slice(None), slice(4 * p, 4 * p + 4), slice(t * P, t * P + P))
                        dve.tensor_tensor(xT_lo[at], by_four(bank[b + t][:, :]), xT_hi[at].bitcast(F32), ALU.subtract)\
                            .then_inc(mx_yT_lo, 1)

                turned_output(0, 0)
                dve.wait_ge(mx_or, 1)
                dve.wait_ge(mx_gate_gain, 2)
                for t in range(2):
                    dve.tensor_tensor(by_four(dn_y[:, t, :]), by_four(bank[4 + t][:, :]), wide(dn_rstd[:, 0, 4 * t:4 * t + 4]),
                                      ALU.mult).then_inc(mx_y, 1)
                    dve.wait_ge(mx_y, 2 * t + 1)
                    dve.tensor_tensor(dn_y[:, t, :], dn_y[:, t, :], mx_gate[:, t, :], ALU.mult).then_inc(mx_y, 1)
                split(n1 + 2)
                turned_output(1, 6)
                split(n1 + 3)
                split(n1 + 4)
            dve.sem_inc(lo_ready, RING)
            norm(0)
            split(0)
            split(1)
            ffn(0, first["ffn0"])
            da()
            norm(2, 1.0, first["ffn1"] + 1)
            ffn(1, first["ffn1"])
            norm(3, 0.5, first["ffn2"] + 1)
            ffn(2, first["ffn2"])
            rt()
            norm(5, 1.0, first["ffn3"] + 1)
            ffn(3, first["ffn3"])
            mix()
            norm(7, 1.0, first["ff2"] + 1)
            ff2(first["ff2"])
            for q in range(4):
                residual(len(last_out) - 1, q, 1.0)

        @block.tensor
        def _(pe):
            def split_product(dst, lT_hi, lT_lo, r_hi, r_lo, start, stop):
                pe.matmul(dst, lT_hi, r_hi, start=start, stop=False)
                pe.matmul(dst, lT_hi, r_lo, start=False, stop=False)
                return pe.matmul(dst, lT_lo, r_hi, start=False, stop=stop)

            def wait_block(n, turns):
                pe.wait_ge(lo_ready, n + 1 + RING + RING * turns)

            def turn(g, q):
                pe.wait_ge(xg_ready, 4 * g + q + 1)
                for k in range(4):
                    at = (q // 2) * 512 + k * P
                    tr = pe.transpose(bank[4 + q][:, k * P:k * P + P], xg[:, q % 2, at:at + P], ident)
                tr.then_inc(xt_psum, 1)

            def in_block(n, j, banks, turns=0, norm=None, done=None):
                wait_block(n, turns)
                hi, lo = by_four(w_hi[:, n % RING, :]), by_four(w_lo[:, n % RING, :])
                for t in range(2):
                    if norm is not None:
                        if norm and 2 * j + t < 3:
                            turn(norm, 2 * j + t + 1)
                        pe.wait_ge(xt_lo_ready, 4 * norm + 2 * j + t + 1)
                    tok = slice(t * P, t * P + P)
                    for k in range(4):
                        mm = split_product(bank[banks + t][:, :], xT_hi[:, 4 * j + k, tok], xT_lo[:, 4 * j + k, tok],
                                           hi[:, k, :], lo[:, k, :], j == 0 and k == 0, j == 1 and k == 3)
                    if j == 1 and t == 0:
                        mm.then_inc(done, 1)
                mm.then_inc(wt_used, 1)

            def out_block(n, lhs, k0, start, stop, turns=0, norm=None):
                wait_block(n, turns)
                hi = w_hi[:, n % RING, :].rearrange("p (k n) -> p k n", k=2)
                lo = w_lo[:, n % RING, :].rearrange("p (k n) -> p k n", k=2)
                for q in range(4):
                    if q == 3 and norm is not None:
                        turn(norm, 0)
                    tok = slice(q % 2 * P, q % 2 * P + P)
                    cols = slice(q // 2 * 512, q // 2 * 512 + 512)
                    for k in range(2):
                        mm = split_product(bank[q][:, :], lhs[0][:, k0 + k, tok], lhs[1][:, k0 + k, tok],
                                           hi[:, k, cols], lo[:, k, cols], start and k == 0, stop and k == 1)
                    if stop and q < 3:
                        mm.then_inc(acc_done, 1)
                mm.then_inc(wt_used, 1)

            def ffn(f, n0):
                g = NORM_OF[f"ffn{f}"]
                cb = FFC * f

                def turn_hidden(c, i=0):
                    pe.wait_ge(hid_ready, 2 * (cb + c + 1) + 2 * i)
                    for t in range(2):
                        for k in range(2):
                            tr = pe.transpose(bank[6][:, k * T + t * P:k * T + t * P + P],
                                              hid[:, t, k * P:k * P + P], ident)
                    tr.then_inc(ht_psum, 1)

                in_block(n0, 0, 0, norm=g)
                in_block(n0 + 1, 1, 0, norm=g, done=in_done)

                def chunk(c, i, start):
                    in_block(n0 + 2, 0, 4, turns=i)
                    if start:
                        turn_hidden(0)
                    in_block(n0 + 3, 1, 4, turns=i, done=in_done)
                    pe.wait_ge(ht_lo_ready, cb + c + i)
                    out_block(n0 + 4, (hT_hi, hT_lo), 0, start, False, turns=i)
                    turn_hidden(c, i)

                chunk(1, 0, True)
                with pe.Fori(1, FFC - 1) as i:
                    chunk(1, i, False)
                pe.wait_ge(ht_lo_ready, cb + FFC)
                out_block(n0 + FFN_BLOCKS - 1, (hT_hi, hT_lo), 0, False, True, norm=g + 1)

            def ff2(n0):
                def turn_hidden(c, i=0):
                    pe.wait_ge(sq_ready, 2 * c + 2 + 2 * i)
                    for b in range(2):
                        for k in range(2):
                            for t in range(2):
                                at = (2 * b + k) * P
                                tr = pe.transpose(bank[6 + b][:, k * T + t * P:k * T + t * P + P],
                                                  hid[:, t, at:at + P], ident)
                        tr.then_inc(ht2_psum, 1)

                def out(c, n, start, stop, i=0, turns=0):
                    for b in range(2):
                        pe.wait_ge(ht2_lo_ready, 2 * c + b + 1 + 2 * i)
                        out_block(n + b, (hT_hi, hT_lo), 2 * b, start and b == 0, stop and b == 1, turns)

                def chunk(c, n, start=False, i=0, turns=0):
                    in_block(n, 0, 4, turns)
                    if start:
                        turn_hidden(0)
                    in_block(n + 1, 1, 4, turns, done=in2_done)
                    out(c - 1, n + 2, start, False, i, turns)
                    turn_hidden(c, i)

                in_block(n0, 0, 0, norm=7)
                in_block(n0 + 1, 1, 0, norm=7, done=in2_done)
                for u in range(3):
                    chunk(1 + u, n0 + 2 + 4 * u, u == 0)
                with pe.Fori(1, 2) as i:
                    for u in range(3):
                        chunk(1 + u, n0 + 2 + 4 * u, False, 3 * i, 4 * i)
                chunk(FF2C - 1, n0 + 4 * FF2C - 6)
                out(FF2C - 1, n0 + 4 * FF2C - 2, False, True)

            def project(n0, m0, g, chunks):
                def chunk(u, turns=0, norm=None):
                    pe.wait_ge(proj_read, 2 * (m0 + u + 1) + 3 * turns)
                    in_block(n0 + 2 * u, 0, u % 3 * 2, turns=turns, norm=norm)
                    in_block(n0 + 2 * u + 1, 1, u % 3 * 2, turns=turns, norm=norm, done=proj_done)

                chunk(0, norm=g)
                chunk(1)
                chunk(2)
                if chunks // 3 > 1:
                    with pe.Fori(1, chunks // 3) as i:
                        for u in range(3):
                            chunk(u, turns=2 * i)
                for u in range(chunks // 3 * 3, chunks):
                    chunk(u)

            def da():
                def out_part(h, q):
                    n = first["da_out"] + h // 2
                    if q == 0:
                        wait_block(n, 0)
                        pe.wait_ge(da_oT_lo, h + 1)
                    cols = slice(h % 2 * D + q // 2 * 512, h % 2 * D + q // 2 * 512 + 512)
                    tok = slice(q % 2 * P, q % 2 * P + P)
                    mm = split_product(bank[q][:, :], xT_hi[:, h, tok], xT_lo[:, h, tok], w_hi[:, n % RING, cols],
                                       w_lo[:, n % RING, cols], h == 0, h == DA_H - 1)
                    if q == 3 and h % 2:
                        mm.then_inc(wt_used, 1)
                    elif h == DA_H - 1:
                        mm.then_inc(acc_done, 1)

                project(first["da_in"], 0, 1, 6)
                pe.wait_ge(proj_read, 6 + 12)
                pe.wait_ge(da_normed, 4)
                for c in range(4):
                    for s in range(2):
                        for h in range(2):
                            for t in range(2):
                                at = s * D + (2 * c + h) * P
                                tr = pe.transpose(bank[2 * c + s][:, h * T + t * P:h * T + t * P + P],
                                                  da_proj[:, t, at:at + P], ident)
                        tr.then_inc(da_turned, 1)
                pe.wait_ge(bias_full, 17)
                both = ident_r.unsqueeze(1).to_broadcast([P, 2, P])
                for i in range(DA_H + 4):
                    if i < DA_H:
                        if i == 0:
                            pe.wait_ge(da_qT, 4)
                            pe.wait_ge(da_kT, 4)
                        for m in range(2):
                            if i:
                                pe.wait_ge(da_exp, 4 * (i - 1) + 2 * m + 2)
                            rows = slice(m * DA_DH, (m + 1) * DA_DH)
                            S = bank[4 + m]
                            pe.matmul(S[:, 0:P], qT[rows, i, 0:P], kT[rows, i, 0:P], start=True, stop=False)
                            pe.matmul(S[:, P:384], qT[rows, i, P:T], kT[rows, i, :], start=False, stop=False)
                            pe.matmul(S[:, 0:384].rearrange("p (c n) -> p c n", c=3)[:, 0::2, :], diag_bias[:, i, :], both,
                                      start=False, stop=False)
                            pe.matmul(S[:, P:T], bias[:, i, P:T], ident, start=False, stop=True)\
                                .then_inc(da_scores, 1)
                    if i >= 4:
                        out_part(i - 4, 0)
                    if 1 <= i <= DA_H:
                        h = i - 1
                        pe.wait_ge(da_mixed, 2 * h + 2)
                        if h:
                            pe.wait_ge(da_mixT, h)
                        if h >= 2:
                            pe.wait_ge(da_oT_lo, h - 1)
                        for b in range(3):
                            tr = pe.transpose(bank[6][:, b * P:b * P + P], mixed[:, h % 2, b * P:b * P + P], ident)
                        tr.then_inc(da_mixT_psum, 1)
                    if i >= 4:
                        out_part(i - 4, 1)
                    if 1 <= i <= DA_H:
                        h = i - 1
                        v = da_proj[:, :, 2 * D + h * P:2 * D + h * P + P]
                        pe.wait_ge(da_mixT, h + 1)
                        if h:
                            pe.wait_ge(da_normed_o, 2 * h)
                        pe.matmul(bank[7][:, 0:P], mixT[:, 0:P], v[:, 0, :], start=True, stop=True)
                        pe.matmul(bank[7][:, P:T], mixT[:, P:T], v[:, 0, :], start=True, stop=False)
                        pe.matmul(bank[7][:, P:T], mixT[:, T:384], v[:, 1, :], start=False, stop=True)\
                            .then_inc(da_o, 1)
                    if i >= 4:
                        out_part(i - 4, 2)
                    if 2 <= i <= DA_H + 1:
                        h = i - 2
                        pe.wait_ge(da_normed_o, 2 * h + 2)
                        pe.wait_ge(da_mixT, min(h + 2, DA_H))
                        if h:
                            pe.wait_ge(da_oT_lo, h)
                        for t in range(2):
                            tr = pe.transpose(bank[6][:, t * P:t * P + P], head_out[:, t, 0:P], ident)
                        tr.then_inc(da_oT_psum, 1)
                    if i == DA_H + 3:
                        turn(2, 0)
                    if i >= 4:
                        out_part(i - 4, 3)

            def rt():
                n0, n1 = first["rt_in"], first["rt_out"]
                project(n0, 6, 4, 6)
                for m in range(6, 12):
                    h = m - 8
                    pe.wait_ge(proj_read, 6 + 2 * (6 + (m - 1 if m >= 8 else 3 + m - 5)))
                    for j in range(2):
                        in_block(n0 + 2 * m + j, j, 2 * rt_pair[m], done=proj_done)
                        if h < 0:
                            c = 2 * (m - 6) + j
                            for s, src in enumerate((rt_q, rt_k)):
                                if c:
                                    pe.wait_ge((rt_qT, rt_kT)[s], c)
                                for k in range(2):
                                    for t in range(2):
                                        at = (2 * c + k) * P
                                        tr = pe.transpose(bank[6 + s][:, k * T + t * P:k * T + t * P + P],
                                                          src[:, t, at:at + P], ident)
                                tr.then_inc(rt_turned, 1)
                        elif j == 0:
                            if h == 0:
                                pe.wait_ge(rt_qT, 4)
                                pe.wait_ge(rt_kT, 4)
                            else:
                                pe.wait_ge(rt_decayed, 2 * h)
                            for cols, keys, queries in ((slice(0, T), slice(0, P), slice(0, T)),
                                                        (slice(T, 384), slice(P, T), slice(P, T))):
                                for k in range(2):
                                    mm = pe.matmul(bank[6][:, cols], kT[:, 2 * h + k, keys], qT[:, 2 * h + k, queries],
                                                   start=k == 0, stop=k == 1)
                            mm.then_inc(rt_scores, 1)
                        else:
                            pe.wait_ge(rt_decayed, 2 * h + 2)
                            if h:
                                pe.wait_ge(rt_y, 2 * h)
                            v = rt_v[:, :, h * 512:h * 512 + 512]
                            att = rt_att[:, h % 2, :]
                            pe.matmul(bank[4][:, :], att[:, 0:P], v[:, 0, :], start=True, stop=True)
                            pe.matmul(bank[5][:, :], att[:, P:T], v[:, 0, :], start=True, stop=False)
                            pe.matmul(bank[5][:, :], att[:, T:384], v[:, 1, :], start=False, stop=True).then_inc(rt_o, 1)

                def turn_y(h):
                    pe.wait_ge(rt_y, 2 * h + 2)
                    if h:
                        pe.wait_ge(rt_yT_lo, 2 * h)
                    for t in range(2):
                        for k in range(4):
                            at = h * 512 + k * P
                            tr = pe.transpose(bank[6 + t][:, k * P:k * P + P], rt_g[:, t, at:at + P], ident)
                        tr.then_inc(rt_yT_psum, 1)

                turn_y(0)
                turn_y(1)
                pe.wait_ge(proj_read, 6 + 2 * 18)
                for h in range(RT_H):
                    pe.wait_ge(rt_yT_lo, 2 * h + 2)
                    for r in range(2):
                        out_block(n1 + 2 * h + r, (xT_hi, xT_lo), h % 2 * 4 + 2 * r, h == 0 and r == 0, h == 3 and r == 1,
                                  norm=5 if h == 3 and r == 1 else None)
                    if h < 2:
                        turn_y(h + 2)

            def mix():
                n0, n1 = first["mix_in"], first["mix_out"]

                def tail():
                    pe.wait_ge(mx_tail_lo, 1)
                    for k in range(KD):
                        mm = split_product(bank[6][0:8, 0:T], tail_hi[:, k, :], tail_lo[:, k, :], xT_hi[:, k, :],
                                           xT_lo[:, k, :], k == 0, k == KD - 1)
                    mm.then_inc(mx_tail, 1)
                    pe.wait_ge(mx_small, MX_SMALL)
                    pe.transpose(bank[7][:, 0:48], conv_row, ident[0:48, 0:48]).then_inc(mx_convw_psum, 1)

                def turn_conv(c):
                    for k in range(2):
                        for t in range(2):
                            at = (c % 2 * 2 + k) * P
                            tr = pe.transpose(bank[2 + c % 4][:, k * T + t * P:k * T + t * P + P],
                                              mx_dn[:, c // 2, t, at:at + P], ident)
                    tr.then_inc(mx_conv_psum, 1)

                def rows(src, b):
                    for u in range(8):
                        mm = pe.matmul(bank[b + u // 4][:, u % 4 * P:u % 4 * P + P],
                                       src[:, u:u + 1].to_broadcast([P, P]), ident, start=True, stop=True)
                    mm.then_inc(mx_rows, 1)

                def to_tokens(s):
                    pe.wait_ge(mx_silu, s + 1)
                    for t in range(2):
                        for h in range(4):
                            tr = pe.transpose(bank[4 + s % 2 * 2 + t][:, h * P:h * P + P],
                                              conv_out[s][:, h, t * P:t * P + P], ident)
                        tr.then_inc(mx_tok_psum, 1)

                def turn_att(c):
                    for s in range(2):
                        for k in range(2):
                            for t in range(2):
                                at = (2 * c + k) * P
                                tr = pe.transpose(bank[2 - 2 * c + s][:, k * T + t * P:k * T + t * P + P],
                                                  mx_att[:, s, t, at:at + P], ident)
                        tr.then_inc(mx_aT_psum, 1)

                def scores(i):
                    if i >= 2:
                        pe.wait_ge(mx_P, 2 * (i - 1))
                    r = slice(i % 2 * AT_DH, (i % 2 + 1) * AT_DH)
                    q, k, S = qT[r, i // 2, :], kT[r, i // 2, :], bank[i % 2]
                    pe.matmul(S[:, 0:P], q[:, 0:P], k[:, 0:P], start=True, stop=False)
                    pe.matmul(S[:, 0:P], bias[:, i, 0:P], flip, start=False, stop=True)
                    pe.matmul(S[:, P:384], q[:, P:T], k, start=True, stop=False)
                    pe.matmul(S[:, P:T], bias[:, i, P:T], flip, start=False, stop=False)
                    pe.matmul(S[:, T:384], bias[:, i, 0:P], flip, start=False, stop=True).then_inc(mx_S, 1)

                def values(h):
                    pe.wait_ge(mx_P, 2 * h + 2)
                    if h:
                        pe.wait_ge(mx_PT, h)
                    for b in range(3):
                        tr = pe.transpose(bank[2][:, b * P:b * P + P], prob_a[:, h % 2, b * P:b * P + P], ident)
                    tr.then_inc(mx_PT_psum, 1)

                def values_2(h):
                    pe.wait_ge(mx_PT, h + 1)
                    if h == 4:
                        pe.wait_ge(mx_ao, 2)
                    v = mx_att[:, 2, :, h * AT_DH:h * AT_DH + AT_DH]
                    o = [bank[3][:, h % 4 * P + t * AT_DH:h % 4 * P + (t + 1) * AT_DH] for t in range(2)]
                    pe.matmul(o[0], probT[:, 0:P], v[:, 0, :], start=True, stop=True)
                    pe.matmul(o[1], probT[:, P:T], v[:, 0, :], start=True, stop=False)
                    pe.matmul(o[1], probT[:, T:384], v[:, 1, :], start=False, stop=True).then_inc(mx_AV, 1)

                def recur(n):
                    t, r = n // 2, slice(n % 2 * CHUNK, n % 2 * CHUNK + CHUNK)
                    if n:
                        pe.wait_ge(mx_state, 4 * (n - 1) + 1)
                        for h in range(4):
                            mm = pe.matmul(bank[6][r, h * P:h * P + P], dn_kcT[:, 4 * t + h, r],
                                           dn_state[(n - 1) % 2][:, h * P:h * P + P], start=True, stop=True)
                        mm.then_inc(mx_KS, 1)
                    else:
                        pe.wait_ge(mx_valsb, 4)
                        pe.wait_ge(mx_qd, 1)
                    pe.wait_ge(mx_vnew, n + 1)
                    if n < 3:
                        for h in range(4):
                            mm = pe.matmul(bank[7][:, h * P:h * P + P], dn_ktail[r, 4 * t + h, :],
                                           dn_vnew[r, h * P:h * P + P], start=True, stop=True)
                        mm.then_inc(mx_SU, 1)
                    for h in range(4):
                        at = slice(h * P, h * P + P)
                        tok = slice(t * P + n % 2 * CHUNK, t * P + n % 2 * CHUNK + CHUNK)
                        if n:
                            pe.matmul(bank[4 + t][r, at], dn_qhT[:, h, tok], dn_state[(n - 1) % 2][:, at], start=True, stop=False)
                        mm = pe.matmul(bank[4 + t][r, at], dn_attT[r, 4 * t + h, r], dn_vnew[r, at],
                                       start=not n, stop=True)
                    mm.then_inc(mx_O, 1)

                def turn_output(p, src, b):
                    for t in range(2):
                        for k in range(4):
                            tr = pe.transpose(bank[b + t][:, k * P:k * P + P], src[:, t, k * P:k * P + P], ident)
                        tr.then_inc(mx_yT_psum, 1)

                for m in range(7):
                    for j in range(2):
                        if j == 0:
                            pe.wait_ge(proj_read, 6 + 2 * (18 + (m if m > 3 else max(m - 2, 0))))
                        if m == 3 and j == 0:
                            tail()
                        elif m == 3:
                            pe.wait_ge(proj_read, 6 + 2 * (18 + 3))
                            pe.wait_ge(mx_tail_sb, 1)
                            for t in range(2):
                                tr = pe.transpose(bank[6][:, t * 8:t * 8 + 8], tail_row[:, t * P:t * P + P], ident[0:8, 0:8])
                            tr.then_inc(mx_tail, 1)
                            for c in range(4):
                                turn_conv(c)
                        elif m == 4 and j == 0:
                            pe.wait_ge(mx_conv_in, 1)
                            pe.wait_ge(mx_conv_in2, 1)
                            turn_conv(4)
                            turn_conv(5)
                        elif m == 4:
                            pe.wait_ge(mx_g, 1)
                            pe.wait_ge(table_full, 32)
                            pe.matmul(bank[6][:, 16:24], cum, gg, start=True, stop=True).then_inc(mx_cum, 1)
                        elif m == 5 and j == 0:
                            pe.wait_ge(mx_dec, 1)
                            pe.matmul(bank[6][:, 24:32], last_row, dec, start=True, stop=True).then_inc(mx_last, 1)
                            pe.wait_ge(mx_conv_in, 3)
                            pe.wait_ge(mx_conv_in2, 3)
                            rows(dec, 4)
                            rows(beta, 2)
                        elif m == 5:
                            pe.wait_ge(mx_exprow, 2)
                            to_tokens(0)
                        elif m == 6 and j == 0:
                            pe.wait_ge(mx_last_diff, 1)
                            pe.wait_ge(mx_convw, 1)
                            to_tokens(1)
                        elif m == 6:
                            pe.wait_ge(mx_tok, 2)
                            to_tokens(2)
                        in_block(n0 + 2 * m + j, j, mx_pair[m] * 2, norm=6 if m == 0 else None, done=proj_done)
                pe.wait_ge(mx_an, 4)
                pe.wait_ge(mx_masked, 2)
                turn_att(0)
                pe.wait_ge(proj_read, 6 + 2 * 25)
                turn_att(1)
                pe.wait_ge(mx_tok, 4)
                pe.wait_ge(mx_vbeta, 2)
                for s in range(2):
                    pe.wait_ge(mx_dnn, s + 1)
                    for t in range(2):
                        for h in range(4):
                            tr = pe.transpose(bank[4 + s * 2 + t][:, h * P:h * P + P], dn_tok[s][:, 4 * t + h, :], ident)
                        tr.then_inc(mx_back_psum, 1)
                pe.wait_ge(mx_bias, 17)
                pe.wait_ge(mx_aq, 2)
                pe.wait_ge(mx_ak, 2)
                scores(0)
                pe.wait_ge(mx_back, 4)
                for b, rhs in ((4, dn_khT), (6, dn_qhT)):
                    for u in range(8):
                        tok = slice(u // 4 * P, u // 4 * P + P)
                        mm = pe.matmul(bank[b + u // 4][:, u % 4 * P:u % 4 * P + P], dn_khT[:, u % 4, tok],
                                       rhs[:, u % 4, tok], start=True, stop=True)
                    mm.then_inc(mx_gram, 1)
                scores(1)
                pe.wait_ge(mx_N0, 1)
                for u in range(8):
                    tr = pe.transpose(bank[4 + u // 4][:, u % 4 * P:u % 4 * P + P], dn_X[:, u, :], ident)
                tr.then_inc(mx_N0T, 1)
                values(0)
                pe.wait_ge(mx_inv0, 2)
                for n in range(1, LEVELS):
                    for b in range(2):
                        pe.wait_ge(mx_MT, 2 * (n - 1) + b + 1)
                        if n == 1:
                            pe.wait_ge(mx_attT, 2)
                        else:
                            pe.wait_ge(mx_inv, 4 * (n - 2) + 2 * b + 2)
                        for u in range(4 * b, 4 * b + 4):
                            mm = pe.matmul(bank[4 + b][:, u % 4 * P:u % 4 * P + P], dn_MT[:, u, :], dn_X[:, u, :],
                                           start=True, stop=True)
                        mm.then_inc(mx_Y, 1)
                        if b == 0:
                            values_2(n - 1)
                    scores(n + 1)
                    for b in range(2):
                        pe.wait_ge(mx_Ysb, 2 * (n - 1) + b + 1)
                        for u in range(4 * b, 4 * b + 4):
                            at = slice(u % 4 * P, u % 4 * P + P)
                            if n < LEVELS - 1:
                                pe.matmul(bank[4 + b][:, at], dn_XT[:, u, :], dn_Y[:, u, :], start=True, stop=True)
                            mm = pe.matmul(bank[6 + b][:, at], dn_Y[:, u, :], dn_XT[:, u, :], start=True, stop=True)
                        mm.then_inc(mx_Z, 1)
                    values(n)
                pe.wait_ge(mx_inv, 4 * (LEVELS - 2) + 2)
                pe.wait_ge(mx_ktail, 2)
                for u in range(8):
                    at = slice(u % 4 * P, u % 4 * P + P)
                    pe.matmul(bank[4 + u // 4][:, at], dn_XT[:, u, :], dn_vbeta[:, u, :], start=True, stop=True)
                    mm = pe.matmul(bank[6 + u // 4][:, at], dn_kbe[:, u, :], dn_XT[:, u, :], start=True, stop=True)
                mm.then_inc(mx_val, 1)
                values_2(5)
                scores(7)
                values(6)
                recur(0)
                values_2(6)
                values(7)
                recur(1)
                values_2(7)
                recur(2)
                pe.wait_ge(mx_ay, 2)
                turn_output(0, att_y, 0)
                recur(3)
                pe.wait_ge(mx_yT_lo, 2)
                out_block(n1, (xT_hi, xT_lo), 0, True, False)
                pe.wait_ge(mx_y, 4)
                turn_output(1, dn_y, 6)
                out_block(n1 + 1, (xT_hi, xT_lo), 2, False, False)
                pe.wait_ge(mx_yT_lo, 4)
                out_block(n1 + 2, (xT_hi, xT_lo), 4, False, False)
                out_block(n1 + 3, (xT_hi, xT_lo), 6, False, True, norm=7)
            pe.sem_inc(wt_used, RING)
            pe.wait_ge(table_full, 16)
            for q in range(4):
                turn(0, q)
            ffn(0, first["ffn0"])
            da()
            ffn(1, first["ffn1"])
            ffn(2, first["ffn2"])
            rt()
            ffn(3, first["ffn3"])
            mix()
            ff2(first["ff2"])


USED = ["x", "ffn1_norm", "ffn1_w_in", "ffn1_w_out", "mix_norm", "ffn2_norm", "ffn2_w_in", "ffn2_w_out",
        "da_w_in", "da_q_gain", "da_k_gain", "da_lambda", "da_subln", "da_w_out", "rt_w_in", "rt_subln",
        "rt_w_out", "mix_norm_gain_2", "w_in_2", "att_q_gain_2", "att_k_gain_2", "rel_bias_2",
        "att_out_gain_2", "dn_conv_w_2", "dn_a_log_2", "dn_dt_bias_2", "dn_out_gain_2", "w_out_2",
        "ffn_norm_gain_2", "w_ff1_2", "w_ff2_2"]


def program(nc, shapes):
    A = {}
    for name, (shape, dtype) in shapes.items():
        A[name] = nc.dram_tensor(f"in_{name}", shape, dtype, kind="ExternalInput").ap()
    out = nc.dram_tensor("out", (1, T, D), F32, kind="ExternalOutput").ap()
    first_then_second_block(nc, A, out)


def kernel(**inputs):
    import concourse.bacc as bacc
    from concourse.bass_utils import run_bass_kernel_spmd

    arrays = {name: np.ascontiguousarray(inputs[name]) for name in USED} | constants()
    nc = bacc.Bacc("TRN2", target_bir_lowering=False, num_devices=1)
    program(nc, {k: (v.shape, mybir.dt.from_np(v.dtype)) for k, v in arrays.items()})
    r = run_bass_kernel_spmd(nc, [{f"in_{k}": v for k, v in arrays.items()}], core_ids=[0])
    return r.results[0]["out"]
```
